# Optimizing a Trainium2 kernel written in Bass

```python
import math
import jax
import jax.numpy as jnp
from jax import lax
import numpy as np
import jax, jax.numpy as jnp

D_MODEL = 1024
BATCH = 1
SEQ = 512
DEPTH = 2

HEAD_DIM = 64
GROUP_HEADS = 4
GROUP_WIDTH = GROUP_HEADS * HEAD_DIM
N_GROUPS = 4
D_MIX = N_GROUPS * GROUP_WIDTH
NSA_HEADS = GROUP_HEADS
GDN_HEADS = GROUP_HEADS
MLSTM_HEADS = GROUP_HEADS
CMP_STRIDE = 16
CMP_BLOCK = 2 * CMP_STRIDE
CMP_HIDDEN = 256
SLC_BLOCK = 64
N_SLC = 16
N_LOCAL_SLC = 2
WINDOW = 512
Q_BLOCK = 128
FORCE = 1e6
N_BUCKETS = 32
MAX_DISTANCE = 128
SC_WIDTH = 3
GDN_CONV = 4
GDN_CHUNK = 64
MLSTM_CHUNK = 64
D_FF = 2816
N_SUBLAYERS = 3
EPS = 1e-6

IN_LAYOUT = (
    ("a_q", GROUP_WIDTH), ("a_k_cmp", HEAD_DIM), ("a_v_cmp", HEAD_DIM),
    ("a_k_slc", HEAD_DIM), ("a_v_slc", HEAD_DIM), ("a_k_win", HEAD_DIM), ("a_v_win", HEAD_DIM),
    ("a_gate", 3 * NSA_HEADS),
    ("b_b", GROUP_WIDTH), ("b_c", GROUP_WIDTH), ("b_x", GROUP_WIDTH),
    ("c_q", GROUP_WIDTH), ("c_k", GROUP_WIDTH), ("c_v", GROUP_WIDTH),
    ("c_beta", GDN_HEADS), ("c_alpha", GDN_HEADS), ("c_z", GROUP_WIDTH),
    ("d_q", GROUP_WIDTH), ("d_k", GROUP_WIDTH), ("d_v", GROUP_WIDTH),
    ("d_i", MLSTM_HEADS), ("d_f", MLSTM_HEADS), ("d_o", GROUP_WIDTH),
)
D_IN = sum(s for _, s in IN_LAYOUT)


def rms_norm(x, g):
    xf = x.astype(jnp.float32)
    y = xf * lax.rsqrt(jnp.mean(xf * xf, axis=-1, keepdims=True) + EPS)
    return (y * g).astype(x.dtype)

def l2_norm(x):
    xf = x.astype(jnp.float32)
    return (xf * lax.rsqrt(jnp.sum(xf * xf, axis=-1, keepdims=True) + EPS)).astype(x.dtype)

def adaln_pre(h, g, shift, scale):
    return rms_norm(h, g) * (1 + scale) + shift

def swiglu(h, w13, w2):
    a, b = jnp.split(h @ w13, 2, axis=-1)
    return (jax.nn.silu(a) * b) @ w2

def causal_dwconv(x, w):
    K, C = w.shape
    return lax.conv_general_dilated(
        x, w[:, None, :], window_strides=(1,), padding=[(K - 1, 0)],
        dimension_numbers=("NWC", "WIO", "NWC"), feature_group_count=C)

def masked_softmax(logits, mask):
    l = jnp.where(mask, logits.astype(jnp.float32), -1e30)
    m = jnp.max(l, axis=-1, keepdims=True)
    e = jnp.where(mask, jnp.exp(l - m), 0.0)
    return e / jnp.maximum(jnp.sum(e, axis=-1, keepdims=True), 1e-30)

def t5_bucket(dist):
    n = jnp.maximum(dist, 0)
    max_exact = N_BUCKETS // 2
    nf = jnp.maximum(n, 1).astype(jnp.float32)
    large = max_exact + (jnp.log(nf / max_exact) / math.log(MAX_DISTANCE / max_exact)
                         * (N_BUCKETS - max_exact)).astype(jnp.int32)
    large = jnp.minimum(large, N_BUCKETS - 1)
    return jnp.where(n < max_exact, n, large)

def nsa_mixer(q, k_cmp, v_cmp, k_slc, v_slc, k_win, v_win, gate_raw, q_norm_g, k_norm_g,
              cmp_pos, cmp_k_w1, cmp_k_w2, cmp_v_w1, cmp_v_w2, t5_table):
    B, T = q.shape[0], q.shape[1]
    dt = q.dtype
    H, dh = NSA_HEADS, HEAD_DIM
    scale = dh ** -0.5
    q = rms_norm(q.reshape(B, T, H, dh), q_norm_g) * scale
    k_slc = rms_norm(k_slc, k_norm_g)
    k_win = rms_norm(k_win, k_norm_g)
    t = jnp.arange(T)

    nc = T // CMP_STRIDE - 1

    def compress(kv, w1, w2):
        ch = kv.reshape(B, T // CMP_STRIDE, CMP_STRIDE, dh)
        blocks = jnp.concatenate([ch[:, :-1], ch[:, 1:]], axis=2) + cmp_pos
        hid = jax.nn.silu(blocks.reshape(B, nc, CMP_BLOCK * dh) @ w1)
        return hid @ w2

    kc = rms_norm(compress(k_cmp, cmp_k_w1, cmp_k_w2), k_norm_g)
    vc = compress(v_cmp, cmp_v_w1, cmp_v_w2)
    cmp_end = jnp.arange(nc) * CMP_STRIDE + CMP_BLOCK - 1
    cmp_dist = t[:, None] - cmp_end[None, :]
    cmp_bias = t5_table[t5_bucket(cmp_dist)].transpose(2, 0, 1)
    cmp_logits = jnp.einsum("bthd,bnd->bhtn", q, kc) + cmp_bias
    p_cmp = masked_softmax(cmp_logits, cmp_dist >= 0)
    o_cmp = jnp.einsum("bhtn,bnd->bthd", p_cmp.astype(dt), vc)

    nblk = T // SLC_BLOCK
    n_sel = min(N_SLC, nblk)
    ci = np.arange(nc)[:, None]
    bj = np.arange(nblk)[None, :]
    overlap = ((ci * CMP_STRIDE < (bj + 1) * SLC_BLOCK)
               & (ci * CMP_STRIDE + CMP_BLOCK > bj * SLC_BLOCK)).astype(np.float32)
    score = jnp.sum(p_cmp, axis=1) @ jnp.asarray(overlap)
    cur = (t // SLC_BLOCK)[:, None]
    blk = jnp.arange(nblk)[None, :]
    forced = (blk == 0) | ((cur - blk >= 0) & (cur - blk < N_LOCAL_SLC))
    score = jnp.where(forced, FORCE, score)
    score = jnp.where(blk <= cur, score, -FORCE)
    _, sel_idx = lax.top_k(score, n_sel)

    ks_blocks = k_slc.reshape(B, nblk, SLC_BLOCK, dh)
    vs_blocks = v_slc.reshape(B, nblk, SLC_BLOCK, dh)
    kw_p = jnp.pad(k_win, ((0, 0), (WINDOW, 0), (0, 0)))
    vw_p = jnp.pad(v_win, ((0, 0), (WINDOW, 0), (0, 0)))
    nq = T // Q_BLOCK
    J = n_sel * SLC_BLOCK

    def qblock(i):
        s = i * Q_BLOCK
        qb = lax.dynamic_slice_in_dim(q, s, Q_BLOCK, axis=1)
        tq = s + jnp.arange(Q_BLOCK)
        kwb = lax.dynamic_slice_in_dim(kw_p, s, WINDOW + Q_BLOCK, axis=1)
        vwb = lax.dynamic_slice_in_dim(vw_p, s, WINDOW + Q_BLOCK, axis=1)
        kpos = s - WINDOW + jnp.arange(WINDOW + Q_BLOCK)
        wd = tq[:, None] - kpos[None, :]
        wmask = (wd >= 0) & (wd < WINDOW) & (kpos[None, :] >= 0)
        wl = jnp.einsum("bqhd,bkd->bhqk", qb, kwb) + t5_table[t5_bucket(wd)].transpose(2, 0, 1)
        o_w = jnp.einsum("bhqk,bkd->bqhd", masked_softmax(wl, wmask).astype(dt), vwb)
        idx = lax.dynamic_slice_in_dim(sel_idx, s, Q_BLOCK, axis=1)
        ksel = jax.vmap(lambda kb, ib: kb[ib])(ks_blocks, idx)
        vsel = jax.vmap(lambda vb, ib: vb[ib])(vs_blocks, idx)
        spos = idx[..., None] * SLC_BLOCK + jnp.arange(SLC_BLOCK)
        sd = (tq[None, :, None, None] - spos).reshape(B, Q_BLOCK, J)
        sl = jnp.einsum("bqhd,bqnsd->bhqns", qb, ksel).reshape(B, H, Q_BLOCK, J)
        sl = sl + t5_table[t5_bucket(sd)].transpose(0, 3, 1, 2)
        ps = masked_softmax(sl, (sd >= 0)[:, None]).astype(dt)
        o_s = jnp.einsum("bhqj,bqjd->bqhd", ps, vsel.reshape(B, Q_BLOCK, J, dh))
        return o_w, o_s

    o_win, o_slc = lax.map(qblock, jnp.arange(nq))
    o_win = o_win.transpose(1, 0, 2, 3, 4).reshape(B, T, H, dh)
    o_slc = o_slc.transpose(1, 0, 2, 3, 4).reshape(B, T, H, dh)

    g = jax.nn.sigmoid(gate_raw.reshape(B, T, H, 3))
    o = g[..., 0:1] * o_cmp + g[..., 1:2] * o_slc + g[..., 2:3] * o_win
    return o.reshape(B, T, GROUP_WIDTH)

def short_conv_mixer(b_gate, c_gate, xs, conv_w):
    return b_gate * causal_dwconv(c_gate * xs, conv_w)

def to_chunks(a, L):
    B, T, H = a.shape[:3]
    a = a.reshape((B, T // L, L, H) + a.shape[3:])
    return a.transpose((1, 0, 3, 2) + tuple(range(4, a.ndim)))

def from_chunks(a):
    N, B, H, L, d = a.shape
    return a.transpose(1, 0, 3, 2, 4).reshape(B, N * L, H, d)

def chunk_gated_delta_rule(q, k, v, g, beta):
    f32 = jnp.float32
    L = GDN_CHUNK
    q, k, v = (to_chunks(a.astype(f32), L) for a in (q, k, v))
    g = to_chunks(g.astype(f32), L)
    beta = to_chunks(beta.astype(f32), L)
    gc = jnp.cumsum(g, axis=-1)
    incl = jnp.tril(jnp.ones((L, L), bool))
    strict = jnp.tril(jnp.ones((L, L), bool), -1)
    seg = jnp.exp(jnp.where(incl, gc[..., :, None] - gc[..., None, :], -jnp.inf))
    kb = k * beta[..., None]
    a_mat = jnp.where(strict, jnp.einsum("nbhid,nbhjd->nbhij", kb, k) * seg, 0.0) + jnp.eye(L, dtype=f32)
    rhs = jnp.concatenate([v * beta[..., None], kb * jnp.exp(gc)[..., None]], axis=-1)
    sol = lax.linalg.triangular_solve(a_mat, rhs, left_side=True, lower=True, unit_diagonal=True)
    u, w = sol[..., :HEAD_DIM], sol[..., HEAD_DIM:]
    qk = jnp.einsum("nbhid,nbhjd->nbhij", q, k) * seg
    q_dec = q * jnp.exp(gc)[..., None]
    k_dec = k * jnp.exp(gc[..., -1:] - gc)[..., None]
    g_tot = jnp.exp(gc[..., -1])

    def step(S, inp):
        u_c, w_c, qd_c, kd_c, qk_c, gt_c = inp
        v_new = u_c - jnp.einsum("bhlk,bhkv->bhlv", w_c, S)
        o = jnp.einsum("bhlk,bhkv->bhlv", qd_c, S) + jnp.einsum("bhij,bhjv->bhiv", qk_c, v_new)
        S = S * gt_c[..., None, None] + jnp.einsum("bhlk,bhlv->bhkv", kd_c, v_new)
        return S, o

    S0 = jnp.zeros(u.shape[1:3] + (HEAD_DIM, HEAD_DIM), f32)
    _, o = lax.scan(step, S0, (u, w, q_dec, k_dec, qk, g_tot))
    return from_chunks(o)

def gated_deltanet(q, k, v, beta_raw, alpha_raw, z, conv_w, A_log, dt_bias, norm_g):
    B, T = q.shape[0], q.shape[1]
    qkv = jax.nn.silu(causal_dwconv(jnp.concatenate([q, k, v], axis=-1), conv_w))
    q, k, v = (a.reshape(B, T, GDN_HEADS, HEAD_DIM) for a in jnp.split(qkv, 3, axis=-1))
    q = l2_norm(q) * HEAD_DIM ** -0.5
    k = l2_norm(k)
    beta = jax.nn.sigmoid(beta_raw)
    g = -jnp.exp(A_log) * jax.nn.softplus(alpha_raw + dt_bias)
    o = chunk_gated_delta_rule(q, k, v, g, beta).astype(z.dtype)
    o = rms_norm(o, norm_g) * jax.nn.silu(z.reshape(B, T, GDN_HEADS, HEAD_DIM))
    return o.reshape(B, T, GROUP_WIDTH)

def mlstm_chunkwise(q, k, v, i_pre, f_pre):
    f32 = jnp.float32
    L = MLSTM_CHUNK
    q, k, v = (to_chunks(a.astype(f32), L) for a in (q, k, v))
    log_i = to_chunks(i_pre.astype(f32), L)
    log_f = to_chunks(jax.nn.log_sigmoid(f_pre.astype(f32)), L)
    b = jnp.cumsum(log_f, axis=-1)
    incl = jnp.tril(jnp.ones((L, L), bool))
    log_w = jnp.where(incl, b[..., :, None] - b[..., None, :] + log_i[..., None, :], -jnp.inf)
    m_intra = jnp.max(log_w, axis=-1)
    log_w_end = b[..., -1:] - b + log_i
    m_end = jnp.max(log_w_end, axis=-1)
    qk = jnp.einsum("nbhid,nbhjd->nbhij", q, k)

    def step(carry, inp):
        C, n, m = carry
        q_c, k_c, v_c, b_c, lw_c, mi_c, lwe_c, me_c, qk_c = inp
        log_inter = b_c + m[..., None]
        m_t = jnp.maximum(log_inter, mi_c)
        w_inter = jnp.exp(log_inter - m_t)
        s = qk_c * jnp.exp(lw_c - m_t[..., None])
        num = (w_inter[..., None] * jnp.einsum("bhlk,bhkv->bhlv", q_c, C)
               + jnp.einsum("bhij,bhjv->bhiv", s, v_c))
        den = w_inter * jnp.einsum("bhlk,bhk->bhl", q_c, n) + jnp.sum(s, axis=-1)
        h = num / jnp.maximum(jnp.abs(den), jnp.exp(-m_t))[..., None]
        m_new = jnp.maximum(b_c[..., -1] + m, me_c)
        w_old = jnp.exp(b_c[..., -1] + m - m_new)
        w_new = jnp.exp(lwe_c - m_new[..., None])
        C = w_old[..., None, None] * C + jnp.einsum("bhl,bhlk,bhlv->bhkv", w_new, k_c, v_c)
        n = w_old[..., None] * n + jnp.einsum("bhl,bhlk->bhk", w_new, k_c)
        return (C, n, m_new), h

    Bsz, H = q.shape[1], q.shape[2]
    carry0 = (jnp.zeros((Bsz, H, HEAD_DIM, HEAD_DIM), f32), jnp.zeros((Bsz, H, HEAD_DIM), f32),
              jnp.zeros((Bsz, H), f32))
    _, h = lax.scan(step, carry0, (q, k, v, b, log_w, m_intra, log_w_end, m_end, qk))
    return from_chunks(h)

def mlstm_mixer(q, k, v, i_raw, f_raw, o_raw, f_bias, norm_g):
    B, T = q.shape[0], q.shape[1]
    heads = lambda a: a.reshape(B, T, MLSTM_HEADS, HEAD_DIM)
    h = mlstm_chunkwise(heads(q), heads(k) * HEAD_DIM ** -0.5, heads(v), i_raw, f_raw + f_bias)
    h = rms_norm(h.astype(q.dtype), norm_g) * jax.nn.sigmoid(heads(o_raw))
    return h.reshape(B, T, GROUP_WIDTH)

def first_inputs(seed: int = 0) -> dict:
    key = jax.random.key(seed)
    ks = jax.random.split(key, 32)
    L, D, F = DEPTH, D_MODEL, D_FF
    nrm = lambda k, shape, s: jax.random.normal(k, shape, jnp.float32) * s
    dt = jnp.exp(jax.random.uniform(ks[22], (L, GDN_HEADS), jnp.float32, math.log(1e-3), math.log(1e-1)))
    return {
        "x": nrm(ks[0], (BATCH, SEQ, D), 1.0),
        "c": nrm(ks[1], (BATCH, D), 1.0),
        "ada_w": nrm(ks[2], (L, D, 3 * N_SUBLAYERS * D), 0.5 * D ** -0.5),
        "ada_b": nrm(ks[3], (L, 3 * N_SUBLAYERS * D), 0.02),
        "norm_g": 1.0 + nrm(ks[4], (L, N_SUBLAYERS, D), 0.02),
        "ffn1_w13": nrm(ks[5], (L, D, 2 * F), D ** -0.5),
        "ffn1_w2": nrm(ks[6], (L, F, D), F ** -0.5),
        "ffn2_w13": nrm(ks[7], (L, D, 2 * F), D ** -0.5),
        "ffn2_w2": nrm(ks[8], (L, F, D), F ** -0.5),
        "w_in": nrm(ks[9], (L, D, D_IN), D ** -0.5),
        "b_in": nrm(ks[10], (L, D_IN), 0.02),
        "q_norm_g": 1.0 + nrm(ks[11], (L, HEAD_DIM), 0.02),
        "k_norm_g": 1.0 + nrm(ks[12], (L, HEAD_DIM), 0.02),
        "cmp_pos": nrm(ks[13], (L, CMP_BLOCK, HEAD_DIM), 0.1),
        "cmp_k_w1": nrm(ks[14], (L, CMP_BLOCK * HEAD_DIM, CMP_HIDDEN), (CMP_BLOCK * HEAD_DIM) ** -0.5),
        "cmp_k_w2": nrm(ks[15], (L, CMP_HIDDEN, HEAD_DIM), CMP_HIDDEN ** -0.5),
        "cmp_v_w1": nrm(ks[16], (L, CMP_BLOCK * HEAD_DIM, CMP_HIDDEN), (CMP_BLOCK * HEAD_DIM) ** -0.5),
        "cmp_v_w2": nrm(ks[17], (L, CMP_HIDDEN, HEAD_DIM), CMP_HIDDEN ** -0.5),
        "t5_table": nrm(ks[18], (N_BUCKETS, NSA_HEADS), 0.5),
        "sc_conv_w": nrm(ks[19], (L, SC_WIDTH, GROUP_WIDTH), SC_WIDTH ** -0.5),
        "gdn_conv_w": nrm(ks[20], (L, GDN_CONV, 3 * GROUP_WIDTH), GDN_CONV ** -0.5),
        "gdn_A_log": jnp.log(jax.random.uniform(ks[21], (L, GDN_HEADS), jnp.float32, 1.0, 16.0)),
        "gdn_dt_bias": dt + jnp.log(-jnp.expm1(-dt)),
        "gdn_norm_g": 1.0 + nrm(ks[23], (L, HEAD_DIM), 0.02),
        "mlstm_f_bias": 3.0 + jax.random.uniform(ks[24], (L, MLSTM_HEADS), jnp.float32, 0.0, 3.0),
        "mlstm_norm_g": 1.0 + nrm(ks[25], (L, HEAD_DIM), 0.02),
        "mix_norm_g": 1.0 + nrm(ks[26], (L, 2, GROUP_WIDTH), 0.02),
        "w_out": nrm(ks[27], (L, D_MIX, D), D_MIX ** -0.5),
    }

def first_block(x, c, ada_w, ada_b, norm_g, ffn1_w13, ffn1_w2, ffn2_w13, ffn2_w2, w_in, b_in,
              q_norm_g, k_norm_g, cmp_pos, cmp_k_w1, cmp_k_w2, cmp_v_w1, cmp_v_w2, t5_table,
              sc_conv_w, gdn_conv_w, gdn_A_log, gdn_dt_bias, gdn_norm_g, mlstm_f_bias,
              mlstm_norm_g, mix_norm_g, w_out):
    B, T, D = x.shape
    names = [n for n, _ in IN_LAYOUT]
    splits = np.cumsum([s for _, s in IN_LAYOUT])[:-1].tolist()
    cond = jax.nn.silu(c)
    for l in range(DEPTH):
        mod = (cond @ ada_w[l] + ada_b[l]).reshape(B, N_SUBLAYERS, 3, 1, D)
        h = adaln_pre(x, norm_g[l, 0], mod[:, 0, 0], mod[:, 0, 1])
        x = x + 0.5 * mod[:, 0, 2] * swiglu(h, ffn1_w13[l], ffn1_w2[l])
        h = adaln_pre(x, norm_g[l, 1], mod[:, 1, 0], mod[:, 1, 1])
        p = dict(zip(names, jnp.split(h @ w_in[l] + b_in[l], splits, axis=-1)))
        y_a = nsa_mixer(p["a_q"], p["a_k_cmp"], p["a_v_cmp"], p["a_k_slc"], p["a_v_slc"],
                        p["a_k_win"], p["a_v_win"], p["a_gate"], q_norm_g[l], k_norm_g[l],
                        cmp_pos[l], cmp_k_w1[l], cmp_k_w2[l], cmp_v_w1[l], cmp_v_w2[l], t5_table)
        y_b = short_conv_mixer(p["b_b"], p["b_c"], p["b_x"], sc_conv_w[l])
        y_c = gated_deltanet(p["c_q"], p["c_k"], p["c_v"], p["c_beta"], p["c_alpha"], p["c_z"],
                             gdn_conv_w[l], gdn_A_log[l], gdn_dt_bias[l], gdn_norm_g[l])
        y_d = mlstm_mixer(p["d_q"], p["d_k"], p["d_v"], p["d_i"], p["d_f"], p["d_o"],
                          mlstm_f_bias[l], mlstm_norm_g[l])
        y = jnp.concatenate([rms_norm(y_a, mix_norm_g[l, 0]), rms_norm(y_b, mix_norm_g[l, 1]), y_c, y_d],
                            axis=-1)
        x = x + mod[:, 1, 2] * (y @ w_out[l])
        h = adaln_pre(x, norm_g[l, 2], mod[:, 2, 0], mod[:, 2, 1])
        x = x + 0.5 * mod[:, 2, 2] * swiglu(h, ffn2_w13[l], ffn2_w2[l])
    return x


D_MIX_2 = D_MODEL
D_SGU = D_MIX_2 // 2
SGU_GROUPS = 4
SGU_GROUP_DIM = D_SGU // SGU_GROUPS
CHUNK = 128
D_ATTN = D_MIX_2 - D_SGU
N_HEADS = 4
HEAD_DIM_2 = D_ATTN // N_HEADS // 2
V_HEAD_DIM = 2 * HEAD_DIM_2
ROT_DIM = HEAD_DIM_2 // 4
ROPE_THETA = 500000.0
CONV_WIDTH = 3
D_IN_2 = 2 * D_SGU + 3 * D_ATTN


def rmsnorm(x, g):
    xf = x.astype(jnp.float32)
    y = xf * lax.rsqrt(jnp.mean(xf * xf, axis=-1, keepdims=True) + EPS)
    return (y * g.astype(jnp.float32)).astype(x.dtype)

def apply_partial_rope(t, cos, sin):
    half = ROT_DIM // 2
    t1 = t[..., :half]
    t2 = t[..., half:ROT_DIM]
    rot = jnp.concatenate([t1 * cos - t2 * sin, t2 * cos + t1 * sin], axis=-1)
    return jnp.concatenate([rot.astype(t.dtype), t[..., ROT_DIM:]], axis=-1)

def sgu_mixer(u, v, v_gain, w_s, b_s):
    B, S, _ = u.shape
    n_chunks = S // CHUNK
    vg = rmsnorm(v.reshape(B, S, SGU_GROUPS, SGU_GROUP_DIM), v_gain.reshape(SGU_GROUPS, SGU_GROUP_DIM))
    vg = vg.reshape(B, n_chunks, CHUNK, SGU_GROUPS, SGU_GROUP_DIM)
    causal = jnp.tril(jnp.ones((CHUNK, CHUNK), dtype=bool))
    w = jnp.where(causal[None], w_s, jnp.zeros_like(w_s))
    mixed = jnp.einsum('gpq,bcqgd->bcpgd', w, vg) + b_s.T[None, None, :, :, None]
    return u * mixed.reshape(B, S, D_SGU)

def diff_attention(q, k, v, positions, lq1, lk1, lq2, lk2, subln_g, layer_idx):
    B, S, _ = q.shape
    q = q.reshape(B, S, N_HEADS, 2, HEAD_DIM_2)
    k = k.reshape(B, S, N_HEADS, 2, HEAD_DIM_2)
    v = v.reshape(B, S, N_HEADS, V_HEAD_DIM)
    inv_freq = ROPE_THETA ** (-jnp.arange(0, ROT_DIM, 2, dtype=jnp.float32) / ROT_DIM)
    ang = positions.astype(jnp.float32)[..., None] * inv_freq
    cos = jnp.cos(ang)[:, :, None, None, :]
    sin = jnp.sin(ang)[:, :, None, None, :]
    q = apply_partial_rope(q, cos, sin)
    k = apply_partial_rope(k, cos, sin)

    lambda_init = 0.8 - 0.6 * float(np.exp(-0.3 * layer_idx))
    lam = (jnp.exp(jnp.sum(lq1.astype(jnp.float32) * lk1.astype(jnp.float32)))
           - jnp.exp(jnp.sum(lq2.astype(jnp.float32) * lk2.astype(jnp.float32)))
           + lambda_init)
    scale = HEAD_DIM_2 ** -0.5

    outs = []
    for start in range(0, S, Q_BLOCK):
        end = start + Q_BLOCK
        qb = q[:, start:end]
        kb = k[:, :end]
        scores = jnp.einsum('bqhmd,bkhmd->bhmqk', qb, kb).astype(jnp.float32) * scale
        q_idx = start + jnp.arange(Q_BLOCK)
        k_idx = jnp.arange(end)
        mask = k_idx[None, :] <= q_idx[:, None]
        scores = jnp.where(mask, scores, -jnp.inf)
        p = jax.nn.softmax(scores, axis=-1)
        attn = p[:, :, 0] - lam * p[:, :, 1]
        outs.append(jnp.einsum('bhqk,bkhd->bqhd', attn.astype(v.dtype), v[:, :end]))
    o = jnp.concatenate(outs, axis=1)
    o = rmsnorm(o, subln_g) * (1.0 - lambda_init)
    return o.reshape(B, S, D_ATTN)

def conv_ffn(h, w_up, conv_w, conv_b, w_down):
    S = h.shape[1]
    up = h @ w_up
    up_p = jnp.pad(up, ((0, 0), (CONV_WIDTH - 1, 0), (0, 0)))
    conv = conv_b
    for j in range(CONV_WIDTH):
        conv = conv + up_p[:, j:j + S] * conv_w[j]
    gate, val = jnp.split(conv, 2, axis=-1)
    return (jax.nn.silu(gate) * val) @ w_down

def second_inputs(seed: int = 0) -> dict:
    key = jax.random.key(seed)
    ks = jax.random.split(key, 20)
    f32 = jnp.float32
    x = jax.random.normal(ks[0], (BATCH, SEQ, D_MODEL), f32)
    positions = jnp.tile(jnp.arange(SEQ, dtype=jnp.int32)[None, :], (BATCH, 1))
    attn_norm = 1.0 + 0.02 * jax.random.normal(ks[1], (DEPTH, D_MODEL), f32)
    w_in = jax.random.normal(ks[2], (DEPTH, D_MODEL, D_IN_2), f32) * D_MODEL ** -0.5
    sgu_v_norm = 1.0 + 0.02 * jax.random.normal(ks[3], (DEPTH, D_SGU), f32)
    sgu_w_spatial = jax.random.normal(ks[4], (DEPTH, SGU_GROUPS, CHUNK, CHUNK), f32) * CHUNK ** -0.5
    sgu_b_spatial = 1.0 + 0.02 * jax.random.normal(ks[5], (DEPTH, SGU_GROUPS, CHUNK), f32)
    lambda_q1 = 0.1 * jax.random.normal(ks[6], (DEPTH, HEAD_DIM_2), f32)
    lambda_k1 = 0.1 * jax.random.normal(ks[7], (DEPTH, HEAD_DIM_2), f32)
    lambda_q2 = 0.1 * jax.random.normal(ks[8], (DEPTH, HEAD_DIM_2), f32)
    lambda_k2 = 0.1 * jax.random.normal(ks[9], (DEPTH, HEAD_DIM_2), f32)
    subln_gain = 1.0 + 0.02 * jax.random.normal(ks[10], (DEPTH, V_HEAD_DIM), f32)
    w_out = jax.random.normal(ks[11], (DEPTH, D_MIX_2, D_MODEL), f32) * D_MIX_2 ** -0.5
    ffn_norm = 1.0 + 0.02 * jax.random.normal(ks[12], (DEPTH, D_MODEL), f32)
    w_up = jax.random.normal(ks[13], (DEPTH, D_MODEL, 2 * D_FF), f32) * D_MODEL ** -0.5
    conv_w = jax.random.normal(ks[14], (DEPTH, CONV_WIDTH, 2 * D_FF), f32) * CONV_WIDTH ** -0.5
    conv_b = 0.02 * jax.random.normal(ks[15], (DEPTH, 2 * D_FF), f32)
    w_down = jax.random.normal(ks[16], (DEPTH, D_FF, D_MODEL), f32) * D_FF ** -0.5
    final_norm = 1.0 + 0.02 * jax.random.normal(ks[17], (D_MODEL,), f32)
    return {"x": x, "positions": positions, "attn_norm": attn_norm, "w_in": w_in,
            "sgu_v_norm": sgu_v_norm, "sgu_w_spatial": sgu_w_spatial, "sgu_b_spatial": sgu_b_spatial,
            "lambda_q1": lambda_q1, "lambda_k1": lambda_k1, "lambda_q2": lambda_q2, "lambda_k2": lambda_k2,
            "subln_gain": subln_gain, "w_out": w_out, "ffn_norm": ffn_norm, "w_up": w_up,
            "conv_w": conv_w, "conv_b": conv_b, "w_down": w_down, "final_norm": final_norm}

def second_block(x, positions, attn_norm, w_in, sgu_v_norm, sgu_w_spatial, sgu_b_spatial,
              lambda_q1, lambda_k1, lambda_q2, lambda_k2, subln_gain, w_out, ffn_norm,
              w_up, conv_w, conv_b, w_down, final_norm):
    h = x
    for l in range(DEPTH):
        n = rmsnorm(h, attn_norm[l])
        proj = n @ w_in[l]
        u, v_sgu, q, k, v_att = jnp.split(
            proj, [D_SGU, 2 * D_SGU, 2 * D_SGU + D_ATTN, 2 * D_SGU + 2 * D_ATTN], axis=-1)
        u = jax.nn.gelu(u)
        v_sgu = jax.nn.gelu(v_sgu)
        y_sgu = sgu_mixer(u, v_sgu, sgu_v_norm[l], sgu_w_spatial[l], sgu_b_spatial[l])
        y_att = diff_attention(q, k, v_att, positions, lambda_q1[l], lambda_k1[l],
                               lambda_q2[l], lambda_k2[l], subln_gain[l], l)
        mixed = jnp.concatenate([y_sgu, y_att], axis=-1)
        h = h + mixed @ w_out[l]
        h = h + conv_ffn(rmsnorm(h, ffn_norm[l]), w_up[l], conv_w[l], conv_b[l], w_down[l])
    return rmsnorm(h, final_norm)


_first_inputs = second_inputs


def second_inputs(seed=0):
    import zlib

    import numpy as np

    out = dict(_first_inputs(seed))
    spreads = {}
    factors = {'sgu_v_norm': 8.0,
     'sgu_b_spatial': 5.202,
     'lambda_q2': 4.067,
     'subln_gain': 4.3,
     'ffn_norm': 3.44,
     'conv_b': 3.186,
     'final_norm': 2.863}
    for name, (base, spread) in spreads.items():
        noise = np.random.default_rng([zlib.crc32(name.encode()), seed]).standard_normal(out[name].shape)
        drawn = base * np.exp(spread * noise) if base else spread * noise
        out[name] = __import__('jax').numpy.asarray(drawn.astype(out[name].dtype))
    for name, factor in factors.items():
        out[name] = (out[name] * factor).astype(out[name].dtype)
    return out


_narrow_inputs = second_inputs


def second_inputs(seed=0):

    out = dict(_narrow_inputs(seed))
    wider = {'sgu_v_norm': 3.57, 'sgu_b_spatial': 3.2, 'subln_gain': 3.07, 'final_norm': 3.23}
    for name, times in wider.items():
        mean = out[name].mean()
        out[name] = (mean + times * (out[name] - mean)).astype(out[name].dtype)
    return out


def setup_inputs(seed=0):
    out = dict(first_inputs(seed))
    for name, value in second_inputs(seed + 1).items():
        if name != "x":
            out[name + "_2"] = value
    return out


def reference(
    x, c, ada_w, ada_b, norm_g, ffn1_w13, ffn1_w2, ffn2_w13, ffn2_w2, w_in, b_in, q_norm_g,
    k_norm_g, cmp_pos, cmp_k_w1, cmp_k_w2, cmp_v_w1, cmp_v_w2, t5_table, sc_conv_w, gdn_conv_w,
    gdn_A_log, gdn_dt_bias, gdn_norm_g, mlstm_f_bias, mlstm_norm_g, mix_norm_g, w_out,
    positions_2, attn_norm_2, w_in_2, sgu_v_norm_2, sgu_w_spatial_2, sgu_b_spatial_2,
    lambda_q1_2, lambda_k1_2, lambda_q2_2, lambda_k2_2, subln_gain_2, w_out_2, ffn_norm_2,
    w_up_2, conv_w_2, conv_b_2, w_down_2, final_norm_2,
):
    x = first_block(
        x, c, ada_w, ada_b, norm_g, ffn1_w13, ffn1_w2, ffn2_w13, ffn2_w2, w_in, b_in, q_norm_g,
        k_norm_g, cmp_pos, cmp_k_w1, cmp_k_w2, cmp_v_w1, cmp_v_w2, t5_table, sc_conv_w,
        gdn_conv_w, gdn_A_log, gdn_dt_bias, gdn_norm_g, mlstm_f_bias, mlstm_norm_g, mix_norm_g,
        w_out,
    )
    return second_block(
        x, positions_2, attn_norm_2, w_in_2, sgu_v_norm_2, sgu_w_spatial_2, sgu_b_spatial_2,
        lambda_q1_2, lambda_k1_2, lambda_q2_2, lambda_k2_2, subln_gain_2, w_out_2, ffn_norm_2,
        w_up_2, conv_w_2, conv_b_2, w_down_2, final_norm_2,
    )


_drawn_inputs = setup_inputs


def setup_inputs(seed=0):
    import zlib

    import numpy as np

    out = dict(_drawn_inputs(seed))
    spreads = {}
    factors = {'q_norm_g': 8.0,
     'k_norm_g': 8.0,
     'gdn_norm_g': 8.0,
     'mlstm_norm_g': 8.0,
     'mix_norm_g': 2.828,
     'lambda_q1_2': 4.917,
     'lambda_k1_2': 3.483}
    for name, (base, spread) in spreads.items():
        noise = np.random.default_rng([zlib.crc32(name.encode()), seed]).standard_normal(out[name].shape)
        drawn = base * np.exp(spread * noise) if base else spread * noise
        out[name] = jnp.asarray(drawn.astype(out[name].dtype))
    for name, factor in factors.items():
        out[name] = (out[name] * factor).astype(out[name].dtype)
    return out
```

```python
from contextlib import ExitStack

import numpy as np

import concourse.bass as bass
from concourse import mybir

F32 = mybir.dt.float32
F32R = mybir.dt.float32r
I32 = mybir.dt.int32
ALU = mybir.AluOpType
ACT = mybir.ActivationFunctionType
AX = mybir.AxisListType

P = 128
T = 512
TT = T // P
D = 1024
KT = D // P
L = 2
FF = 2816
FT = FF // P
KH = FT // 2
EPS = 1e-6
NMOD = 9 * KT
N_NEXT = 3 * KT
ADA1 = 5 * KT // 2
ADA2 = 4 * KT // 2

U_UP1 = 0
U_DN1 = U_UP1 + 2 * FT
U_IN = U_DN1 + 2 * KT
N_IN = 30
U_CMP = U_IN + N_IN
U_OUT = U_CMP + 8
U_UP2 = U_OUT + KT
U_DN2 = U_UP2 + 2 * FT
U_END = U_DN2 + 2 * KT

C_NORM = 0
C_ADAB = C_NORM + 3 * KT
C_BIN = C_ADAB + NMOD
C_QG = C_BIN + N_IN
C_KG = C_QG + 1
C_SCW = C_KG + 1
C_GDW = C_SCW + 6
C_MIXB = C_GDW + 24
C_MIXA = C_MIXB + 2
C_GDN = C_MIXA + 2
C_MLS = C_GDN + 1
C_SMB = C_MLS + 1
C_SMA = C_SMB + 1
C_POS = C_SMA + 1
C_END1 = C_POS + 16

V_IN = 0
N_IN2 = 20
V_OUT = V_IN + N_IN2
V_UP = V_OUT + KT
V_DN = V_UP + 2 * FT

E_NORM = 0
E_FIN = E_NORM + 2 * KT
E_SGU = E_FIN + KT
E_SUB = E_SGU + 4
E_LAM = E_SUB + 1
E_LIN = E_LAM + 4
E_CW = E_LIN + 2
E_CB = E_CW + 6 * FT
E_END = E_CB + 2 * FT
QU, QV, QQ, QK_, QA, QY = 0, 4, 8, 12, 16, 20
Y2_TILES = (QU, QU + 1, QU + 2, QU + 3, QY, QY + 1, QY + 2, QY + 3)
ROT = 16
TURN = (6.28125, 0.0019350051879882812, float(2 * np.pi - 6.28125 - 0.0019350051879882812))
ROUND = 1.5 * 2 ** 23

PA_Q, PA_KS, PA_KW, PA_KC, PA_VC, PA_VSW, PS, PB_B, PB_C, PB_X = 0, 2, 3, 4, 5, 6, 7, 8, 10, 12
PC_Q, PC_K, PC_V, PC_Z, PD_Q, PD_K, PD_V, PD_O = 14, 16, 18, 20, 22, 24, 26, 28
R_I, R_F, R_AL, R_BE = 32, 64, 68, 96
K_BE, K_GC, K_A, K_M, NCOL = 12, 16, 20, 24, 28

H = 4
HD = 64
NB = 32
NCB = 31
MASKED = -1e30

Y_TILES = (PA_Q, PA_Q + 1, PB_B, PB_B + 1, PC_Z, PC_Z + 1, PD_O, PD_O + 1)
HEAD_NORMS = ((PA_Q, 1.0, 1), (PA_Q + 1, 1.0, 1), (PA_KS, 1.0 / HD, 0), (PA_KW, 1.0 / HD, 0),
              (PC_Q, 64.0, 1), (PC_Q + 1, 64.0, 1), (PC_K, 1.0, 0), (PC_K + 1, 1.0, 0))

X_ID, X_ONE, X_BO, X_CM, X_CMT, X_SA, X_CS, X_SG, X_EPS = 0, P, 2 * P, 3 * P, 4 * P, 5 * P, 5 * P + 4, 5 * P + 32, 5 * P + 33
X_E64 = X_EPS + 1
X_MS = X_E64 + 1
X_TRI = X_MS + NCOL
X_ROT = X_TRI + P
X_IF = X_ROT + P
X_END = X_IF + 1


def later(i):
    return not isinstance(i, int) or i > 0


def wt_count(u):
    return 2 * (u + 1) - (u + 1) // TT


def n_ar(k):
    return 5 + k


def n_mr(k):
    return 6 + k


def n_cols(k):
    return 7 + k


def n_bg(k):
    return 8 + k


def n_em(k):
    return 3 + k


def n_egc(k):
    return 4 * k - 3


def n_b_cx(k):
    return k


def n_b_y(k):
    return 2 * k + 1


def n_b_sq(k):
    return 2 * k + 2


def n_d_dd(k):
    return 4 * k - 2


def n_d_rc(k):
    return 4 * k - 1


def n_d_od(k):
    return 4 * k


def n_o_red(k):
    return 4 * k - 3


def n_o_nrm(k):
    return 4 * k - 2


def n_o_y(k):
    return 4 * ((k - 1) // 2) + (k - 1) % 2 + 3


def n_c_ktc(k):
    return k


def n_c_kbt(k):
    return 2 + k


def n_c_kb(k):
    return 3 + 2 * k


def n_c_vb(k):
    return 4 + 2 * k


def n_c_tmp(k):
    return 12 + k


def n_c_kd(k):
    return 3 * k - 2


def n_c_nn(k):
    return 3 * k - 1


def n_c_qk(k):
    return 3 * k


def n_c_n0(k):
    return 11 + 2 * k


def n_c_p0(k):
    return 12 + 2 * k


def n_c_vtc(k):
    return k


def n_c_egp(k):
    return 2 + k


def n_c_seg(k):
    return 4 + k


def n_c_x0(k):
    return 20 + k


def n_a_hc(k):
    return k


def n_a_hb(k):
    return 2 + k


def n_a_hd(k):
    return 3 + k


def n_a_hr(k):
    return 4 + k


def n_a_hid(k):
    return 5 + k


def n_a_vcz(k):
    return 6 + k


def n_a_kcf(k):
    return 7 + k


def n_a_kcq(k):
    return 8 + k


def n_a_vcb(k):
    return 9 + k


def n_a_kcn(k):
    return 13 + k


def n_a_v6(k):
    return 14 + k


def n_a_c1(k):
    return 6 * k - 5


def n_a_cmx(k):
    return 6 * k - 4


def n_a_cnm(k):
    return 6 * k - 3


def n_a_c2(k):
    return 6 * k - 2


def n_a_cs(k):
    return 6 * k - 1


def n_a_cg(k):
    return 6 * k


def n_a_rc(k):
    return 7 * k - 6


def n_a_cf(k):
    return 7 * k - 5


def n_a_y(k):
    return 7 * ((k - 1) // 5) + (k - 1) % 5 + 3


class Names:
    pass


def build(nc, a, out):
    ctx = ExitStack()
    with ctx:
        base = (nc.sbuf_base + 63) // 64 * 64
        arena = ctx.enter_context(nc.sbuf_tensor("arena", [P, (nc.sbuf_usable_end - base) // 4 - 16], F32))
        top = [base]

        def place(name, shape, dt=F32, at=None):
            size = 4 * int(np.prod(shape[1:]))
            if at is None:
                at = top[0]
                top[0] += (size + 31) // 32 * 32
            return nc.alloc_sbuf_tensor_at(name, shape, dt, offset=at)

        TB = 4 * T
        o_h = base + KT * TB
        o_g = o_h + 2 * KT * TB
        xT = place("xT", [P, KT, T])
        hH = place("hH", [P, KT, T], F32R)
        hL = place("hL", [P, KT, T], F32R)
        gH = place("gH", [P, FT, T], F32R)
        gL = place("gL", [P, FT, T], F32R)
        wR = [place(f"wR{i}", [P, KH, P]) for i in range(2)]
        wH = [place(f"wH{i}", [P, KH, P], F32R) for i in range(2)]
        wL = [place(f"wL{i}", [P, KH, P], F32R) for i in range(2)]
        sumsq = place("sumsq", [P, T])
        sqt = place("sqt", [P, T])
        rstd = place("rstd", [P, T])
        xn = place("xn", [P, 2, T])
        hf = place("hf", [P, 2, T])
        o_misc = top[0]
        sil = place("sil", [P, T])
        gf = place("gf", [P, T])
        cst = place("cst", [P, X_END])
        par = place("par", [P, max(C_END1, E_END)])
        mod = place("mod", [P, NMOD + N_NEXT])
        modA = place("modA", [P, 3 * KT])
        gate = place("gate", [P, 3 * KT])
        cond = place("cond", [P, D])
        acc = place("acc", [P, 2, 2])
        o_cst_end = {"bm": top[0]}
        bm = place("bm", [P, H, T])
        o_cst_end["cb"] = top[0]
        cb = place("cb", [P, TT, H, 32])
        tab = place("tab", [NB + 1, H])
        assert top[0] <= nc.sbuf_usable_end - 64, top[0] - nc.sbuf_usable_end
        pm = place("pm", [P, 2 * FT, T], at=o_g)
        ht = place("ht", [P, 2 * KT, T], at=o_h)
        xin = place("xin", [P, TT, D], at=o_g + 12 * TB)
        ada0 = [place(f"ada0{j}", [P, KT, D], at=at) for j, at in enumerate((o_g + 28 * TB, o_h, o_g + 28 * TB))]
        adaw = [place(f"adaw{j}", [P, D], at=at)
                for j, at in enumerate((o_misc - 4 * TB, o_misc - 2 * TB, o_g + 20 * TB, o_g + 42 * TB))]

        def pmv(name, tile, shape, dt=F32):
            return place(name, shape, dt, at=o_g + int(tile * TB))

        def htv(name, tile, shape, dt=F32):
            return place(name, shape, dt, at=o_h + int(tile * TB))

        OHR = pmv("ohr", 0, [NB + 1, 640])
        OHF = pmv("ohf", 2, [NB + 1, 1056])
        FLIP = pmv("flip", 5, [P, P])
        SKEW = pmv("skew", 6, [P, H, T])
        LM = pmv("LM", 30, [P, 7, P])
        RS = pmv("RS", 31.75, [P, T])
        w2k = pmv("w2k", 32.75, [P, 2, P])
        w2v = pmv("w2v", 33.25, [P, 2, HD])
        COL = pmv("COL", 33.5, [P, TT, NCOL])
        EM = pmv("EM", 33.75, [P, TT, H])
        EGC = pmv("EGC", 33.78125, [P, TT, H])
        NGC = pmv("NGC", 33.8125, [P, TT, H])
        BG = pmv("BG", 33.84375, [P, TT, H])
        DD = pmv("DD", 33.875, [P, TT, H])
        HR = pmv("HR", 33.90625, [P, TT, H])
        sma = pmv("sma", 33.9375, [P, 1])
        cv = xn
        nsq = hf
        smt = sumsq
        AR = sil
        MR = gf
        NM = [pm[:, 34 + h, :] for h in range(H)]
        VD = pmv("VD", 38, [P, TT, H, HD + 1])
        WD = pmv("WD", 40.5, [P, 2, P])
        WT_ = pmv("WTm", 41, [P, 2, T])
        ST_ = [htv(f"STm{i}", 4 * i, [P, TT, T]) for i in range(2)]
        OD = htv("OD", 8, [P, TT, H * HD])
        OQ = htv("OQ", 10, [P, TT, H * HD])
        SEG = [htv(f"SEG{h}", h, [P, TT, P]) for h in range(H)]
        ZZ = SEG
        NN = [htv(f"NN{h}", 4 + h, [P, TT, P]) for h in range(H)]
        XX = [pmv(f"XX{h}", PD_Q + h, [P, TT, P]) for h in range(H)]
        PP = [pmv(f"PP{h}", (26, 27, 34, 35)[h], [P, TT, P]) for h in range(H)]
        QK = [pmv(f"QK{h}", 36 + h, [P, TT, P]) for h in range(H)]
        TMP = [pmv(f"TMP{i}", 40 + i, [P, TT, P]) for i in range(2)]
        NK = TMP
        KD = [htv(f"KD{i}", 12 + i, [P, TT, P]) for i in range(2)]
        KB = [htv(f"KB{i}", 14 + i, [P, TT, P]) for i in range(2)]
        VB = [pmv(f"VB{i}", 42 + i, [P, TT, P]) for i in range(2)]
        KTM = [htv(f"KTM{i}", 8 + i, [P, TT, P]) for i in range(2)]
        VTM = [pmv(f"VTM{i}", PB_C + i, [P, TT, P]) for i in range(2)]
        EGP = [pmv(f"EGP{i}", PB_X + i, [P, T]) for i in range(2)]
        KBT = [pmv(f"KBT{i}", PC_V + i, [P, T]) for i in range(2)]
        UU = VTM
        WW = [pmv(f"WW{i}", PC_K + i, [P, T]) for i in range(2)]
        SSt = place("SSt", [P, 2, 2, P], at=o_misc - 4 * TB)
        VN = place("VN", [P, H, HD], at=o_misc - 2 * TB)
        X2 = place("X2", [P, 16, 32], at=o_misc - 4 * TB)
        X2H = [htv(f"X2H{i}", 12 + i, [P, 16, 32], F32R) for i in range(2)]
        X2L = [htv(f"X2L{i}", 14 + i, [P, 16, 32], F32R) for i in range(2)]
        o_s = o_misc - 7 * TB
        HID = place("HID", [P, 4, 32], at=o_s)
        HIE = place("HIE", [P, 4, 32], at=o_s + 512)
        HIC = place("HIC", [P, 4], at=o_s + 1024)
        KCF = place("KCF", [P, 32], at=o_s + 1088)
        KCQ = place("KCQ", [P, 32], at=o_s + 1088 + 128)
        VCB = place("VCB", [P, H, HD], at=o_s + TB)
        LC = place("LC", [P, H, 32], at=o_s + TB + 1536)
        PCT = place("PCT", [P, P], at=o_s + TB + 1024)
        KCB = place("KCB", [P, 2, 32], at=o_s + 1600)
        MX = place("MX", [P, 12], at=o_s + 1088 + 256)
        SM = place("SM", [P, 2, 12], at=o_s + 1408)
        CF = place("CF", [P, 12], at=o_s + 1504)
        V6 = htv("V6", 0, [P, TT, P])
        LL = [pmv(f"LL{i}", 34 + 4 * i, [P, H, T]) for i in range(2)]
        PTR = [htv(f"PTR{i}", 1 + i, [P, T]) for i in range(4)]
        YA = htv("YA", 6, [P, TT, H * HD])
        YT = htv("YT", 10, [P, H, HD])
        YQ = htv("YQ", 8, [P, TT, H * HD])

        o_bm = o_cst_end["bm"]
        COS = place("COS", [P, T], at=o_bm)
        SIN = place("SIN", [P, T], at=o_bm + TB)
        CMASK = place("CMASK", [P, T], at=o_bm + 2 * TB)
        WS = place("WS", [P, 4, P], at=o_bm + 3 * TB)
        BS = place("BS", [P, 4, P], at=o_cst_end["cb"])
        POSI = htv("POSI", 0, [P, T], I32)
        ANG = htv("ANG", 1, [P, T])
        TRN = htv("TRN", 2, [P, T])
        RED = [htv(f"RED{i}", 3 + i, [P, T]) for i in range(2)]
        VG = [htv(f"VG{g}", g, [P, TT, P]) for g in range(4)]
        LG = [htv(f"LG{i}", 4 + 2 * i, [P, 2, T]) for i in range(2)]
        AD = [htv(f"AD{i}", 8 + i, [P, T]) for i in range(2)]
        ADT = [htv(f"ADT{i}", 10 + i, [P, T]) for i in range(2)]
        RTM = [htv(f"RTM{i}", 12 + i, [P, T]) for i in range(2)]
        SGT = [htv(f"SGT{i}", 14 + i, [P, TT, P]) for i in range(2)]
        VA = [pmv(f"VA{h}", 24 + h, [P, TT, P]) for h in range(4)]
        YD = pmv("YD", 28, [P, TT, 4 * P])
        YDQ = pmv("YDQ", 32, [P, TT, 4 * P])
        MX2 = place("MX2", [P, 2, 2], at=o_s)
        NX2 = place("NX2", [P, 2, 2], at=o_s + 32)
        SM2 = place("SM2", [P, 2, 2], at=o_s + 64)
        RC2 = place("RC2", [P, 2, 2], at=o_s + 96)
        RT2 = place("RT2", [P, 2, 1], at=o_s + 128)
        LQ = place("LQ", [P, 2], at=o_s + 160)
        LE = place("LE", [P, 2], at=o_s + 192)
        NL = place("NL", [P, 1], at=o_s + 224)
        HR2 = place("HR2", [P, TT, 4], at=o_s + 256)

        ident = cst[:, X_ID:X_ID + P]
        ones = cst[:, X_ONE:X_ONE + P]
        heads = cst[:, X_BO:X_BO + P]
        causal = cst[:, X_CM:X_CM + P]
        causalT = cst[:, X_CMT:X_CMT + P]
        tri = cst[:, X_TRI:X_TRI + P]
        rot = cst[:, X_ROT:X_ROT + P]
        eps = cst[:, X_EPS:X_EPS + 1]
        eps64 = cst[:, X_E64:X_E64 + 1]
        bank = [ctx.enter_context(nc.psum_tensor(f"bank{i}", [P, 512], F32)) for i in range(8)]

        def col(c, n=1):
            return par[:, c:c + n]

        def cbank(i):
            return bank[(5, 7)[i % 2]]

        def bc(ap, shape):
            return ap.broadcast_to(shape)

        S = Names()
        layer_sems = []

        def sem(name, layered=True):
            s = ctx.enter_context(nc.semaphore(name))
            if layered:
                layer_sems.append(s)
            return s

        S.const_in = sem("const_in", False)
        S.x_in = sem("x_in", False)
        S.x_turned = sem("x_turned", False)
        S.x_copied = sem("x_copied", False)
        S.tab_in = sem("tab_in", False)
        S.tab_set = sem("tab_set", False)
        S.bias_ps = sem("bias_ps", False)
        S.bias_sb = sem("bias_sb", False)
        S.bias_out = sem("bias_out", False)
        S.skew_in = sem("skew_in", False)
        S.bm_ps = sem("bm_ps", False)
        S.bm_set = sem("bm_set", False)
        S.cb_ps = sem("cb_ps", False)
        S.cb_set = sem("cb_set", False)
        S.fin = sem("fin", False)
        S.stored0 = sem("stored0", False)
        S.stored1 = sem("stored1", False)
        S.release = sem("release", False)
        S.acked = sem("acked", False)
        S.pos_in = sem("pos_in", False)
        S.trig_v = sem("trig_v", False)
        S.trig_a = sem("trig_a", False)
        S.trig_free = sem("trig_free", False)
        S.first_sums = sem("first_sums", False)
        S.cond = sem("cond", False)
        S.ada0_in0 = sem("ada0_in0", False)
        S.ada0_in1 = sem("ada0_in1", False)
        S.ada0_in2 = sem("ada0_in2", False)
        S.ada0_done = sem("ada0_done", False)
        S.const2_in = sem("const2_in", False)
        S.first_sq = sem("first_sq", False)
        S.arrived = sem("arrived")
        S.w_in0 = sem("w_in0")
        S.w_in1 = sem("w_in1")
        S.w_hi = sem("w_hi")
        S.w_lo = sem("w_lo")
        S.w_used = sem("w_used")
        S.sil = sem("sil")
        S.g_mul = sem("g_mul")
        S.g_hi = sem("g_hi")
        S.g_lo = sem("g_lo")
        S.x_new = sem("x_new")
        S.par_in = sem("par_in")
        S.ada_in0 = sem("ada_in0")
        S.ada_in1 = sem("ada_in1")
        S.ada_in2 = sem("ada_in2")
        S.ada_in3 = sem("ada_in3")
        S.ada_sum = sem("ada_sum")
        S.ada_done = sem("ada_done")
        S.mod_set = sem("mod_set")
        S.pool = sem("pool")
        S.sumsq = sem("sumsq")
        S.ms = sem("ms")
        S.ln = sem("ln")
        S.rstd = sem("rstd")
        S.last_sq = sem("last_sq")
        S.hf = sem("hf")
        S.h_hi = sem("h_hi")
        S.h_lo = sem("h_lo")
        S.mixc_in0 = sem("mixc_in0")
        S.mixc_in1 = sem("mixc_in1")
        S.mixc_in2 = sem("mixc_in2")
        S.mixc_in3 = sem("mixc_in3")
        S.pm = sem("pm")
        S.cv = sem("cv")
        S.conv_silu = sem("conv_silu")
        S.g_sig = sem("g_sig")
        S.sm_v = sem("sm_v")
        S.sm_a = sem("sm_a")
        S.ar_ps = sem("ar_ps")
        S.colp = sem("colp")
        S.b_pool = sem("b_pool")
        S.b_cv = sem("b_cv")
        S.b_ss = sem("b_ss")
        S.b_rs = sem("b_rs")
        S.n_sq = sem("n_sq")
        S.n_ss = sem("n_ss")
        S.n_rs = sem("n_rs")
        S.n_out = sem("n_out")
        S.d_nmp = sem("d_nmp")
        S.d_nm = sem("d_nm")
        S.d_vt = sem("d_vt")
        S.d_vd = sem("d_vd")
        S.d_one = sem("d_one")
        S.d_s = sem("d_s")
        S.d_wd = sem("d_wd")
        S.d_wt = sem("d_wt")
        S.d_nd = sem("d_nd")
        S.d_post = sem("d_post")
        S.d_sv = sem("d_sv")
        S.o_sq = sem("o_sq")
        S.o_v = sem("o_v")
        S.o_rs = sem("o_rs")
        S.o_t = sem("o_t")
        S.c_kt = sem("c_kt")
        S.c_v1 = sem("c_v1")
        S.c_vt = sem("c_vt")
        S.c_a = sem("c_a")
        S.c_bp = sem("c_bp")
        S.c_gp = sem("c_gp")
        S.c_grp = sem("c_grp")
        S.c_v2 = sem("c_v2")
        S.c_kk = sem("c_kk")
        S.c_kq = sem("c_kq")
        S.c_qd = sem("c_qd")
        S.c_xt = sem("c_xt")
        S.c_nk = sem("c_nk")
        S.c_z = sem("c_z")
        S.c_zc = sem("c_zc")
        S.c_xz = sem("c_xz")
        S.c_xu = sem("c_xu")
        S.c_zp = sem("c_zp")
        S.c_pu = sem("c_pu")
        S.c_u = sem("c_u")
        S.c_uc = sem("c_uc")
        S.c_w = sem("c_w")
        S.c_wc = sem("c_wc")
        S.c_wp = sem("c_wp")
        S.c_vn = sem("c_vn")
        S.c_o = sem("c_o")
        S.c_od = sem("c_od")
        S.c_sp = sem("c_sp")
        S.c_st = sem("c_st")
        S.a_x2 = sem("a_x2")
        S.a_x2h = sem("a_x2h")
        S.a_x2l = sem("a_x2l")
        S.a_v = sem("a_v")
        S.a_he = sem("a_he")
        S.a_kc = sem("a_kc")
        S.a_kcs = sem("a_kcs")
        S.a_kcr = sem("a_kcr")
        S.a_vt = sem("a_vt")
        S.a_cl = sem("a_cl")
        S.a_cv = sem("a_cv")
        S.a_ce = sem("a_ce")
        S.a_ct = sem("a_ct")
        S.a_ctc = sem("a_ctc")
        S.a_co = sem("a_co")
        S.a_s = sem("a_s")
        S.a_l = sem("a_l")
        S.a_nm = sem("a_nm")
        S.a_e = sem("a_e")
        S.a_t = sem("a_t")
        S.a_tc = sem("a_tc")
        S.a_pv = sem("a_pv")
        S.a_yv = sem("a_yv")
        S.y_hi = sem("y_hi")
        S.y_lo = sem("y_lo")
        S.w_in = [S.w_in0, S.w_in1]
        S.ws_in = S.ada_in0
        S.bs_in = S.ada_in1
        S.ws_set = S.b_pool
        S.lam_v = S.b_cv
        S.lam_ps = S.b_ss
        S.lam_e = S.b_rs
        S.gelu = S.conv_silu
        S.rot_ps = S.c_kt
        S.rot_cos = S.c_qd
        S.rot_sin = S.c_v1
        S.rot_x = S.c_v2
        S.va_t = S.d_vt
        S.va_sb = S.d_vd
        S.vg_t = S.c_vt
        S.vg_sb = S.c_a
        S.mixed = S.c_u
        S.mix_b = S.c_uc
        S.mix_y = S.c_w
        S.s_ps = S.a_s
        S.s_max = S.a_l
        S.s_neg = S.a_nm
        S.s_exp = S.a_e
        S.s_small = S.a_v
        S.s_diff = S.a_cv
        S.s_t = S.a_t
        S.s_tsb = S.a_tc
        S.s_val = S.a_pv
        S.s_y = S.a_yv
        S.f_tap = S.c_z
        S.f_conv = S.c_xu
        S.ada_in = [S.ada_in0, S.ada_in1, S.ada_in2, S.ada_in3]
        S.ada0_in = [S.ada0_in0, S.ada0_in1, S.ada0_in2]
        S.stored = [S.stored0, S.stored1]
        bias_dram = nc.dram_tensor("bias_by_distance", (H, 640), F32, kind="Internal").ap()

        block = ctx.enter_context(nc.Block())

        def end_layer(e, l):
            e.sem_inc(S.arrived, 1)
            e.wait_ge(S.release, l + 1)
            e.sem_inc(S.acked, 1)

        @block.sync
        def _(sp):
            sp.dma_start(cst[:, :], a["cst"]).then_inc(S.const_in, 16)
            sp.dma_start(cond[:, :], bc(a["c"], [P, D])).then_inc(S.const_in, 16)
            sp.dma_start(xin[:, :, :], a["x"].rearrange("(t p) d -> p t d", p=P)).then_inc(S.x_in, 16)
            sp.wait_ge(S.tab_set, 1)
            sp.dma_start(tab[0:NB, :], a["t5_table"]).then_inc(S.tab_in, 16)
            sp.dma_start(OHR[:, :], a["c_ohr"]).then_inc(S.tab_in, 16)
            sp.dma_start(OHF[:, :], a["c_ohf"]).then_inc(S.tab_in, 16)
            sp.dma_start(FLIP[:, :], a["c_flip"]).then_inc(S.tab_in, 16)
            for j in range(2):
                sp.dma_start(ada0[j][:, :, :], a["ada_first"][:, j * KT:(j + 1) * KT]).then_inc(S.ada0_in[j], 16)
            sp.wait_ge(S.bias_sb, 1)
            sp.dma_start(bias_dram, hf[0:H, :, :].rearrange("p a b -> p (a b)")[:, 0:640]).then_inc(S.bias_out, 16)
            sp.wait_ge(S.bias_out, 16)
            sp.dma_start(SKEW[:, :, :], bass.AP(bias_dram.tensor, 0, [[1, P], [640, H], [1, T]])).then_inc(S.skew_in, 16)
            sp.wait_ge(S.ada0_done, 1)
            sp.dma_start(ada0[2][:, :, :], a["ada_first"][:, 2 * KT:3 * KT]).then_inc(S.ada0_in[2], 16)
            sp.wait_ge(S.bm_set, H)
            sp.wait_ge(S.cb_set, 1)
            sp.wait_ge(S.x_turned, KT)

            def unit(u, src, tiles, n, first=False):
                if not first:
                    sp.wait_ge(S.w_lo, u - 1)
                sp.dma_start(wR[n][:, 0:tiles, :], src).then_inc(S.w_in[n], 16)

            def stream(ubase, count, w, l, tiles):
                if ubase == 0:
                    for n in range(2):
                        unit(n, w[l, n], tiles, n, True)
                with sp.Fori(1 if ubase == 0 else 0, count // 2) as i:
                    for n in range(2):
                        unit(ubase + 2 * i + n, w[l, 2 * i + n], tiles, n)

            def stream_ada(ubase, w, aw, l, norm, turns, done):
                def tiles(t, parity, wait=True):
                    if wait:
                        sp.wait_ge(S.ada_done, done + t - 1)
                    for j in range(2):
                        s = 2 * parity + j
                        sp.dma_start(adaw[s][:, :], aw[l, 2 * t + j]).then_inc(S.ada_in[s], 16)

                for n in range(2):
                    unit(ubase + n, w[l, n], KT, n, ubase == 0)
                sp.wait_ge(S.h_lo, KT * (norm + 1))
                tiles(0, 0, False)
                tiles(1, 1, False)

                def turn(t, parity, ada):
                    for n in range(2):
                        unit(ubase + 2 * t + n, w[l, 2 * t + n], KT, n)
                    if ada:
                        tiles(t, parity)
                turn(1, 1, False)
                with sp.Fori(1, turns // 2) as i:
                    for e in range(2):
                        turn(2 * i + e, e, True)
                with sp.Fori(turns, FT) as i:
                    turn(i, 0, False)

            def layer1(l):
                sp.dma_start(par[:, 0:C_END1], a["par1"][l]).then_inc(S.par_in, 16)
                stream_ada(U_UP1, a["ffn1_w13"], a["ada_w1"], l, 0, ADA1, 0)
                stream(U_DN1, 2 * KT, a["ffn1_w2"], l, KH)
                stream(U_IN, N_IN, a["w_in"], l, KT)
                sp.wait_ge(S.x_new, KT)
                sp.dma_start(LM[:, :, :], a["c_lm"]).then_inc(S.mixc_in0, 16)
                sp.dma_start(RS[64:72, :], a["c_rs"]).then_inc(S.mixc_in1, 16)
                sp.dma_start(w2k[:, :, :], a["w2k"][l]).then_inc(S.mixc_in2, 16)
                sp.dma_start(w2v[:, :, :], a["w2v"][l]).then_inc(S.mixc_in3, 16)
                stream(U_CMP, 8, a["cmp_w1"], l, KT)
                stream(U_OUT, KT, a["w_out"], l, KT)
                stream_ada(U_UP2, a["ffn2_w13"], a["ada_w2"], l, 2, ADA2, ADA1)
                stream(U_DN2, 2 * KT, a["ffn2_w2"], l, KH)

            with sp.Fori(0, L) as l:
                layer1(l)
                sp.wait_ge(S.arrived, 4)
                for s in layer_sems:
                    sp.sem_clear(s)
                sp.sem_inc(S.release, 1)

            sp.dma_start(POSI[:, :], bass.AP(a["positions"].tensor, 0, [[0, P], [1, T]])).then_inc(S.pos_in, 16)
            sp.wait_ge(S.trig_a, 2)

            def layer2(l):
                sp.dma_start(par[:, 0:E_END], a["par2"][l]).then_inc(S.par_in, 16)
                sp.dma_start(WS[:, :, :], a["sgu_w"][l]).then_inc(S.ws_in, 16)
                sp.dma_start(BS[:, :, :], bc(a["sgu_b"][l], [P, 4, P])).then_inc(S.bs_in, 16)
                stream(V_IN, N_IN2, a["w_in2"], l, KT)
                stream(V_OUT, KT, a["w_out2"], l, KT)
                stream(V_UP, 2 * FT, a["w_up"], l, KT)
                stream(V_DN, 2 * KT, a["w_down"], l, KH)

            with sp.Fori(0, L) as l:
                layer2(l)
                sp.wait_ge(S.arrived, 4)
                for s in layer_sems:
                    sp.sem_clear(s)
                sp.sem_inc(S.release, 1)

            for t in range(TT):
                sp.wait_ge(S.fin, 8 * (t + 1))
                sp.dma_start(out[t * P:(t + 1) * P, :], xin[:, t, :]).then_inc(S.stored[t % 2], 16)
            for s in S.stored:
                sp.wait_ge(s, 16 * (TT // 2))

        @block.scalar
        def _(act):
            def hi(u, count, tiles, n, first=False):
                act.wait_ge(S.w_in[n], 16 * count)
                if not first:
                    act.wait_ge(S.w_used, u - 1)
                act.activation(wH[n][:, 0:tiles, :], wR[n][:, 0:tiles, :], ACT.Copy).then_inc(S.w_hi, 1)

            def hi_ahead(ubase, i, n, tiles):
                hi(ubase + 2 * i + n + 2, ubase // 2 + i + 2, tiles, n)

            def up(ubase, gbase, next_tiles):
                def turn(i, tiles):
                    hi_ahead(ubase, i, 0, tiles)
                    act.wait_ge(S.w_used, ubase + 2 * i + 1)
                    if gbase or later(i):
                        act.wait_ge(S.g_mul, gbase + i)
                    act.activation(sil[:, :], bank[0][:, :], ACT.Silu).then_inc(S.sil, 1)
                    hi_ahead(ubase, i, 1, tiles)
                turn(0, KT)
                with act.Fori(1, FT - 1) as i:
                    turn(i, KT)
                turn(FT - 1, next_tiles)

            def plain(ubase, pairs, tiles, next_tiles):
                with act.Fori(0, pairs - 1) as i:
                    for n in range(2):
                        hi_ahead(ubase, i, n, tiles)
                if next_tiles:
                    for n in range(2):
                        hi_ahead(ubase, pairs - 1, n, next_tiles)

            def norm(n, sub):
                act.wait_ge(S.ms, n + 1)
                inverse_root(rstd[:, :], bank[6][:, :], 1.0 / D, eps, S.rstd)
                for k in range(KT):
                    act.wait_ge(S.hf, KT * n + k + 1)
                    act.activation(hH[:, k, :], hf[:, k % 2, :], ACT.Identity,
                                   bias=mod[:, 3 * sub * KT + k:3 * sub * KT + k + 1]).then_inc(S.h_hi, 1)

            def last_square(xnew):
                act.wait_ge(S.x_new, xnew)
                act.activation(sqt[:, :], xT[:, KT - 1, :], ACT.Square).then_inc(S.last_sq, 1)

            logs = [0]

            def inverse_root(dst, src, scale, bias, out):
                act.activation(dst, src, ACT.Ln, bias=bias, scale=scale).then_inc(S.ln, 1)
                logs[0] += 1
                act.wait_ge(S.ln, logs[0])
                act.activation(dst, dst, ACT.Exp, scale=-0.5).then_inc(out, 1)

            def scalars():
                act.wait_ge(S.pm, N_IN)
                for j in range(2):
                    act.activation(pm[:, PC_Z + j, :], pm[:, PC_Z + j, :], ACT.Silu)
                for j in range(6):
                    act.wait_ge(S.cv, 4 * (j + 1))
                    act.activation(pm[:, PC_Q + j, :], cv[:, j % 2, :], ACT.Silu).then_inc(S.conv_silu, 1)
                act.activation(pm[0:12, PS, :], pm[0:12, PS, :], ACT.Sigmoid).then_inc(S.g_sig, 1)
                act.activation(pm[R_BE:R_BE + 4, PS, :], pm[R_BE:R_BE + 4, PS, :], ACT.Sigmoid).then_inc(S.g_sig, 1)
                for j in range(2):
                    act.activation(pm[:, PD_O + j, :], pm[:, PD_O + j, :], ACT.Sigmoid)
                r = slice(R_F, R_F + 8)
                act.activation(sma[r, :], par[r, C_SMA:C_SMA + 1], ACT.Exp).then_inc(S.sm_a, 1)
                act.wait_ge(S.sm_v, 2)
                act.activation(smt[r, :], smt[r, :], ACT.Exp, scale=-1.0).then_inc(S.sm_a, 1)
                act.wait_ge(S.sm_a, 2)
                act.activation(smt[r, :], smt[r, :], ACT.Ln, bias=ones[r, 0:1]).then_inc(S.sm_a, 1)
                act.wait_ge(S.sm_v, n_cols(1))
                act.activation(EM[:, :, :], COL[:, :, K_M:K_M + 4], ACT.Exp, scale=-1.0).then_inc(S.sm_a, 1)
                act.activation(EGC[:, :, :], COL[:, :, K_GC:K_GC + 4], ACT.Exp).then_inc(S.sm_a, 1)

            def mix_b():
                act.wait_ge(S.b_ss, 1)
                act.wait_ge(S.b_pool, n_b_y(2))
                inverse_root(pm[:, PB_X, :], bank[5][:, :], 1.0 / (2 * P), eps, S.b_rs)

            def head_norms():
                for n, (tile, scale, b) in enumerate(HEAD_NORMS):
                    act.wait_ge(S.n_ss, n + 1)
                    if n >= 2:
                        act.wait_ge(S.n_out, n - 1)
                    inverse_root(cv[:, n % 2, :], bank[4 + n % 2][:, :], scale, eps64 if b else eps, S.n_rs)

            def head_out(n):
                act.wait_ge(S.o_v, n_o_red(n + 1))
                inverse_root(HR[:, :, :], HR[:, :, :], 1.0 / HD, eps, S.o_rs)

            def mix_d():
                for h in range(H):
                    act.wait_ge(S.d_nmp, h + 1)
                    act.activation(NM[h], bank[h][:, :], ACT.Copy, scale=-1.0).then_inc(S.d_nm, 1)
                for h in range(H):
                    for j in range(TT):
                        u = TT * h + j
                        act.wait_ge(S.d_wd, u + 1)
                        if u >= 2:
                            act.wait_ge(S.d_sv, u - 1)
                        act.activation(WT_[:, u % 2, j * P:(j + 1) * P], WD[:, u % 2, :], ACT.Exp,
                                       bias=COL[:, j, K_A + h:K_A + h + 1]).then_inc(S.d_wt, 1)
                        if j < TT - 1:
                            act.activation(WT_[:, u % 2, (j + 1) * P:], NM[h][:, (j + 1) * P:], ACT.Exp,
                                           bias=COL[:, j, K_A + h:K_A + h + 1]).then_inc(S.d_wt, 1)
                head_out(0)

            def mix_c():
                for p in range(2):
                    act.wait_ge(S.c_vt, p + 1)
                    act.activation(VTM[p][:, :, :], bank[2 + p][:, :].rearrange("p (t c) -> p t c", t=TT),
                                   ACT.Copy).then_inc(S.c_a, 1)
                for p in range(2):
                    act.wait_ge(S.c_gp, p + 1)
                    act.activation(EGP[p][:, :], bank[6 + p][:, :], ACT.Exp).then_inc(S.c_a, 1)
                for h in range(H):
                    act.wait_ge(S.c_v1, n_c_tmp(h + 1))
                    for t in range(TT):
                        act.activation(SEG[h][:, t, :], TMP[h % 2][:, t, :], ACT.Exp,
                                       bias=NGC[:, t, h:h + 1]).then_inc(S.c_a, 1)
                for h in range(H):
                    act.wait_ge(S.c_xt, h + 1)
                    act.activation(XX[h][:, :, :], bank[h][:, :].rearrange("p (t c) -> p t c", t=TT),
                                   ACT.Copy).then_inc(S.c_a, 1)
                with act.Fori(1, 7) as k:
                    for h in range(H):
                        act.wait_ge(S.c_z, 4 * k + h - 3)
                        act.activation(ZZ[h][:, :, :], bank[h][:, :].rearrange("p (t c) -> p t c", t=TT),
                                       ACT.Copy).then_inc(S.c_zc, 1)
                for p in range(2):
                    act.wait_ge(S.c_w, p + 1)
                    act.activation(WW[p][:, :], bank[2 + p][:, :], ACT.Copy).then_inc(S.c_wc, 1)
                for t in range(TT):
                    act.wait_ge(S.c_o, t + 1)
                    act.activation(OD[:, t, :], bank[5 + t % 2][:, 0:H * HD], ACT.Copy).then_inc(S.c_od, 1)
                head_out(1)

            def mix_a():
                for j in range(2):
                    act.wait_ge(S.a_x2, 5 * (j + 1))
                    act.activation(X2H[j][:, :, :], X2[:, :, :], ACT.Copy).then_inc(S.a_x2h, 1)
                for i in range(4):
                    for n in range(2):
                        hi_ahead(U_CMP, i, n, KT)
                act.wait_ge(S.a_v, n_a_hb(1))
                act.activation(HIE[:, :, :], HID[:, :, :], ACT.Exp, scale=-1.0).then_inc(S.a_he, 1)
                act.wait_ge(S.a_kcs, 1)
                inverse_root(KCQ[:, :], bank[6][:, 32:64], 1.0 / HD, eps, S.a_kcr)
                for n in range(2 * TT + 1):
                    i, b = n // 2, n % 2
                    if b == 0 and n < 2 * TT:
                        act.wait_ge(S.a_cv, n_a_c2(i + 1))
                        act.activation(LC[:, :, :], LC[:, :, :], ACT.Exp).then_inc(S.a_ce, 1)
                        act.wait_ge(S.a_ct, i + 1)
                        act.activation(PCT[:, :], cbank(i)[:, P:2 * P], ACT.Copy).then_inc(S.a_ctc, 1)
                    if n:
                        for h in range(H):
                            u = 4 * (n - 1) + h
                            w = ((n - 1) // 2 + 1) * P
                            act.wait_ge(S.a_t, u + 1)
                            if u >= 4:
                                act.wait_ge(S.a_pv, u - 3)
                            act.activation(PTR[h][:, 0:w], bank[2 + h % 2][:, 0:w], ACT.Copy).then_inc(S.a_tc, 1)
                    if n == 2 * TT:
                        break
                    act.wait_ge(S.a_nm, n + 1)
                    w = (i + 1) * P
                    for h in range(H):
                        act.activation(LL[b][:, h, 0:w], LL[b][:, h, 0:w], ACT.Exp,
                                       bias=MX[:, 4 * (b + 1) + h:4 * (b + 1) + h + 1],
                                       accum_out=SM[:, i % 2, 4 * (b + 1) + h:4 * (b + 1) + h + 1]).then_inc(S.a_e, 1)
                act.wait_ge(S.o_v, n_o_red(3))
                inverse_root(HR[:, 0:1, :], HR[:, 0:1, :], 1.0 / (2 * P), eps, S.o_rs)

            def mix_out():
                act.wait_ge(S.o_v, n_o_y(6))
                for k, tile in enumerate(Y_TILES):
                    act.activation(hH[:, k, :], pm[:, tile, :], ACT.Copy).then_inc(S.y_hi, 1)

            act.wait_ge(S.const_in, 32)
            act.activation(cond[:, :], cond[:, :], ACT.Silu).then_inc(S.cond, 1)
            act.wait_ge(S.x_copied, KT)
            act.activation(sqt[:, :], xT[:, KT - 1, :], ACT.Square).then_inc(S.first_sums, 1)

            def layer1(l):
                for n in range(2):
                    hi(n, 1, KT, n, True)
                norm(0, 0)
                up(U_UP1, 0, KH)
                plain(U_DN1, KT, KH, KT)
                last_square(KT)
                norm(1, 1)
                plain(U_IN, N_IN // 2, KT, KT)
                scalars()
                mix_b()
                head_norms()
                mix_d()
                mix_c()
                mix_a()
                mix_out()
                plain(U_OUT, KT // 2, KT, KT)
                last_square(2 * KT)
                norm(2, 2)
                up(U_UP2, FT, KH)
                plain(U_DN2, KT, KH, 0)
                last_square(3 * KT)
                act.wait_ge(S.last_sq, 3)

            with act.Fori(0, L) as l:
                layer1(l)
                end_layer(act, l)

            act.wait_ge(S.trig_v, 22)
            act.activation(SIN[:, :], RED[0][:, :], ACT.Sin).then_inc(S.trig_a, 1)
            act.activation(COS[:, :], RED[1][:, :], ACT.Sin).then_inc(S.trig_a, 1)

            def mix2():
                act.wait_ge(S.lam_ps, 1)
                act.activation(LE[:, :], bank[6][:, 0:2], ACT.Exp).then_inc(S.lam_e, 1)
                act.wait_ge(S.pm, N_IN2)
                for tile in (4, 5, 6, 7, 0, 1, 2, 3):
                    act.activation(pm[:, tile, :], pm[:, tile, :], ACT.Gelu_apprx_tanh).then_inc(S.gelu, 1)
                for h in range(4):
                    act.wait_ge(S.va_t, h + 1)
                    act.activation(VA[h][:, :, :], bank[2 + h % 2][:, :].rearrange("p (t c) -> p t c", t=TT),
                                   ACT.Copy).then_inc(S.va_sb, 1)
                for g in range(4):
                    act.wait_ge(S.n_ss, g + 1)
                    if g >= 2:
                        act.wait_ge(S.n_out, g - 1)
                    inverse_root(cv[:, g % 2, :], bank[4 + g % 2][:, :], 1.0 / P, eps, S.n_rs)
                for g in range(4):
                    act.wait_ge(S.vg_t, g + 1)
                    act.activation(VG[g][:, :, :], bank[6 + g % 2][:, :].rearrange("p (t c) -> p t c", t=TT),
                                   ACT.Copy).then_inc(S.vg_sb, 1)
                for n in range(17):
                    if n < 16:
                        w = (n % TT + 1) * P
                        act.wait_ge(S.s_neg, n + 1)
                        for m in range(2):
                            act.activation(LG[n % 2][:, m, 0:w], LG[n % 2][:, m, 0:w], ACT.Exp, bias=NX2[:, n % 2, m:m + 1],
                                           scale=HD ** -0.5, accum_out=SM2[:, n % 2, m:m + 1]).then_inc(S.s_exp, 1)
                    if n:
                        u = n - 1
                        w = (u % TT + 1) * P
                        act.wait_ge(S.s_t, u + 1)
                        if u >= 2:
                            act.wait_ge(S.s_val, u - 1)
                        act.activation(ADT[u % 2][:, 0:w], bank[4 + u % 2][:, 0:w], ACT.Copy).then_inc(S.s_tsb, 1)
                act.wait_ge(S.o_v, 1)
                inverse_root(HR2[:, :, :], HR2[:, :, :], 1.0 / P, eps, S.o_rs)
                act.wait_ge(S.o_v, 6)
                for k, tile in enumerate(Y2_TILES):
                    act.activation(hH[:, k, :], pm[:, tile, :], ACT.Copy).then_inc(S.y_hi, 1)

            def up2(ubase, next_tiles):
                def last_tap(i, half):
                    tile = i + FT * half
                    act.activation(xn[:, half, :], bank[half][:, :], ACT.Identity, bias=par[:, bass.ds(E_CB + tile, 1)],
                                   scale=par[:, bass.ds(E_CW + 3 * tile + 2, 1)]).then_inc(S.f_tap, 1)

                def turn(i, tiles):
                    hi_ahead(ubase, i, 0, tiles)
                    act.wait_ge(S.w_used, ubase + 2 * i + 1)
                    if later(i):
                        act.wait_ge(S.g_mul, i)
                    last_tap(i, 0)
                    act.wait_ge(S.f_conv, 4 * i + 2)
                    act.activation(sil[:, :], xn[:, 0, :], ACT.Silu).then_inc(S.sil, 1)
                    act.wait_ge(S.w_used, ubase + 2 * i + 2)
                    last_tap(i, 1)
                    hi_ahead(ubase, i, 1, tiles)
                turn(0, KT)
                with act.Fori(1, FT - 1) as i:
                    turn(i, KT)
                turn(FT - 1, next_tiles)

            def layer2(l):
                logs[0] = 0
                for n in range(2):
                    hi(n, 1, KT, n, True)
                norm(0, 0)
                plain(V_IN, N_IN2 // 2, KT, KT)
                mix2()
                plain(V_OUT, KT // 2, KT, KT)
                last_square(KT)
                norm(1, 1)
                up2(V_UP, KH)
                plain(V_DN, KT, KH, 0)
                last_square(2 * KT)
                act.wait_ge(S.last_sq, 2)

            with act.Fori(0, L) as l:
                layer2(l)
                end_layer(act, l + L)
            logs[0] = 0
            act.wait_ge(S.ms, 1)
            inverse_root(rstd[:, :], bank[6][:, :], 1.0 / D, eps, S.rstd)

        @block.vector
        def _(dve):
            dve.memset(tab[:, :], MASKED).then_inc(S.tab_set, 1)
            for k in range(KT):
                dve.wait_ge(S.x_turned, k + 1)
                dve.tensor_copy(xT[:, k, :], bank[k][:, :]).then_inc(S.x_copied, 1)
            def dots(w, dst):
                return dve.tensor_tensor_reduce(w, w, cond[:, :], 1.0, 0.0, ALU.mult, ALU.add, dst)
            dve.wait_ge(S.cond, 1)

            def first(j):
                dve.wait_ge(S.ada0_in[j], 16)
                for t in range(KT):
                    mm = dots(ada0[j][:, t, :], mod[:, NMOD + j * KT + t:NMOD + j * KT + t + 1])
                mm.then_inc(S.ada0_done, 1)
            dve.wait_ge(S.bias_ps, 1)
            brow = hf[0:H, :, :].rearrange("p a b -> p (a b)")
            dve.tensor_copy(brow[:, 0:512], bank[0][0:H, :])
            dve.tensor_copy(brow[:, 512:640], bank[1][0:H, 0:P]).then_inc(S.bias_sb, 1)
            for j in range(2):
                first(j)
            dve.wait_ge(S.cb_ps, 1)
            dve.tensor_copy(cb[:, :, :, :], bank[2][:, :].rearrange("p (i h n) -> p i h n", i=TT, h=H)).then_inc(S.cb_set, 1)
            for h in range(H):
                dve.wait_ge(S.bm_ps, h + 1)
                dve.tensor_copy(bm[:, h, :], bank[4 + h][:, :]).then_inc(S.bm_set, 1)

            first(2)
            dve.wait_ge(S.ada0_done, 3)

            def lo(u, tiles, n):
                dve.wait_ge(S.w_hi, u + 1)
                dve.tensor_tensor(wL[n][:, 0:tiles, :], wR[n][:, 0:tiles, :], wH[n][:, 0:tiles, :].bitcast(F32),
                                  ALU.subtract).then_inc(S.w_lo, 1)

            def up(ubase, gbase, next_tiles, turns, done):
                def columns(i, parity):
                    for j in range(2):
                        s = 2 * parity + j
                        dve.wait_ge(S.ada_in[s], 8 * (done + i - parity) + 16)
                        dots(adaw[s][:, :], acc[:, parity, j:j + 1]).then_inc(S.ada_sum, 1)
                    dve.wait_ge(S.ada_sum, 2 * (done + i) + 2)
                    dve.tensor_copy(mod[:, bass.ds(N_NEXT + 2 * (done + i), 2)], acc[:, parity, :]).then_inc(S.ada_done, 1)

                def turn(i, tiles):
                    lo(ubase + 2 * i + 2, tiles, 0)
                    dve.wait_ge(S.sil, gbase + i + 1)
                    dve.wait_ge(S.w_used, ubase + 2 * i + 2)
                    dve.tensor_tensor(gf[:, :], bank[1][:, :], sil[:, :], ALU.mult).then_inc(S.g_mul, 1)
                    dve.wait_ge(S.g_mul, gbase + i + 1)
                    dve.tensor_copy(gH[:, i, :], gf[:, :]).then_inc(S.g_hi, 1)
                    dve.wait_ge(S.g_hi, gbase + i + 1)
                    dve.tensor_tensor(gL[:, i, :], gf[:, :], gH[:, i, :].bitcast(F32), ALU.subtract).then_inc(S.g_lo, 1)
                    lo(ubase + 2 * i + 3, tiles, 1)

                with dve.Fori(0, turns // 2) as i:
                    for e in range(2):
                        turn(2 * i + e, KT)
                        columns(2 * i + e, e)
                dve.wait_ge(S.ada_done, done + turns)
                with dve.Fori(turns, FT - 1) as i:
                    turn(i, KT)
                turn(FT - 1, next_tiles)

            def add_to_x(m, b, sub):
                dve.scalar_tensor_tensor(xT[:, m, :], bank[b][:, :], gate[:, bass.ds(sub * KT + m, 1)],
                                         xT[:, m, :], ALU.mult, ALU.add).then_inc(S.x_new, 1)

            def down(ubase, sub, next_tiles):
                def tile(m, b, tiles):
                    if tiles:
                        for n in range(2):
                            lo(ubase + 2 * m + 2 + n, tiles, n)
                    dve.wait_ge(S.w_used, ubase + 2 * m + 2)
                    add_to_x(m, b, sub)
                with dve.Fori(0, KT // 2 - 1) as j:
                    for n in range(2):
                        tile(2 * j + n, 2 + n, KH)
                tile(KT - 2, 2, KH)
                tile(KT - 1, 3, next_tiles)

            def project_in(ubase, count, bcol, next_tiles):
                def turn(i, tiles):
                    for n in range(2):
                        lo(ubase + 2 * i + n + 2, tiles, n)
                        dve.wait_ge(S.w_used, ubase + 2 * i + n + 1)
                        if bcol is None:
                            dve.tensor_copy(pm[:, 2 * i + n, :], bank[n][:, :]).then_inc(S.pm, 1)
                        else:
                            dve.tensor_scalar(pm[:, 2 * i + n, :], bank[n][:, :], par[:, bass.ds(bcol + 2 * i + n, 1)], None,
                                              ALU.add).then_inc(S.pm, 1)
                with dve.Fori(0, count // 2 - 1) as i:
                    turn(i, KT)
                turn(count // 2 - 1, next_tiles)

            def project_out(ubase, sub, next_tiles):
                def turn(i, tiles):
                    for n in range(2):
                        if tiles:
                            lo(ubase + 2 * i + n + 2, tiles, n)
                        dve.wait_ge(S.w_used, ubase + 2 * i + n + 1)
                        add_to_x(2 * i + n, n, sub)
                with dve.Fori(0, KT // 2 - 1) as i:
                    turn(i, KT)
                turn(KT // 2 - 1, next_tiles)

            def norm(n, sub):
                def low(k):
                    dve.wait_ge(S.h_hi, KT * n + k + 1)
                    dve.scalar_tensor_tensor(hL[:, k, :], hf[:, k % 2, :], mod[:, 3 * sub * KT + k:3 * sub * KT + k + 1],
                                             hH[:, k, :].bitcast(F32), ALU.add, ALU.subtract).then_inc(S.h_lo, 1)
                dve.wait_ge(S.rstd, n + 1)
                for k in range(KT):
                    if k >= 2:
                        dve.wait_ge(S.h_lo, KT * n + k - 1)
                    dve.scalar_tensor_tensor(hf[:, k % 2, :], xT[:, k, :], modA[:, sub * KT + k:sub * KT + k + 1], rstd[:, :],
                                             ALU.mult, ALU.mult).then_inc(S.hf, 1)
                    if k:
                        low(k - 1)
                low(KT - 1)

            def conv(dst, src, wcol, taps, sem, n):
                dve.tensor_scalar(dst, src, col(wcol + taps - 1), None, ALU.mult).then_inc(sem, 1)
                for d in range(1, taps):
                    dve.wait_ge(sem, n + d)
                    dve.scalar_tensor_tensor(dst[:, d:], src[:, 0:T - d], col(wcol + taps - 1 - d), dst[:, d:],
                                             ALU.mult, ALU.add).then_inc(sem, 1)

            def scalars():
                dve.wait_ge(S.pm, N_IN)
                for j in range(6):
                    if j >= 2:
                        dve.wait_ge(S.conv_silu, j - 1)
                    conv(cv[:, j % 2, :], pm[:, PC_Q + j, :], C_GDW + 4 * j, 4, S.cv, 4 * j)
                r = slice(R_F, R_F + 8)
                z = pm[r, PS, :]
                dve.tensor_scalar(z, z, par[r, C_SMB:C_SMB + 1], cst[r, X_SG:X_SG + 1], ALU.add, ALU.mult).then_inc(S.sm_v, 1)
                dve.wait_ge(S.sm_v, 1)
                dve.scalar_tensor_tensor(smt[r, :], z, -1.0, z, ALU.mult, ALU.max).then_inc(S.sm_v, 1)
                dve.wait_ge(S.sm_a, 3)
                dve.scalar_tensor_tensor(z, z, 0.0, smt[r, :], ALU.max, ALU.add).then_inc(S.sm_v, 1)
                dve.wait_ge(S.sm_v, 3)
                dve.wait_ge(S.sm_a, n_egc(1))
                dve.tensor_scalar(smt[r, :], z, sma[r, :], -1.0, ALU.mult, ALU.mult).then_inc(S.sm_v, 1)
                dve.wait_ge(S.sm_v, 4)
                dve.wait_ge(S.mixc_in1, 16)
                dve.tensor_tensor_scan(z, RS[r, :], smt[r, :], 0.0, ALU.mult, ALU.add).then_inc(S.sm_v, 1)
                dve.wait_ge(S.ar_ps, 1)
                dve.tensor_copy(AR[0:4, :], bank[7][0:4, :]).then_inc(S.sm_v, 1)
                dve.wait_ge(S.sm_v, n_ar(1))
                dve.tensor_tensor_scan(MR[0:4, :], AR[0:4, :], AR[0:4, :], 0.0, ALU.max, ALU.max).then_inc(S.sm_v, 1)
                dve.wait_ge(S.colp, 1)
                dve.tensor_copy(COL[:, :, :], bank[6][:, 0:TT * NCOL].rearrange("p (t c) -> p t c", t=TT)).then_inc(S.sm_v, 1)
                dve.wait_ge(S.sm_v, n_cols(1))
                dve.tensor_scalar(NGC[:, :, :], COL[:, :, K_GC:K_GC + 4], -1.0, None, ALU.mult)
                dve.wait_ge(S.sm_a, n_egc(2))
                dve.tensor_tensor(BG[:, :, :], COL[:, :, K_BE:K_BE + 4], EGC[:, :, :], ALU.mult).then_inc(S.sm_v, 1)

            def mix_b():
                for j in range(2):
                    dve.wait_ge(S.b_pool, n_b_cx(2))
                    conv(pm[:, PB_X + j, :], pm[:, PB_C + j, :], C_SCW + 3 * j, 3, S.b_cv, 3 * j)
                dve.wait_ge(S.b_rs, 1)
                for j in range(2):
                    y = pm[:, PB_B + j, :]
                    dve.scalar_tensor_tensor(y, y, col(C_MIXB + j), pm[:, PB_X, :], ALU.mult, ALU.mult)

            def head_norms():
                for n, (tile, scale, b) in enumerate(HEAD_NORMS):
                    dve.wait_ge(S.n_rs, n + 1)
                    y = pm[:, tile, :]
                    if tile < PS:
                        g = C_QG if tile < PA_KS else C_KG
                        dve.scalar_tensor_tensor(y, y, col(g), cv[:, n % 2, :], ALU.mult, ALU.mult).then_inc(S.n_out, 1)
                    else:
                        dve.tensor_tensor(y, y, cv[:, n % 2, :], ALU.mult).then_inc(S.n_out, 1)

            def head_out(n, gain, tile):
                dve.wait_ge(S.o_sq, n + 1)
                dve.tensor_reduce(HR[:, :, :], OQ[:, :, :].rearrange("p t (h d) -> p t h d", h=H), AX.X,
                                  ALU.add).then_inc(S.o_v, 1)
                dve.wait_ge(S.o_rs, n + 1)
                o = OD[:, :, :].rearrange("p t (h d) -> p (t h) d", h=H)
                dve.tensor_tensor(o, o, bc(HR[:, :, :].rearrange("p t h -> p (t h)").unsqueeze(2), [P, TT * H, HD]),
                                  ALU.mult).then_inc(S.o_v, 1)
                for j in range(2):
                    dve.wait_ge(S.o_t, 2 * n + j + 1)
                    y = pm[:, tile + j, :]
                    dve.scalar_tensor_tensor(y, bank[2 + j][:, :], col(gain), y, ALU.mult, ALU.mult).then_inc(S.o_v, 1)

            def mix_d():
                for p in range(2):
                    dve.wait_ge(S.d_vt, p + 1)
                    dve.tensor_copy(VD[:, :, 2 * p:2 * p + 2, 0:HD],
                                    bank[4 + p][:, :].rearrange("p (t h d) -> p t h d", t=TT, h=2)).then_inc(S.d_vd, 1)

                def numden(h):
                    nd = bank[h % 2][:, 0:TT * (HD + 1)].rearrange("p (t c) -> p t c", t=TT)
                    dve.wait_ge(S.d_nd, h + 1)
                    if h:
                        dve.wait_ge(S.d_post, n_d_od(h))
                    dve.scalar_tensor_tensor(DD[:, :, 0], nd[:, :, HD], -1.0, EM[:, :, h], ALU.mult,
                                             ALU.max).then_inc(S.d_post, 1)
                    dve.wait_ge(S.d_post, n_d_dd(h + 1) - 1)
                    dve.tensor_tensor(DD[:, :, 0], nd[:, :, HD], DD[:, :, 0], ALU.max).then_inc(S.d_post, 1)
                    dve.wait_ge(S.d_post, n_d_dd(h + 1))
                    dve.reciprocal(DD[:, :, 1], DD[:, :, 0]).then_inc(S.d_post, 1)
                    dve.wait_ge(S.d_post, n_d_rc(h + 1))
                    dve.tensor_tensor(OD[:, :, h * HD:(h + 1) * HD], nd[:, :, 0:HD],
                                      bc(DD[:, :, 1:2], [P, TT, HD]), ALU.mult).then_inc(S.d_post, 1)
                for h in range(H):
                    for j in range(TT):
                        u = TT * h + j
                        if u == 0:
                            dve.wait_ge(S.d_nm, H)
                            dve.wait_ge(S.sm_a, n_em(1))
                        if u >= 2:
                            dve.wait_ge(S.d_wt, wt_count(u - 2))
                        dve.tensor_tensor(WD[:, u % 2, :], NM[h][:, j * P:(j + 1) * P], causalT, ALU.add).then_inc(S.d_wd, 1)
                        dve.wait_ge(S.d_s, u + 1)
                        dve.wait_ge(S.d_wt, wt_count(u))
                        if h >= 2 and j == 0:
                            dve.wait_ge(S.d_nd, h - 1)
                        dve.scalar_tensor_tensor(ST_[h % 2][:, j, j * P:], bank[6 + u % 2][:, j * P:], HD ** -0.5,
                                                 WT_[:, u % 2, j * P:], ALU.mult, ALU.mult).then_inc(S.d_sv, 1)
                    if h:
                        numden(h - 1)
                numden(H - 1)
                head_out(0, C_MLS, PD_O)

            def mix_c():
                v4 = lambda b: bank[b][:, :].rearrange("p (t c) -> p t c", t=TT)
                for p in range(2):
                    dve.wait_ge(S.c_kt, p + 1)
                    dve.tensor_copy(KTM[p][:, :, :], v4(p)).then_inc(S.c_v1, 1)
                for p in range(2):
                    dve.wait_ge(S.c_bp, p + 1)
                    dve.wait_ge(S.c_vt, 2)
                    dve.tensor_tensor(KBT[p][:, :], pm[:, PC_K + p, :], bank[4 + p][:, :], ALU.mult).then_inc(S.c_v1, 1)
                dve.wait_ge(S.sm_v, n_bg(1))
                dve.wait_ge(S.c_v1, n_c_ktc(2))
                dve.wait_ge(S.c_a, n_c_vtc(2))
                for p in range(2):
                    for half in range(2):
                        h = 2 * p + half
                        f = slice(half * HD, (half + 1) * HD)
                        dve.tensor_tensor(KB[p][:, :, f], KTM[p][:, :, f], bc(BG[:, :, h:h + 1], [P, TT, HD]),
                                          ALU.mult).then_inc(S.c_v1, 1)
                        dve.tensor_tensor(VB[p][:, :, f], VTM[p][:, :, f],
                                          bc(COL[:, :, K_BE + h:K_BE + h + 1], [P, TT, HD]), ALU.mult).then_inc(S.c_v1, 1)
                for h in range(H):
                    dve.wait_ge(S.c_grp, h + 1)
                    if h >= 2:
                        dve.wait_ge(S.c_a, n_c_seg(TT * (h - 1)))
                    dve.tensor_tensor(TMP[h % 2][:, :, :], v4(h), bc(causalT.unsqueeze(1), [P, TT, P]),
                                      ALU.add).then_inc(S.c_v1, 1)
                for h in range(H):
                    p, f = h // 2, slice(h % 2 * HD, (h % 2 + 1) * HD)
                    dve.wait_ge(S.c_a, n_c_seg(TT * (h + 1)))
                    dve.tensor_tensor(KD[p][:, :, f], KTM[p][:, :, f], bc(SEG[h][:, :, P - 1:P], [P, TT, HD]),
                                      ALU.mult).then_inc(S.c_v2, 1)
                    dve.wait_ge(S.c_kk, h + 1)
                    dve.tensor_tensor(NN[h][:, :, :], v4(4 + h % 2), SEG[h][:, :, :], ALU.mult).then_inc(S.c_v2, 1)
                    dve.wait_ge(S.c_kq, h + 1)
                    dve.tensor_tensor(QK[h][:, :, :], v4(6 + h % 2), SEG[h][:, :, :], ALU.mult).then_inc(S.c_v2, 1)
                dve.wait_ge(S.mixc_in0, 16)
                for h in range(H):
                    dve.wait_ge(S.c_v2, n_c_nn(h + 1))
                    dve.tensor_tensor(PP[h][:, :, :], NN[h][:, :, :], bc(LM[:, 0, :].unsqueeze(1), [P, TT, P]),
                                      ALU.mult).then_inc(S.c_v2, 1)
                    dve.wait_ge(S.c_v2, n_c_n0(h + 1))
                    dve.scalar_tensor_tensor(PP[h][:, :, :], PP[h][:, :, :], -1.0, bc(ident.unsqueeze(1), [P, TT, P]),
                                             ALU.mult, ALU.add).then_inc(S.c_v2, 1)
                with dve.Fori(1, 7) as k:
                    for h in range(H):
                        u = 4 * k + h - 4
                        dve.wait_ge(S.c_xz, u + 1)
                        dve.tensor_tensor(XX[h][:, :, :], XX[h][:, :, :], v4(4 + h % 2), ALU.subtract).then_inc(S.c_xu, 1)
                        dve.wait_ge(S.c_zp, u + 1)
                        dve.tensor_tensor(PP[h][:, :, :], PP[h][:, :, :], v4(6 + h % 2), ALU.subtract).then_inc(S.c_pu, 1)
                for p in range(2):
                    dve.wait_ge(S.c_u, p + 1)
                    dve.tensor_copy(UU[p][:, :, :], v4(p)).then_inc(S.c_uc, 1)
                for t in range(TT):
                    if t:
                        dve.wait_ge(S.c_wp, t)
                        dve.wait_ge(S.c_sp, t)
                        dve.wait_ge(S.c_o, t)
                    else:
                        dve.wait_ge(S.c_uc, 2)
                    for p in range(2):
                        v = VN[:, 2 * p:2 * p + 2, :].rearrange("p h d -> p (h d)")
                        if t:
                            dve.tensor_tensor(v, UU[p][:, t, :], bank[4][:, p * P:(p + 1) * P],
                                              ALU.subtract).then_inc(S.c_vn, 1)
                        else:
                            dve.tensor_copy(v, UU[p][:, t, :]).then_inc(S.c_vn, 1)
                    if t < TT - 1:
                        dve.wait_ge(S.c_sp, t + 1)
                        if t:
                            dve.wait_ge(S.c_st, 4 * t)
                            dve.wait_ge(S.c_o, t + 1)
                        else:
                            dve.wait_ge(S.c_qd, 3)
                        for h in range(H):
                            r = slice(h % 2 * HD, (h % 2 + 1) * HD)
                            new, old = (SSt[r, (t + n) % 2, h // 2, r] for n in (1, 0))
                            if t:
                                dve.scalar_tensor_tensor(new, old, EGP[h // 2][r, (t + 1) * P - 1:(t + 1) * P],
                                                         bank[7][r, h * HD:(h + 1) * HD], ALU.mult, ALU.add).then_inc(S.c_st, 1)
                            else:
                                dve.tensor_copy(new, bank[7][r, h * HD:(h + 1) * HD]).then_inc(S.c_st, 1)
                head_out(1, C_GDN, PC_Z)

            def mix_a():
                dve.wait_ge(S.c_od, TT)
                for j in range(2):
                    src = pm[:, PA_KC + j, :].rearrange("p (n s e) -> p n s e", s=8, e=2)
                    if j:
                        dve.wait_ge(S.a_x2h, 1)
                        dve.wait_ge(S.a_x2l, 1)
                    for e in range(2):
                        r = slice(e * HD, (e + 1) * HD)
                        for g in range(2):
                            dve.tensor_copy(X2[r, 8 * g:8 * g + 8, 0:NCB],
                                            src[r, g:g + NCB, :, e].rearrange("p n s -> p s n")).then_inc(S.a_x2, 1)
                    dve.tensor_copy(X2[:, :, NCB], col(C_POS, 16)).then_inc(S.a_x2, 1)
                    dve.wait_ge(S.a_x2h, j + 1)
                    dve.tensor_tensor(X2L[j][:, :, :], X2[:, :, :], X2H[j][:, :, :].bitcast(F32), ALU.subtract).then_inc(S.a_x2l, 1)
                for i in range(4):
                    for n in range(2):
                        lo(U_CMP + 2 * i + n + 2, KT, n)
                dve.wait_ge(S.w_used, U_CMP + 8)
                dve.tensor_copy(HID[:, :, :], bank[5][:, 0:P].rearrange("p (a n) -> p a n", a=4)).then_inc(S.a_v, 1)
                dve.wait_ge(S.a_v, n_a_hc(1))
                dve.tensor_copy(HIC[:, :], HID[:, :, NCB]).then_inc(S.a_v, 1)
                dve.wait_ge(S.a_v, n_a_hc(2))
                dve.tensor_tensor(HID[:, :, :], HID[:, :, :], bc(HIC[:, :].unsqueeze(2), [P, 4, 32]), ALU.add).then_inc(S.a_v, 1)
                dve.wait_ge(S.a_he, 1)
                dve.tensor_scalar(HIE[:, :, :], HIE[:, :, :], 1.0, None, ALU.add).then_inc(S.a_v, 1)
                dve.wait_ge(S.a_v, n_a_hd(1))
                dve.reciprocal(HIE[:, :, :], HIE[:, :, :]).then_inc(S.a_v, 1)
                dve.wait_ge(S.a_v, n_a_hr(1))
                dve.tensor_tensor(HID[:, :, :], HID[:, :, :], HIE[:, :, :], ALU.mult).then_inc(S.a_v, 1)
                dve.memset(KCB[:, :, :], 0.0)
                dve.memset(VCB[:, :, :], 0.0).then_inc(S.a_v, 1)
                dve.wait_ge(S.a_kc, 1)
                dve.tensor_copy(KCF[:, :], bank[6][:, 0:32]).then_inc(S.a_v, 1)
                dve.wait_ge(S.a_v, n_a_kcf(1))
                dve.tensor_tensor(KCQ[:, :], KCF[:, :], KCF[:, :], ALU.mult).then_inc(S.a_v, 1)
                dve.wait_ge(S.a_kc, 2)
                dve.wait_ge(S.a_v, n_a_vcz(1))
                for h in range(H):
                    dve.tensor_copy(VCB[32 * h:32 * h + 32, h, :], bank[7][32 * h:32 * h + 32, 0:HD]).then_inc(S.a_v, 1)
                dve.wait_ge(S.a_kcr, 1)
                for e in range(2):
                    r = slice(e * HD, (e + 1) * HD)
                    mm = dve.scalar_tensor_tensor(KCB[r, e, :], KCF[r, :], par[r, C_KG:C_KG + 1], KCQ[r, :], ALU.mult, ALU.mult)
                mm.then_inc(S.a_v, 1)
                dve.wait_ge(S.a_vt, 1)
                dve.tensor_copy(V6[:, :, :], bank[4][:, :].rearrange("p (t c) -> p t c", t=TT)).then_inc(S.a_v, 1)

                def compressed(i):
                    dve.wait_ge(S.a_cl, i + 1)
                    if i:
                        dve.wait_ge(S.a_ct, i)
                    dve.tensor_tensor(LC[:, :, :], cbank(i)[:, 0:P].rearrange("p (h n) -> p h n", h=H), cb[:, i, :, :],
                                      ALU.add).then_inc(S.a_cv, 1)
                    dve.wait_ge(S.a_cv, n_a_c1(i + 1))
                    if i:
                        dve.wait_ge(S.a_cv, n_a_cnm(i))
                    dve.tensor_reduce(MX[:, 0:4], LC[:, :, :], AX.X, ALU.max).then_inc(S.a_cv, 1)
                    dve.wait_ge(S.a_cv, n_a_cmx(i + 1))
                    dve.tensor_scalar(MX[:, 0:4], MX[:, 0:4], MASKED / 10, -1.0, ALU.max, ALU.mult).then_inc(S.a_cv, 1)
                    dve.wait_ge(S.a_cv, n_a_cnm(i + 1))
                    dve.tensor_tensor(LC[:, :, :], LC[:, :, :], bc(MX[:, 0:4].unsqueeze(2), [P, H, 32]), ALU.add).then_inc(S.a_cv, 1)
                    dve.wait_ge(S.a_ce, i + 1)
                    if i >= 2:
                        dve.wait_ge(S.a_yv, n_a_rc(i - 1))
                    dve.tensor_reduce(SM[:, i % 2, 0:4], LC[:, :, :], AX.X, ALU.add).then_inc(S.a_cv, 1)
                    dve.wait_ge(S.a_cv, n_a_cs(i + 1))
                    dve.tensor_scalar(SM[:, i % 2, 0:4], SM[:, i % 2, 0:4], 1e-30, None, ALU.max).then_inc(S.a_cv, 1)

                def combine(i):
                    dve.wait_ge(S.a_e, 8 * (i + 1))
                    dve.wait_ge(S.a_cv, n_a_cg(i + 1))
                    if i:
                        dve.wait_ge(S.a_yv, n_a_y(5 * i))
                    dve.reciprocal(CF[:, :], SM[:, i % 2, :]).then_inc(S.a_yv, 1)
                    dve.wait_ge(S.a_yv, n_a_rc(i + 1))
                    c = CF[:, :].rearrange("p (b h) -> p b h", b=3)
                    dve.tensor_tensor(c, c, COL[:, i, 0:12].rearrange("p (h b) -> p b h", b=3), ALU.mult).then_inc(S.a_yv, 1)
                    dve.wait_ge(S.a_yv, n_a_cf(i + 1))
                    dve.wait_ge(S.a_co, i + 1)
                    dve.wait_ge(S.a_pv, 8 * (i + 1))
                    y = YA[:, i, :].rearrange("p (h d) -> p h d", h=H)
                    v = lambda ap: ap.rearrange("p (h d) -> p h d", h=H)
                    cc = lambda b: bc(CF[:, 4 * b:4 * b + 4].unsqueeze(2), [P, H, HD])
                    dve.tensor_tensor(y, v(cbank(i)[:, 256:512]), cc(0), ALU.mult).then_inc(S.a_yv, 1)
                    for b in range(2):
                        dve.tensor_tensor(YT[:, :, :], v(bank[4][:, 256 * b:256 * (b + 1)]), cc(b + 1), ALU.mult).then_inc(S.a_yv, 1)
                        dve.wait_ge(S.a_yv, n_a_y(5 * i + 2 + 2 * b))
                        dve.tensor_tensor(y, y, YT[:, :, :], ALU.add).then_inc(S.a_yv, 1)
                        dve.wait_ge(S.a_yv, n_a_y(5 * i + 3 + 2 * b))

                for n in range(2 * TT + 1):
                    i, b = n // 2, n % 2
                    if n < 2 * TT:
                        if b == 0:
                            compressed(i)
                        w = (i + 1) * P
                        if n >= 2:
                            dve.wait_ge(S.a_t, 4 * (n - 1))
                            dve.wait_ge(S.a_e, 4 * (n - 1))
                        for h in range(H):
                            dve.wait_ge(S.a_s, 4 * n + h + 1)
                            dve.tensor_tensor_reduce(LL[b][:, h, 0:w], bank[h % 2][:, 0:w], bm[:, h, 384 - P * i:384 - P * i + w],
                                                     1.0, MASKED, ALU.add, ALU.max,
                                                     MX[:, 4 * (b + 1) + h:4 * (b + 1) + h + 1]).then_inc(S.a_l, 1)
                        dve.wait_ge(S.a_l, 4 * (n + 1))
                        m = MX[:, 4 * (b + 1):4 * (b + 2)]
                        dve.tensor_scalar(m, m, -1.0, None, ALU.mult).then_inc(S.a_nm, 1)
                    if b == 0 and n:
                        combine(i - 1)
                dve.wait_ge(S.o_sq, 3)
                dve.tensor_reduce(HR[:, 0, :], YQ[:, :, :], AX.X, ALU.add).then_inc(S.o_v, 1)
                dve.wait_ge(S.o_rs, 3)
                dve.tensor_tensor(YA[:, :, :], YA[:, :, :], bc(HR[:, 0, :].unsqueeze(2), [P, TT, H * HD]),
                                  ALU.mult).then_inc(S.o_v, 1)
                for j in range(2):
                    dve.wait_ge(S.o_t, 4 + j + 1)
                    dve.tensor_scalar(pm[:, j, :], bank[2 + j][:, :], col(C_MIXA + j), None, ALU.mult).then_inc(S.o_v, 1)

            def mix_out():
                for k, tile in enumerate(Y_TILES):
                    dve.wait_ge(S.y_hi, k + 1)
                    dve.tensor_tensor(hL[:, k, :], pm[:, tile, :], hH[:, k, :].bitcast(F32), ALU.subtract).then_inc(S.y_lo, 1)

            def scaled(s, done):
                dve.scalar_tensor_tensor(modA[:, s * KT:(s + 1) * KT], mod[:, (3 * s + 1) * KT:(3 * s + 2) * KT], 1.0,
                                         col(C_NORM + s * KT, KT), ALU.add, ALU.mult).then_inc(S.mod_set, 1)
                if s < 2:
                    set_gate(s)
                dve.wait_ge(S.mod_set, done + (2 if s < 2 else 1))

            def set_gate(s):
                dve.tensor_scalar(gate[:, s * KT:(s + 1) * KT], mod[:, (3 * s + 2) * KT:(3 * s + 3) * KT],
                                  1.0 if s == 1 else 0.5, None, ALU.mult).then_inc(S.mod_set, 1)

            def layer1(l):
                dve.wait_ge(S.par_in, 16)
                dve.tensor_tensor(mod[:, 0:N_NEXT], mod[:, NMOD:NMOD + N_NEXT], col(C_ADAB, N_NEXT), ALU.add).then_inc(S.mod_set, 1)
                dve.wait_ge(S.mod_set, 1)
                scaled(0, 1)
                for n in range(2):
                    lo(n, KT, n)
                norm(0, 0)
                up(U_UP1, 0, KH, ADA1, 0)
                c = slice(N_NEXT, 8 * KT)
                dve.tensor_tensor(mod[:, c], mod[:, c], par[:, C_ADAB + N_NEXT:C_ADAB + 8 * KT], ALU.add).then_inc(S.mod_set, 1)
                down(U_DN1, 0, KT)
                scaled(1, 4)
                norm(1, 1)
                project_in(U_IN, N_IN, C_BIN, KT)
                scalars()
                mix_b()
                head_norms()
                mix_d()
                mix_c()
                mix_a()
                mix_out()
                project_out(U_OUT, 1, KT)
                scaled(2, 6)
                norm(2, 2)
                up(U_UP2, FT, KH, ADA2, ADA1)
                c = slice(8 * KT, NMOD)
                dve.tensor_tensor(mod[:, c], mod[:, c], par[:, C_ADAB + 8 * KT:C_ADAB + NMOD], ALU.add).then_inc(S.mod_set, 1)
                dve.wait_ge(S.mod_set, 8)
                set_gate(2)
                dve.wait_ge(S.mod_set, 9)
                down(U_DN2, 2, 0)

            with dve.Fori(0, L) as l:
                layer1(l)
                end_layer(dve, l)

            chain = [0]

            def step(mm):
                mm.then_inc(S.trig_v, 1)
                chain[0] += 1
                dve.wait_ge(S.trig_v, chain[0])
            dve.wait_ge(S.pos_in, 16)
            step(dve.memset(CMASK[:, 0:384], 0.0))
            step(dve.tensor_copy(CMASK[:, 384:512], causal))
            step(dve.tensor_copy(TRN[:, :], POSI[:, :]))
            step(dve.tensor_scalar(ANG[:, :], TRN[:, :], cst[:, X_IF:X_IF + 1], None, ALU.mult))
            for q in range(2):
                step(dve.tensor_scalar(TRN[:, :], ANG[:, :], 0.5 / np.pi, 0.25 * q, ALU.mult, ALU.add))
                step(dve.tensor_scalar(TRN[:, :], TRN[:, :], ROUND, None, ALU.add))
                step(dve.tensor_scalar(TRN[:, :], TRN[:, :], ROUND, None, ALU.subtract))
                r = RED[q][:, :]
                step(dve.scalar_tensor_tensor(r, TRN[:, :], -TURN[0], ANG[:, :], ALU.mult, ALU.add))
                step(dve.scalar_tensor_tensor(r, TRN[:, :], -TURN[1], r, ALU.mult, ALU.add))
                step(dve.scalar_tensor_tensor(r, TRN[:, :], -TURN[2], r, ALU.mult, ALU.add))
                step(dve.tensor_scalar(r, r, 0.5 * np.pi * q, None, ALU.add))
                step(dve.tensor_scalar(r, r, 3.1415925, -3.1415925, ALU.min, ALU.max))
                if q == 0:
                    step(dve.memset(mod[:, :], 0.0))
                    step(dve.memset(gate[:, :], 1.0))
            assert chain[0] == 22

            def mix2():
                r = slice(0, HD)
                dve.tensor_tensor(LQ[r, :], par[r, E_LAM:E_LAM + 2], par[r, E_LAM + 2:E_LAM + 4], ALU.mult).then_inc(S.lam_v, 1)
                dve.wait_ge(S.lam_e, 1)
                dve.scalar_tensor_tensor(NL[:, :], LE[:, 0:1], -1.0, LE[:, 1:2], ALU.mult, ALU.add).then_inc(S.lam_v, 1)
                dve.wait_ge(S.lam_v, 2)
                dve.tensor_tensor(NL[:, :], NL[:, :], par[:, E_LIN:E_LIN + 1], ALU.subtract).then_inc(S.lam_v, 1)
                for c in range(8):
                    dve.wait_ge(S.rot_ps, c + 1)
                    dve.tensor_tensor(RTM[c % 2][:, :], bank[c % 2][:, :], SIN[:, :], ALU.mult).then_inc(S.rot_sin, 1)
                    dve.wait_ge(S.rot_sin, c + 1)
                    dve.wait_ge(S.rot_cos, c + 1)
                    y = pm[:, QQ + c, :]
                    dve.tensor_tensor(y, y, RTM[c % 2][:, :], ALU.add).then_inc(S.rot_x, 1)
                for g in range(4):
                    dve.wait_ge(S.n_rs, g + 1)
                    y = pm[:, QV + g, :]
                    dve.scalar_tensor_tensor(y, y, col(E_SGU + g), cv[:, g % 2, :], ALU.mult, ALU.mult).then_inc(S.n_out, 1)
                dve.wait_ge(S.gelu, 8)
                dve.wait_ge(S.bs_in, 16)
                for g in range(4):
                    dve.wait_ge(S.mixed, g + 1)
                    dve.tensor_tensor(SGT[g % 2][:, :, :], bank[2 + g % 2][:, :].rearrange("p (t c) -> p t c", t=TT),
                                      bc(BS[:, g:g + 1, :], [P, TT, P]), ALU.add).then_inc(S.mix_b, 1)
                    dve.wait_ge(S.mix_b, g + 1)
                    y = pm[:, QU + g, :].rearrange("p (t c) -> p t c", t=TT)
                    dve.tensor_tensor(y, y, SGT[g % 2][:, :, :], ALU.mult).then_inc(S.mix_y, 1)
                for n in range(18):
                    if n < 16:
                        i, b = n % TT, n % 2
                        w = (i + 1) * P
                        for m in range(2):
                            dve.wait_ge(S.s_ps, 2 * n + m + 1)
                            if n >= 2:
                                dve.wait_ge(S.s_diff, n - 1)
                            dve.tensor_tensor_reduce(LG[b][:, m, 0:w], bank[2 * b + m][:, 0:w],
                                                     CMASK[:, 384 - P * i:384 - P * i + w], 1.0, MASKED, ALU.add, ALU.max,
                                                     MX2[:, b, m:m + 1]).then_inc(S.s_max, 1)
                        dve.wait_ge(S.s_max, 2 * n + 2)
                        dve.tensor_scalar(NX2[:, b, :], MX2[:, b, :], -HD ** -0.5, None, ALU.mult).then_inc(S.s_neg, 1)
                    if 1 <= n < 17:
                        u = n - 1
                        i, b = u % TT, u % 2
                        w = (i + 1) * P
                        dve.wait_ge(S.s_exp, 2 * u + 2)
                        if u >= 2:
                            dve.wait_ge(S.s_y, u - 1)
                        dve.reciprocal(RC2[:, b, :], SM2[:, b, :]).then_inc(S.s_small, 1)
                        dve.wait_ge(S.s_small, 2 * u + 1)
                        dve.scalar_tensor_tensor(RT2[:, b, :], RC2[:, b, 1:2], NL[:, 0:1], SM2[:, b, 0:1], ALU.mult,
                                                 ALU.mult).then_inc(S.s_small, 1)
                        dve.wait_ge(S.s_small, 2 * u + 2)
                        if u >= 2:
                            dve.wait_ge(S.s_t, u - 1)
                        dve.scalar_tensor_tensor(AD[b][:, 0:w], LG[b][:, 1, 0:w], RT2[:, b, :], LG[b][:, 0, 0:w], ALU.mult,
                                                 ALU.add).then_inc(S.s_diff, 1)
                    if n >= 2:
                        v = n - 2
                        h, i = v // TT, v % TT
                        dve.wait_ge(S.s_val, v + 1)
                        dve.tensor_scalar(YD[:, i, h * P:(h + 1) * P], bank[6 + v % 2][:, 0:P], RC2[:, v % 2, 0:1], None,
                                          ALU.mult).then_inc(S.s_y, 1)
                dve.wait_ge(S.o_sq, 1)
                dve.tensor_reduce(HR2[:, :, :], YDQ[:, :, :].rearrange("p t (h d) -> p t h d", h=4), AX.X,
                                  ALU.add).then_inc(S.o_v, 1)
                dve.wait_ge(S.o_rs, 1)
                o = YD[:, :, :].rearrange("p t (h d) -> p (t h) d", h=4)
                dve.tensor_tensor(o, o, bc(HR2[:, :, :].rearrange("p t h -> p (t h)").unsqueeze(2), [P, TT * 4, P]),
                                  ALU.mult).then_inc(S.o_v, 1)
                for h in range(4):
                    dve.wait_ge(S.o_t, h + 1)
                    dve.tensor_scalar(pm[:, QY + h, :], bank[h][:, :], col(E_SUB), col(E_LIN + 1), ALU.mult,
                                      ALU.mult).then_inc(S.o_v, 1)
                for k, tile in enumerate(Y2_TILES):
                    dve.wait_ge(S.y_hi, k + 1)
                    dve.tensor_tensor(hL[:, k, :], pm[:, tile, :], hH[:, k, :].bitcast(F32), ALU.subtract).then_inc(S.y_lo, 1)

            def up2(ubase, next_tiles):
                def taps(i, half):
                    dve.wait_ge(S.f_tap, 2 * i + half + 1)
                    for d in (1, 2):
                        y = xn[:, half, d:]
                        dve.scalar_tensor_tensor(y, bank[half][:, 0:T - d], par[:, bass.ds(E_CW + 3 * (i + FT * half) + 2 - d, 1)],
                                                 y, ALU.mult, ALU.add).then_inc(S.f_conv, 1)
                        dve.wait_ge(S.f_conv, 4 * i + 2 * half + d)

                def turn(i, tiles):
                    lo(ubase + 2 * i + 2, tiles, 0)
                    taps(i, 0)
                    taps(i, 1)
                    dve.wait_ge(S.sil, i + 1)
                    dve.tensor_tensor(gf[:, :], xn[:, 1, :], sil[:, :], ALU.mult).then_inc(S.g_mul, 1)
                    lo(ubase + 2 * i + 3, tiles, 1)
                    dve.wait_ge(S.g_mul, i + 1)
                    dve.tensor_copy(gH[:, i, :], gf[:, :]).then_inc(S.g_hi, 1)
                    dve.wait_ge(S.g_hi, i + 1)
                    dve.tensor_tensor(gL[:, i, :], gf[:, :], gH[:, i, :].bitcast(F32), ALU.subtract).then_inc(S.g_lo, 1)
                with dve.Fori(0, FT - 1) as i:
                    turn(i, KT)
                turn(FT - 1, next_tiles)

            def layer2(l):
                dve.wait_ge(S.par_in, 16)
                dve.tensor_copy(modA[:, 0:2 * KT], par[:, E_NORM:E_NORM + 2 * KT]).then_inc(S.mod_set, 1)
                for n in range(2):
                    lo(n, KT, n)
                dve.wait_ge(S.mod_set, 1)
                norm(0, 0)
                project_in(V_IN, N_IN2, None, KT)
                mix2()
                project_out(V_OUT, 0, KT)
                norm(1, 1)
                up2(V_UP, KH)
                down(V_DN, 1, 0)

            with dve.Fori(0, L) as l:
                layer2(l)
                end_layer(dve, l + L)

            dve.wait_ge(S.rstd, 1)
            for k in range(KT):
                dve.scalar_tensor_tensor(xT[:, k, :], xT[:, k, :], col(E_FIN + k), rstd[:, :], ALU.mult,
                                         ALU.mult).then_inc(S.x_new, 1)
            for t in range(TT):
                for k in range(KT):
                    n = t * KT + k
                    dve.wait_ge(S.x_turned, KT + n + 1)
                    dve.tensor_copy(xin[:, t, k * P:(k + 1) * P], bank[n % 4][:, 0:P]).then_inc(S.fin, 1)

        @block.gpsimd
        def _(pool):
            pool.wait_ge(S.x_copied, KT)

            def square_sum(xbase, n, chain=S.pool, done=S.sumsq):
                c = (2 * KT - 3) * n
                for m in range(KT - 1):
                    if xbase is not None:
                        pool.wait_ge(S.x_new, xbase + m + 1)
                    dst = rstd if m else sumsq
                    pool.tensor_tensor(dst[:, :], xT[:, m, :], xT[:, m, :], ALU.mult).then_inc(chain, 1)
                    if m:
                        pool.wait_ge(chain, c + 2 * m)
                        pool.tensor_tensor(sumsq[:, :], sumsq[:, :], rstd[:, :], ALU.add).then_inc(chain, 1)
                        pool.wait_ge(chain, c + 2 * m + 1)
                pool.sem_inc(done, 1)

            def mix_b():
                pool.wait_ge(S.pm, N_IN)
                for j in range(2):
                    y = pm[:, PB_C + j, :]
                    pool.tensor_tensor(y, y, pm[:, PB_X + j, :], ALU.mult).then_inc(S.b_pool, 1)
                for j in range(2):
                    pool.wait_ge(S.b_cv, 3 * (j + 1))
                    y = pm[:, PB_B + j, :]
                    pool.tensor_tensor(y, y, pm[:, PB_X + j, :], ALU.mult).then_inc(S.b_pool, 1)
                    pool.wait_ge(S.b_pool, n_b_y(j + 1))
                    pool.tensor_tensor(pm[:, PB_C + j, :], y, y, ALU.mult).then_inc(S.b_pool, 1)

            def head_norms():
                pool.wait_ge(S.conv_silu, 6)
                pool.wait_ge(S.h_hi, 2 * KT)
                for n, (tile, scale, b) in enumerate(HEAD_NORMS):
                    if n >= 2:
                        pool.wait_ge(S.n_ss, n - 1)
                    pool.tensor_tensor(nsq[:, n % 2, :], pm[:, tile, :], pm[:, tile, :], ALU.mult).then_inc(S.n_sq, 1)

            def head_out(n, ready, count):
                pool.wait_ge(ready, count)
                pool.tensor_tensor(OQ[:, :, :], OD[:, :, :], OD[:, :, :], ALU.mult).then_inc(S.o_sq, 1)

            def mix_c():
                pool.wait_ge(S.c_a, n_c_egp(2))
                pool.wait_ge(S.c_kq, H)
                for p in range(2):
                    y = pm[:, PC_Q + p, :]
                    pool.tensor_tensor(y, y, EGP[p][:, :], ALU.mult).then_inc(S.c_qd, 1)
                pool.memset(SSt[:, :, :, :], 0.0).then_inc(S.c_qd, 1)

                def level(k):
                    for h in range(H):
                        u = 4 * k + h - 4
                        if u >= 2:
                            pool.wait_ge(S.c_z, u - 1)
                        pool.tensor_tensor(NK[h % 2][:, :, :], NN[h][:, :, :],
                                           bc(LM[:, k:k + 1, :], [P, TT, P]), ALU.mult).then_inc(S.c_nk, 1)
                pool.wait_ge(S.c_a, n_c_seg(TT * H))
                pool.wait_ge(S.c_v2, n_c_nn(H))
                for k in range(1, 7):
                    level(k)

            def mix_a():
                pool.wait_ge(S.a_yv, n_a_y(5 * TT))
                pool.tensor_tensor(YQ[:, :, :], YA[:, :, :], YA[:, :, :], ALU.mult).then_inc(S.o_sq, 1)

            def layer1(l):
                square_sum(0, 0)
                mix_b()
                head_norms()
                pool.memset(VD[:, :, :, HD:HD + 1], 1.0).then_inc(S.d_one, 1)
                head_out(0, S.d_post, n_d_od(H))
                mix_c()
                head_out(1, S.c_od, TT)
                mix_a()
                square_sum(KT, 1)
                square_sum(2 * KT, 2)

            square_sum(None, 0, S.first_sq, S.first_sums)

            with pool.Fori(0, L) as l:
                layer1(l)
                end_layer(pool, l)

            pool.wait_ge(S.trig_a, 2)

            def layer2(l):
                pool.wait_ge(S.ws_in, 16)
                pool.tensor_tensor(WS[:, :, :], WS[:, :, :], bc(tri.unsqueeze(1), [P, 4, P]), ALU.mult).then_inc(S.ws_set, 1)
                for c in range(8):
                    pool.wait_ge(S.rot_ps, c + 1)
                    y = pm[:, QQ + c, :]
                    pool.tensor_tensor(y, y, COS[:, :], ALU.mult).then_inc(S.rot_cos, 1)
                for g in range(4):
                    pool.wait_ge(S.gelu, g + 1)
                    if g >= 2:
                        pool.wait_ge(S.n_ss, g - 1)
                    elif g == 0:
                        pool.wait_ge(S.h_lo, KT)
                    pool.tensor_tensor(nsq[:, g % 2, :], pm[:, QV + g, :], pm[:, QV + g, :], ALU.mult).then_inc(S.n_sq, 1)
                pool.wait_ge(S.s_y, 16)
                pool.tensor_tensor(YDQ[:, :, :], YD[:, :, :], YD[:, :, :], ALU.mult).then_inc(S.o_sq, 1)
                square_sum(0, 0)
                square_sum(KT, 1)

            with pool.Fori(0, L) as l:
                layer2(l)
                end_layer(pool, l + L)

        @block.tensor
        def _(pe):
            pe.wait_ge(S.const_in, 32)
            pe.wait_ge(S.x_in, 16)
            for k in range(KT):
                for t in range(TT):
                    mm = pe.transpose(bank[k][:, t * P:(t + 1) * P], xin[:, t, k * P:(k + 1) * P], ident)
                mm.then_inc(S.x_turned, 1)
            pe.wait_ge(S.tab_in, 64)
            pe.wait_ge(S.x_copied, KT)
            pe.matmul(bank[0][0:H, :], tab[:, :], OHR[:, 0:512], start=True, stop=True)
            pe.matmul(bank[1][0:H, 0:P], tab[:, :], OHR[:, 512:640], start=True, stop=True).then_inc(S.bias_ps, 1)
            for i in range(TT):
                for n in range(32):
                    d0 = P * i - 16 * n - 31 + 527
                    mm = pe.matmul(bank[2][:, i * P:(i + 1) * P].rearrange("p (h n) -> p h n", h=H)[:, :, n],
                                   OHF[:, d0:d0 + P], tab[:, :], start=True, stop=True)
            mm.then_inc(S.cb_ps, 1)
            pe.wait_ge(S.skew_in, 16)
            for h in range(H):
                pe.matmul(bank[4 + h][:, :], FLIP[:, :], SKEW[:, h, :], start=True, stop=True).then_inc(S.bm_ps, 1)
            pe.wait_ge(S.bm_set, H)
            pe.wait_ge(S.cb_set, 1)
            pe.wait_ge(S.first_sums, 2)

            def products(o, n, tiles, rH, rL, k0, start, stop, ready=None):
                for k in range(tiles):
                    if ready:
                        pe.wait_ge(ready[0], ready[1] + k + 1)
                    r = k0 + k
                    pe.matmul(o, wH[n][:, k, :], rH[:, r, :], start=start and k == 0, stop=False)
                    pe.matmul(o, wL[n][:, k, :], rH[:, r, :], start=False, stop=False)
                    mm = pe.matmul(o, wH[n][:, k, :], rL[:, r, :], start=False, stop=stop and k == tiles - 1)
                mm.then_inc(S.w_used, 1)

            def up(ubase, gbase, ready):
                def turn(i, ready=None):
                    pe.wait_ge(S.w_lo, ubase + 2 * i + 1)
                    if gbase or later(i):
                        pe.wait_ge(S.sil, gbase + i)
                    products(bank[0][:, :], 0, KT, hH, hL, 0, True, True, ready)
                    pe.wait_ge(S.w_lo, ubase + 2 * i + 2)
                    if gbase or later(i):
                        pe.wait_ge(S.g_mul, gbase + i)
                    products(bank[1][:, :], 1, KT, hH, hL, 0, True, True)
                turn(0, ready)
                with pe.Fori(1, FT) as i:
                    turn(i)

            def down(ubase, xbase, gdone):
                pe.wait_ge(S.g_lo, gdone)

                def tile(m, b):
                    for n in range(2):
                        pe.wait_ge(S.w_lo, ubase + 2 * m + n + 1)
                        if n == 0 and (xbase or not isinstance(m, int)):
                            pe.wait_ge(S.x_new, xbase + m - 1)
                        products(bank[b][:, :], n, KH, gH, gL, n * KH, n == 0, n == 1)
                for n in range(2):
                    tile(n, 2 + n)
                with pe.Fori(1, KT // 2) as j:
                    for n in range(2):
                        tile(2 * j + n, 2 + n)

            def project(ubase, pairs, out_sem, obase, ready):
                def turn(i, ready=None):
                    for n in range(2):
                        pe.wait_ge(S.w_lo, ubase + 2 * i + n + 1)
                        if later(i):
                            pe.wait_ge(out_sem, obase + 2 * i + n - 1)
                        products(bank[n][:, :], n, KT, hH, hL, 0, True, True, None if n else ready)
                turn(0, ready)
                with pe.Fori(1, pairs) as i:
                    turn(i)

            def mean_square(n):
                if n:
                    pe.wait_ge(S.sumsq, n)
                pe.matmul(bank[6][:, :], ones, sumsq[:, :], start=True, stop=False)
                if n:
                    pe.wait_ge(S.last_sq, n)
                pe.matmul(bank[6][:, :], ones, sqt[:, :], start=False, stop=True).then_inc(S.ms, 1)

            def scalars():
                pe.wait_ge(S.g_sig, 2)
                pe.wait_ge(S.sm_v, 5)
                pe.matmul(bank[7][0:4, :], cst[:, X_SA:X_SA + 4], pm[:, PS, :], start=True, stop=True).then_inc(S.ar_ps, 1)
                pe.wait_ge(S.sm_v, n_mr(1))
                for t in range(TT):
                    c = bank[6][:, t * NCOL:(t + 1) * NCOL]
                    pe.matmul(c, pm[:, PS, t * P:(t + 1) * P], cst[:, X_CS:X_CS + NCOL], start=True, stop=False)
                    mm = pe.matmul(c, MR[0:4, t * P:(t + 1) * P], cst[0:4, X_MS:X_MS + NCOL], start=False, stop=True)
                mm.then_inc(S.colp, 1)

            def mix_b():
                for j in range(2):
                    pe.wait_ge(S.b_pool, n_b_sq(j + 1))
                    mm = pe.matmul(bank[5][:, :], ones, pm[:, PB_C + j, :], start=j == 0, stop=j == 1)
                mm.then_inc(S.b_ss, 1)
                pe.wait_ge(S.b_rs, 1)

            def head_norms():
                for n in range(len(HEAD_NORMS)):
                    pe.wait_ge(S.n_sq, n + 1)
                    if n >= 2:
                        pe.wait_ge(S.n_rs, n - 1)
                    pe.matmul(bank[4 + n % 2][:, :], heads, nsq[:, n % 2, :], start=True, stop=True).then_inc(S.n_ss, 1)

            def turn_tiles(b, src, sem):
                for t in range(TT):
                    mm = pe.transpose(bank[b][:, t * P:(t + 1) * P], src(t), ident)
                mm.then_inc(sem, 1)

            def head_out(n, src=None):
                pe.wait_ge(S.o_v, n_o_nrm(n + 1))
                for j in range(2):
                    turn_tiles(2 + j, lambda t: (src or OD)[:, t, j * P:(j + 1) * P], S.o_t)

            def half(h):
                return slice(h % 2 * HD, (h % 2 + 1) * HD)

            def mix_d():
                pe.wait_ge(S.n_rs, len(HEAD_NORMS))
                for h in range(H):
                    pe.matmul(bank[h][:, :], bc(ident[0:4, h:h + 1], [4, P]), MR[0:4, :], start=True, stop=True).then_inc(S.d_nmp, 1)
                for p in range(2):
                    turn_tiles(4 + p, lambda t: pm[:, PD_V + p, t * P:(t + 1) * P], S.d_vt)

                def numden(h):
                    pe.wait_ge(S.d_sv, TT * (h + 1))
                    if h == 0:
                        pe.wait_ge(S.d_nm, 2)
                        pe.wait_ge(S.d_vd, 2)
                        pe.wait_ge(S.d_one, 1)
                    if h >= 2:
                        pe.wait_ge(S.d_post, n_d_od(h - 1))
                    for i in range(TT):
                        for j in range(i + 1):
                            mm = pe.matmul(bank[h % 2][:, i * (HD + 1):(i + 1) * (HD + 1)], ST_[h % 2][:, j, i * P:(i + 1) * P],
                                           VD[:, j, h, :], start=j == 0, stop=j == i)
                    mm.then_inc(S.d_nd, 1)
                for h in range(H):
                    for j in range(TT):
                        u = TT * h + j
                        if u >= 2:
                            pe.wait_ge(S.d_sv, u - 1)
                        pe.matmul(bank[6 + u % 2][:, j * P:], pm[half(h), PD_K + h // 2, j * P:(j + 1) * P],
                                  pm[half(h), PD_Q + h // 2, j * P:], start=True, stop=True).then_inc(S.d_s, 1)
                    if h:
                        numden(h - 1)
                numden(H - 1)
                head_out(0)

            def mix_c():
                pe.wait_ge(S.o_v, n_o_y(2))
                pe.wait_ge(S.n_out, len(HEAD_NORMS))
                for p in range(2):
                    turn_tiles(p, lambda t: pm[:, PC_K + p, t * P:(t + 1) * P], S.c_kt)
                for p in range(2):
                    turn_tiles(2 + p, lambda t: pm[:, PC_V + p, t * P:(t + 1) * P], S.c_vt)
                for p in range(2):
                    r = R_BE + 2 * p
                    for e in range(2):
                        mm = pe.matmul(bank[4 + p][half(e), :], bc(ident[:, r + e:r + e + 1], [P, HD]), pm[:, PS, :],
                                       start=True, stop=True)
                    mm.then_inc(S.c_bp, 1)
                for p in range(2):
                    r = R_AL + 2 * p
                    for e in range(2):
                        mm = pe.matmul(bank[6 + p][half(e), :], bc(ident[:, r + e:r + e + 1], [P, HD]), pm[:, PS, :],
                                       start=True, stop=True)
                    mm.then_inc(S.c_gp, 1)
                pe.wait_ge(S.c_v1, n_c_ktc(2))
                pe.wait_ge(S.c_a, n_c_vtc(2))
                for h in range(H):
                    pe.matmul(bank[h][:, :], bc(ident[:, R_AL + h:R_AL + h + 1], [P, P]), pm[:, PS, :], start=True,
                              stop=True).then_inc(S.c_grp, 1)
                pe.wait_ge(S.c_v1, n_c_kbt(2))
                pe.wait_ge(S.c_a, n_c_egp(2))
                for h in range(H):
                    if h >= 2:
                        pe.wait_ge(S.c_v2, n_c_nn(h - 1))
                        pe.wait_ge(S.c_v2, n_c_qk(h - 1))
                    for b, r, sem in ((4, KBT[h // 2][half(h), :], S.c_kk), (6, pm[half(h), PC_Q + h // 2, :], S.c_kq)):
                        for t in range(TT):
                            mm = pe.matmul(bank[b + h % 2][:, t * P:(t + 1) * P],
                                           pm[half(h), PC_K + h // 2, t * P:(t + 1) * P], r[:, t * P:(t + 1) * P],
                                           start=True, stop=True)
                        mm.then_inc(sem, 1)
                for h in range(H):
                    pe.wait_ge(S.c_v2, n_c_p0(h + 1))
                    pe.wait_ge(S.c_v1, n_c_tmp(H))
                    turn_tiles(h, lambda t: PP[h][:, t, :], S.c_xt)
                pe.wait_ge(S.c_a, n_c_x0(H))
                pe.wait_ge(S.c_v2, n_c_nn(H))
                pe.wait_ge(S.c_v2, n_c_qk(H))
                def square(k, h):
                    u = 4 * k + h - 4
                    pe.wait_ge(S.c_zc, u + 1)
                    if later(k - 1) or h >= 2:
                        pe.wait_ge(S.c_pu, u - 1)
                    for t in range(TT):
                        mm = pe.matmul(bank[4 + h % 2][:, t * P:(t + 1) * P], PP[h][:, t, :], ZZ[h][:, t, :], start=True, stop=True)
                    mm.then_inc(S.c_xz, 1)
                    for t in range(TT):
                        mm = pe.matmul(bank[6 + h % 2][:, t * P:(t + 1) * P], ZZ[h][:, t, :], PP[h][:, t, :], start=True, stop=True)
                    mm.then_inc(S.c_zp, 1)

                def level(k):
                    for h in range(H):
                        pe.wait_ge(S.c_nk, 4 * k + h - 3)
                        if later(k - 1):
                            pe.wait_ge(S.c_xu, 4 * k + h - 7)
                        for t in range(TT):
                            mm = pe.matmul(bank[h][:, t * P:(t + 1) * P], NK[h % 2][:, t, :], XX[h][:, t, :], start=True, stop=True)
                        mm.then_inc(S.c_z, 1)
                        if h:
                            square(k, h - 1)
                    square(k, H - 1)
                level(1)
                with pe.Fori(2, 7) as k:
                    level(k)

            def mix_c_scan():
                pe.wait_ge(S.c_pu, 24)
                pe.wait_ge(S.c_v1, n_c_kb(H))
                pe.wait_ge(S.c_v1, n_c_vb(H))
                for p in range(2):
                    for t in range(TT):
                        for h in (2 * p, 2 * p + 1):
                            mm = pe.matmul(bank[p][:, t * P + h % 2 * HD:t * P + (h % 2 + 1) * HD], PP[h][:, t, :],
                                           VB[p][:, t, half(h)], start=True, stop=True)
                    mm.then_inc(S.c_u, 1)
                for p in range(2):
                    for t in range(TT):
                        for h in (2 * p, 2 * p + 1):
                            mm = pe.matmul(bank[2 + p][half(h), t * P:(t + 1) * P], KB[p][:, t, half(h)], PP[h][:, t, :],
                                           start=True, stop=True)
                    mm.then_inc(S.c_w, 1)
                pe.wait_ge(S.c_wc, 2)
                pe.wait_ge(S.c_qd, 2)
                pe.wait_ge(S.c_v2, n_c_kd(H))
                for t in range(TT):
                    c = slice(t * P, (t + 1) * P)
                    if t:
                        pe.wait_ge(S.c_st, 4 * t)
                        for p in range(2):
                            mm = pe.matmul(bank[4][:, p * P:(p + 1) * P], WW[p][:, c], SSt[:, t % 2, p, :], start=True, stop=True)
                        mm.then_inc(S.c_wp, 1)
                    if t >= 2:
                        pe.wait_ge(S.c_od, t - 1)
                    pe.wait_ge(S.c_vn, 2 * (t + 1))
                    for h in range(H):
                        o = bank[5 + t % 2][:, h * HD:(h + 1) * HD]
                        if t and h % 2 == 0:
                            pe.matmul(bank[5 + t % 2][:, h * HD:(h + 2) * HD], pm[:, PC_Q + h // 2, c], SSt[:, t % 2, h // 2, :],
                                      start=True, stop=False)
                        mm = pe.matmul(o, QK[h][:, t, :], VN[:, h, :], start=t == 0, stop=t == 0 or h % 2 == 1)
                    mm.then_inc(S.c_o, 1)
                    if t < TT - 1:
                        for h in range(H):
                            mm = pe.matmul(bank[7][half(h), h * HD:(h + 1) * HD], KD[h // 2][:, t, half(h)],
                                           VN[:, h, :], start=True, stop=True)
                        mm.then_inc(S.c_sp, 1)
                head_out(1)

            def mix_a():
                pe.wait_ge(S.a_x2l, 2)
                pe.wait_ge(S.c_od, TT)
                turn_tiles(4, lambda t: pm[:, PA_VSW, t * P:(t + 1) * P], S.a_vt)
                for c in range(8):
                    kv, hd, g = c // 4, c // 2 % 2, c % 2
                    pe.wait_ge(S.w_lo, U_CMP + c + 1)
                    products(bank[5][:, (2 * kv + hd) * 32:(2 * kv + hd + 1) * 32], c % 2, KT, X2H[kv], X2L[kv], g * KT,
                             g == 0, g == 1)
                pe.wait_ge(S.a_v, n_a_hid(1))
                pe.wait_ge(S.mixc_in2, 16)
                pe.wait_ge(S.mixc_in3, 16)
                for hd in range(2):
                    mm = pe.matmul(bank[6][:, 0:32], w2k[:, hd, :], HID[:, hd, :], start=hd == 0, stop=hd == 1)
                mm.then_inc(S.a_kc, 1)
                for h in range(H):
                    for hd in range(2):
                        mm = pe.matmul(bank[7][32 * h:32 * h + 32, 0:HD], HID[:, 2 + hd, :], w2v[:, hd, :],
                                       start=hd == 0, stop=hd == 1)
                mm.then_inc(S.a_kc, 1)
                pe.wait_ge(S.a_v, n_a_kcq(1))
                pe.matmul(bank[6][:, 32:64], heads, KCQ[:, :], start=True, stop=True).then_inc(S.a_kcs, 1)
                pe.wait_ge(S.a_v, n_a_kcn(1))
                pe.wait_ge(S.a_v, n_a_vcb(H))
                pe.wait_ge(S.a_v, n_a_v6(1))
                q = lambda h, i: pm[half(h), PA_Q + h // 2, i * P:(i + 1) * P]
                for n in range(2 * TT + 1):
                    i, b = n // 2, n % 2
                    if n < 2 * TT:
                        if b == 0:
                            if i >= 2:
                                pe.wait_ge(S.a_yv, n_a_y(5 * i - 9))
                            for p in range(2):
                                mm = pe.matmul(cbank(i)[:, p * HD:(p + 1) * HD], pm[:, PA_Q + p, i * P:(i + 1) * P],
                                               KCB[:, :, :].rearrange("p e n -> p (e n)"), start=True, stop=True)
                            mm.then_inc(S.a_cl, 1)
                        for h in range(H):
                            u = 4 * n + h
                            if u >= 2:
                                pe.wait_ge(S.a_l, u - 1)
                            pe.matmul(bank[h % 2][:, 0:(i + 1) * P], q(h, i), pm[half(h), PA_KS + b, 0:(i + 1) * P],
                                      start=True, stop=True).then_inc(S.a_s, 1)
                        if b == 0:
                            pe.wait_ge(S.a_ce, i + 1)
                            pe.transpose(cbank(i)[:, P:2 * P], LC[:, :, :].rearrange("p h n -> p (h n)"), ident).then_inc(S.a_ct, 1)
                            pe.wait_ge(S.a_ctc, i + 1)
                            pe.matmul(cbank(i)[:, 256:512], PCT[:, :], VCB[:, :, :].rearrange("p h d -> p (h d)"), start=True,
                                      stop=True).then_inc(S.a_co, 1)
                    if n:
                        i, b = (n - 1) // 2, (n - 1) % 2

                        def values(h):
                            pe.wait_ge(S.a_tc, 4 * (n - 1) + h + 1)
                            if i and b == 0 and h == 0:
                                pe.wait_ge(S.a_yv, n_a_y(5 * i))
                            o = bank[4][:, 256 * b + HD * h:256 * b + HD * (h + 1)]
                            for t in range(i + 1):
                                mm = pe.matmul(o, PTR[h][:, t * P:(t + 1) * P], V6[:, t, b * HD:(b + 1) * HD],
                                               start=t == 0, stop=t == i)
                            mm.then_inc(S.a_pv, 1)
                        for h in range(H):
                            u = 4 * (n - 1) + h
                            pe.wait_ge(S.a_e, u + 1)
                            if u >= 2:
                                pe.wait_ge(S.a_tc, u - 1)
                            for t in range(i + 1):
                                mm = pe.transpose(bank[2 + h % 2][:, t * P:(t + 1) * P], LL[b][:, h, t * P:(t + 1) * P], ident)
                            mm.then_inc(S.a_t, 1)
                            if h:
                                values(h - 1)
                        values(H - 1)
                head_out(2, YA)

            def layer1(l):
                mean_square(0)
                up(U_UP1, 0, (S.h_lo, 0))
                down(U_DN1, 0, FT)
                mean_square(1)
                project(U_IN, N_IN // 2, S.pm, 0, (S.h_lo, KT))
                scalars()
                mix_b()
                head_norms()
                mix_d()
                mix_c()
                mix_c_scan()
                mix_a()
                project(U_OUT, KT // 2, S.x_new, KT, (S.y_lo, 0))
                mean_square(2)
                up(U_UP2, FT, (S.h_lo, 2 * KT))
                down(U_DN2, 2 * KT, 2 * FT)
                pe.wait_ge(S.x_new, 3 * KT)

            with pe.Fori(0, L) as l:
                layer1(l)
                end_layer(pe, l)

            pe.wait_ge(S.trig_a, 2)

            def mix2():
                pe.wait_ge(S.lam_v, 1)
                pe.matmul(bank[6][:, 0:2], ones[0:HD, :], LQ[0:HD, :], start=True, stop=True).then_inc(S.lam_ps, 1)
                pe.wait_ge(S.pm, N_IN2)
                for c in range(8):
                    if c >= 2:
                        pe.wait_ge(S.rot_sin, c - 1)
                    pe.matmul(bank[c % 2][:, :], rot, pm[:, QQ + c, :], start=True, stop=True).then_inc(S.rot_ps, 1)
                for h in range(4):
                    if h >= 2:
                        pe.wait_ge(S.va_sb, h - 1)
                    turn_tiles(2 + h % 2, lambda t: pm[:, QA + h, t * P:(t + 1) * P], S.va_t)
                for g in range(4):
                    pe.wait_ge(S.n_sq, g + 1)
                    if g >= 2:
                        pe.wait_ge(S.n_rs, g - 1)
                    pe.matmul(bank[4 + g % 2][:, :], ones, nsq[:, g % 2, :], start=True, stop=True).then_inc(S.n_ss, 1)
                for g in range(4):
                    pe.wait_ge(S.n_out, g + 1)
                    if g >= 2:
                        pe.wait_ge(S.vg_sb, g - 1)
                    turn_tiles(6 + g % 2, lambda t: pm[:, QV + g, t * P:(t + 1) * P], S.vg_t)
                pe.wait_ge(S.va_sb, 4)
                pe.wait_ge(S.ws_set, 1)
                for g in range(4):
                    pe.wait_ge(S.vg_sb, g + 1)
                    if g >= 2:
                        pe.wait_ge(S.mix_b, g - 1)
                    for t in range(TT):
                        mm = pe.matmul(bank[2 + g % 2][:, t * P:(t + 1) * P], VG[g][:, t, :], WS[:, g, :], start=True, stop=True)
                    mm.then_inc(S.mixed, 1)
                pe.wait_ge(S.rot_x, 8)
                pe.wait_ge(S.mix_b, 4)
                for n in range(18):
                    if n < 16:
                        h, i, b = n // TT, n % TT, n % 2
                        if n >= 2:
                            pe.wait_ge(S.s_max, 2 * n - 2)
                        for m in range(2):
                            pe.matmul(bank[2 * b + m][:, 0:(i + 1) * P], pm[half(m), QQ + h, i * P:(i + 1) * P],
                                      pm[half(m), QK_ + h, 0:(i + 1) * P], start=True, stop=True).then_inc(S.s_ps, 1)
                    if 1 <= n < 17:
                        u = n - 1
                        pe.wait_ge(S.s_diff, u + 1)
                        if u >= 2:
                            pe.wait_ge(S.s_tsb, u - 1)
                        for t in range(u % TT + 1):
                            mm = pe.transpose(bank[4 + u % 2][:, t * P:(t + 1) * P], AD[u % 2][:, t * P:(t + 1) * P], ident)
                        mm.then_inc(S.s_t, 1)
                    if n >= 2:
                        v = n - 2
                        h, i = v // TT, v % TT
                        pe.wait_ge(S.s_tsb, v + 1)
                        if v >= 2:
                            pe.wait_ge(S.s_y, v - 1)
                        for t in range(i + 1):
                            mm = pe.matmul(bank[6 + v % 2][:, 0:P], ADT[v % 2][:, t * P:(t + 1) * P], VA[h][:, t, :],
                                           start=t == 0, stop=t == i)
                        mm.then_inc(S.s_val, 1)
                pe.wait_ge(S.o_v, 2)
                for h in range(4):
                    turn_tiles(h, lambda t: YD[:, t, h * P:(h + 1) * P], S.o_t)

            def up2(ubase, ready):
                def turn(i, ready=None):
                    for half in range(2):
                        pe.wait_ge(S.w_lo, ubase + 2 * i + half + 1)
                        if later(i):
                            pe.wait_ge(S.f_conv, 4 * i - 2 + 2 * half)
                        products(bank[half][:, :], half, KT, hH, hL, 0, True, True, None if half else ready)
                turn(0, ready)
                with pe.Fori(1, FT) as i:
                    turn(i)

            def layer2(l):
                mean_square(0)
                project(V_IN, N_IN2 // 2, S.pm, 0, (S.h_lo, 0))
                mix2()
                project(V_OUT, KT // 2, S.x_new, 0, (S.y_lo, 0))
                mean_square(1)
                up2(V_UP, (S.h_lo, KT))
                down(V_DN, KT, FT)
                pe.wait_ge(S.x_new, 2 * KT)

            with pe.Fori(0, L) as l:
                layer2(l)
                end_layer(pe, l + L)
            mean_square(0)
            pe.wait_ge(S.x_new, KT)

            for t in range(TT):
                for k in range(KT):
                    n = t * KT + k
                    if n >= 4:
                        pe.wait_ge(S.fin, n - 3)
                    pe.transpose(bank[n % 4][:, 0:P], xT[:, k, t * P:(t + 1) * P], ident).then_inc(S.x_turned, 1)


def col_tiles(w, tiles):
    l, k, n = w.shape
    w = w.reshape(l, k // P // tiles, tiles, P, n // P, P)
    return w.transpose(0, 4, 1, 3, 2, 5).reshape(l, (n // P) * (k // P // tiles), P, tiles, P)


def bucket(dist):
    n = np.maximum(dist, 0)
    f = np.maximum(n, 1).astype(np.float32)
    large = 16 + (np.log(f / np.float32(16)) / np.float32(np.log(8.0)) * np.float32(16)).astype(np.int32)
    return np.where(dist < 0, NB, np.where(n < 16, n, np.minimum(large, NB - 1)))


def constants():
    c = np.zeros((P, X_END), np.float32)
    i = np.arange(P)
    c[:, X_ID:X_ID + P] = np.eye(P)
    c[:, X_ONE:X_ONE + P] = 1
    c[:, X_BO:X_BO + P] = i[:, None] // HD == i[None, :] // HD
    c[:, X_CM:X_CM + P] = np.where(i[None, :] <= i[:, None], 0, MASKED)
    c[:, X_CMT:X_CMT + P] = np.where(i[None, :] >= i[:, None], 0, MASKED)
    for h in range(H):
        for k in (X_SA, X_CS + K_A):
            c[R_I + h, k + h] = 1
            c[R_F + h, k + h] = -1
        c[R_F + h, X_CS + K_M + h] = 1
        c[R_BE + h, X_CS + K_BE + h] = 1
        c[R_AL + h, X_CS + K_GC + h] = 1
        c[R_F + h, X_SG] = -1
        c[R_AL + h, X_SG] = 1
    c[0:12, X_CS:X_CS + 12] = np.eye(12)
    c[:, X_TRI:X_TRI + P] = i[None, :] >= i[:, None]
    d = i % HD
    for src in np.flatnonzero(d < ROT):
        if d[src] < ROT // 2:
            c[src, X_ROT + src + ROT // 2] = 1
        else:
            c[src, X_ROT + src - ROT // 2] = -1
    theta = np.float32(500000.0) ** (-np.arange(0, ROT, 2, dtype=np.float32) / np.float32(ROT))
    c[:, X_IF] = np.where(d < ROT, theta[d % (ROT // 2)], 0)
    c[0:H, X_MS + K_M:X_MS + K_M + H] = np.eye(H)
    c[:, X_EPS] = EPS
    c[:, X_E64] = HD * EPS
    one_hot = lambda d: (np.arange(NB + 1)[:, None] == bucket(d)[None, :]).astype(np.float32)
    level = np.zeros((P, 7, P), np.float32)
    for k in range(7):
        same = i[:, None] >> (k + 1) == i[None, :] >> (k + 1)
        level[:, k] = same & ((i[:, None] >> k) % 2 == 0) & ((i[None, :] >> k) % 2 == 1)
    sums = np.ones((8, T), np.float32)
    sums[4:, ::P] = 0
    return {"cst": c, "c_lm": level, "c_rs": sums, "c_ohr": one_hot(511 - np.arange(640)),
            "c_ohf": one_hot(np.arange(1056) - 527), "c_flip": np.eye(P, dtype=np.float32)[::-1]}


SPLIT = (("a_q", 256), ("a_k_cmp", 64), ("a_v_cmp", 64), ("a_k_slc", 64), ("a_v_slc", 64), ("a_k_win", 64), ("a_v_win", 64),
         ("a_gate", 12), ("b_b", 256), ("b_c", 256), ("b_x", 256), ("c_q", 256), ("c_k", 256), ("c_v", 256), ("c_beta", 4),
         ("c_alpha", 4), ("c_z", 256), ("d_q", 256), ("d_k", 256), ("d_v", 256), ("d_i", 4), ("d_f", 4), ("d_o", 256))


def project_columns():
    at, o = {}, 0
    for n, w in SPLIT:
        at[n] = np.arange(o, o + w)
        o += w
    pad = o
    s = np.full(P, pad)
    s[0:12] = at["a_gate"]
    for r, n in ((R_I, "d_i"), (R_F, "d_f"), (R_AL, "c_alpha"), (R_BE, "c_beta")):
        s[r:r + 4] = at[n]
    order = [at["a_q"], at["a_k_slc"], at["a_k_slc"], at["a_k_win"], at["a_k_win"], at["a_k_cmp"], at["a_k_cmp"],
             at["a_v_cmp"], at["a_v_cmp"], at["a_v_slc"], at["a_v_win"], s, at["b_b"], at["b_c"], at["b_x"],
             at["c_q"], at["c_k"], at["c_v"], at["c_z"], at["d_q"], at["d_k"], at["d_v"], at["d_o"]]
    return np.concatenate(order)


def layout(inputs):
    f = lambda n: np.asarray(inputs[n])
    r = constants()
    z = lambda *s: np.zeros(s, np.float32)
    r["x"] = f("x")[0]
    r["c"] = f("c")
    r["t5_table"] = f("t5_table")
    pairs = lambda w: col_tiles(w, KT).reshape(L, 2, FT, P, KT, P).transpose(0, 2, 1, 3, 4, 5).reshape(L, 2 * FT, P, KT, P)
    order = project_columns()
    w_in = np.concatenate([f("w_in"), z(L, D, 1)], axis=2)[:, :, order]
    b_in = np.concatenate([f("b_in"), z(L, 1)], axis=1)[:, order]
    r["w_in"] = col_tiles(w_in, KT)
    r["w_out"] = col_tiles(f("w_out"), KT)
    for n in ("ffn1", "ffn2"):
        r[n + "_w13"] = pairs(f(n + "_w13"))
        r[n + "_w2"] = col_tiles(f(n + "_w2"), KH)
    r["cmp_w1"] = np.concatenate([col_tiles(f(n), KT) for n in ("cmp_k_w1", "cmp_v_w1")], axis=1)
    half = lambda w: w.reshape(L, 2, P, HD).transpose(0, 2, 1, 3)
    r["w2k"] = np.concatenate([half(f("cmp_k_w2"))] * 2, axis=3)
    r["w2v"] = half(f("cmp_v_w2"))
    ada = f("ada_w").transpose(0, 2, 1).reshape(L, NMOD, P, D)
    first = ada[:, 0:N_NEXT]
    r["ada_first"] = first[0].transpose(1, 0, 2)
    r["ada_w1"] = ada[:, N_NEXT:8 * KT]
    r["ada_w2"] = np.concatenate([ada[:, 8 * KT:], np.concatenate([first[1:], first[-1:]])], axis=1)
    cols = lambda v: v.reshape(L, -1, P).transpose(0, 2, 1)
    taps = lambda v: v.reshape(L, v.shape[1], -1, P).transpose(0, 3, 2, 1).reshape(L, P, -1)
    twice = lambda v: np.concatenate([v, v], axis=1)[:, :, None]
    small = z(L, P, 2)
    small[:, R_F:R_F + 4, 0] = f("mlstm_f_bias")
    small[:, R_AL:R_AL + 4, 0] = f("gdn_dt_bias")
    small[:, R_AL:R_AL + 4, 1] = f("gdn_A_log")
    mix = f("mix_norm_g")
    r["par1"] = np.concatenate([cols(f("norm_g")), cols(f("ada_b")), cols(b_in), twice(f("q_norm_g")), twice(f("k_norm_g")),
                                taps(f("sc_conv_w")), taps(f("gdn_conv_w")), cols(mix[:, 1]), cols(mix[:, 0]),
                                twice(f("gdn_norm_g")), twice(f("mlstm_norm_g")), small, cols(f("cmp_pos"))], axis=2)
    r["positions"] = f("positions_2")
    r["w_in2"] = col_tiles(f("w_in_2"), KT)
    r["w_out2"] = col_tiles(f("w_out_2"), KT)
    r["w_up"] = pairs(f("w_up_2"))
    r["w_down"] = col_tiles(f("w_down_2"), KH)
    r["sgu_w"] = f("sgu_w_spatial_2").transpose(0, 3, 1, 2)
    r["sgu_b"] = f("sgu_b_spatial_2")[:, None]
    lam = np.stack([f(f"lambda_{n}_2") for n in ("q1", "q2", "k1", "k2")], axis=2)
    init = 0.8 - 0.6 * np.exp(-0.3 * np.arange(L))
    r["par2"] = np.concatenate([
        cols(f("attn_norm_2")), cols(f("ffn_norm_2")), cols(np.stack([f("final_norm_2")] * L)), cols(f("sgu_v_norm_2")),
        cols(f("subln_gain_2")), np.concatenate([lam, z(L, P - HD, 4)], axis=1),
        np.broadcast_to(np.stack([init, 1 - init], axis=1)[:, None].astype(np.float32), (L, P, 2)),
        taps(f("conv_w_2")), cols(f("conv_b_2"))], axis=2)
    return {k: np.ascontiguousarray(v) for k, v in r.items()}


def kernel(**inputs):
    import concourse.bacc as bacc
    from concourse.bass_utils import run_bass_kernel_spmd

    nc = bacc.Bacc("TRN2", target_bir_lowering=False, num_devices=1)
    arrays = layout(inputs)
    args = {n: nc.dram_tensor(f"in_{n}", v.shape, mybir.dt.from_np(v.dtype), kind="ExternalInput").ap()
            for n, v in arrays.items()}
    out = nc.dram_tensor("out", (T, D), F32, kind="ExternalOutput").ap()
    build(nc, args, out)
    r = run_bass_kernel_spmd(nc, [{f"in_{n}": v for n, v in arrays.items()}], core_ids=[0])
    return r.results[0]["out"].reshape(1, T, D)
```

```python
from contextlib import ExitStack

import numpy as np

import concourse.bass as bass
from concourse import mybir

F32 = mybir.dt.float32
F32R = mybir.dt.float32r
I32 = mybir.dt.int32
ALU = mybir.AluOpType
ACT = mybir.ActivationFunctionType
AX = mybir.AxisListType

P = 128
T = 512
TT = T // P
D = 1024
KT = D // P
L = 2
FF = 2816
FT = FF // P
KH = FT // 2
EPS = 1e-6
NMOD = 9 * KT
N_NEXT = 3 * KT
ADA1 = 5 * KT // 2
ADA2 = 4 * KT // 2

U_UP1 = 0
U_DN1 = U_UP1 + 2 * FT
U_IN = U_DN1 + 2 * KT
N_IN = 30
N_IN0 = 20
U_MIXED = U_IN + N_IN0
U_LAST = U_MIXED + 16
U_OUT = U_LAST + 2
U_UP2 = U_OUT + KT
U_DN2 = U_UP2 + 2 * FT

C_NORM = 0
C_ADAB = C_NORM + 3 * KT
C_BIN = C_ADAB + NMOD
C_QG = C_BIN + N_IN
C_KG = C_QG + 1
C_SCW = C_KG + 1
C_GDW = C_SCW + 6
C_MIXB = C_GDW + 24
C_MIXA = C_MIXB + 2
C_GDN = C_MIXA + 2
C_MLS = C_GDN + 1
C_SMB = C_MLS + 1
C_SMA = C_SMB + 1
C_POS = C_SMA + 1
C_END1 = C_POS + 16

V_IN = 0
N_IN2 = 20
V_OUT = V_IN + N_IN2
V_UP = V_OUT + KT
V_DN = V_UP + 2 * FT

N_IN0_2 = 8

E_NORM = 0
E_FIN = E_NORM + 2 * KT
E_SGU = E_FIN + KT
E_SUB = E_SGU + 4
E_LAM = E_SUB + 1
E_LIN = E_LAM + 4
E_CW = E_LIN + 2
E_CB = E_CW + 6 * FT
E_END = E_CB + 2 * FT
QU, QV, QQ, QK_, QA, QY = 0, 4, 8, 12, 16, 20
Y2_TILES = (QU, QU + 1, QU + 2, QU + 3, QY, QY + 1, QY + 2, QY + 3)
ROT = 16
TURN = (6.28125, 0.0019350051879882812, float(2 * np.pi - 6.28125 - 0.0019350051879882812))
ROUND = 1.5 * 2 ** 23

PA_Q, PA_KS, PA_KW, PA_KC, PA_VC, PA_VSW, PS, PB_B, PB_C, PB_X = 0, 2, 3, 4, 5, 6, 7, 8, 10, 12
PC_Q, PC_K, PC_V, PC_Z, PD_Q, PD_K, PD_V, PD_O = 14, 16, 18, 20, 22, 24, 26, 28
R_I, R_F, R_AL, R_BE = 32, 64, 68, 96
K_BE, K_GC, K_A, K_M, NCOL = 12, 16, 20, 24, 28

H = 4
HD = 64
NB = 32
NCB = 31
MASKED = -1e30

Y_TILES = (PA_Q, PA_Q + 1, PB_B, PB_B + 1, PC_Z, PC_Z + 1, PD_O, PD_O + 1)
HEAD_NORMS = ((PA_Q, 1.0, 1), (PA_Q + 1, 1.0, 1), (PA_KS, 1.0 / HD, 0), (PA_KW, 1.0 / HD, 0),
              (PC_Q, 64.0, 1), (PC_Q + 1, 64.0, 1), (PC_K, 1.0, 0), (PC_K + 1, 1.0, 0))

X_ID, X_ONE, X_BO, X_CM, X_CMT, X_SA, X_CS, X_SG, X_EPS = 0, P, 2 * P, 3 * P, 4 * P, 5 * P, 5 * P + 4, 5 * P + 32, 5 * P + 33
X_E64 = X_EPS + 1
X_MS = X_E64 + 1
X_TRI = X_MS + NCOL
X_ROT = X_TRI + P
X_IF = X_ROT + P
X_END = X_IF + 1


def later(i):
    return not isinstance(i, int) or i > 0


def wt_count(u):
    return 2 * (u + 1) - (u + 1) // TT


def n_ar(k):
    return 5 + k


def n_mr(k):
    return 6 + k


def n_cols(k):
    return 7 + k


def n_bg(k):
    return 8 + k


def n_em(k):
    return 3 + k


def n_egc(k):
    return 4 * k - 3


def n_b_cx(k):
    return k


def n_b_y(k):
    return 2 * k + 1


def n_b_sq(k):
    return 2 * k + 2


def n_d_dd(k):
    return 4 * k - 2


def n_d_rc(k):
    return 4 * k - 1


def n_d_od(k):
    return 4 * k


def n_o_red(k):
    return 4 * k - 3


def n_o_nrm(k):
    return 4 * k - 2


def n_o_y(k):
    return 4 * ((k - 1) // 2) + (k - 1) % 2 + 3


def n_c_ktc(k):
    return k


def n_c_kbt(k):
    return 2 + k


def n_c_kb(k):
    return 3 + 2 * k


def n_c_vb(k):
    return 4 + 2 * k


def n_c_tmp(k):
    return 12 + k


def n_c_kd(k):
    return 3 * k - 2


def n_c_nn(k):
    return 3 * k - 1


def n_c_qk(k):
    return 3 * k


def n_c_n0(k):
    return 11 + 2 * k


def n_c_p0(k):
    return 12 + 2 * k


def n_c_vtc(k):
    return k


def n_c_egp(k):
    return 2 + k


def n_c_seg(k):
    return 4 + k


def n_c_x0(k):
    return 20 + k


def n_a_hc(k):
    return k


def n_a_hb(k):
    return 2 + k


def n_a_hd(k):
    return 3 + k


def n_a_hr(k):
    return 4 + k


def n_a_hid(k):
    return 5 + k


def n_a_vcz(k):
    return 6 + k


def n_a_kcf(k):
    return 7 + k


def n_a_kcq(k):
    return 8 + k


def n_a_vcb(k):
    return 9 + k


def n_a_kcn(k):
    return 13 + k


def n_a_v6(k):
    return 14 + k


def n_a_c1(k):
    return 6 * k - 5


def n_a_cmx(k):
    return 6 * k - 4


def n_a_cnm(k):
    return 6 * k - 3


def n_a_c2(k):
    return 6 * k - 2


def n_a_cs(k):
    return 6 * k - 1


def n_a_cg(k):
    return 6 * k


def n_a_rc(k):
    return 7 * k - 6


def n_a_cf(k):
    return 7 * k - 5


def n_a_y(k):
    return 7 * ((k - 1) // 5) + (k - 1) % 5 + 3


class Names:
    pass


def build(nc, a, out):
    ctx = ExitStack()
    with ctx:
        base = (nc.sbuf_base + 63) // 64 * 64
        arena = ctx.enter_context(nc.sbuf_tensor("arena", [P, (nc.sbuf_usable_end - base) // 4 - 16], F32))
        top = [base]

        def place(name, shape, dt=F32, at=None):
            size = 4 * int(np.prod(shape[1:]))
            if at is None:
                at = top[0]
                top[0] += (size + 31) // 32 * 32
            return nc.alloc_sbuf_tensor_at(name, shape, dt, offset=at)

        TB = 4 * T
        o_h = base + KT * TB
        o_g = o_h + 2 * KT * TB
        xT = place("xT", [P, KT, T])
        hH = place("hH", [P, KT, T], F32R)
        hL = place("hL", [P, KT, T], F32R)
        gH = place("gH", [P, FT, T], F32R)
        gL = place("gL", [P, FT, T], F32R)
        wR = [place(f"wR{i}", [P, KH, P]) for i in range(2)]
        wH = [place(f"wH{i}", [P, KH, P], F32R) for i in range(2)]
        wL = [place(f"wL{i}", [P, KH, P], F32R) for i in range(2)]
        sumsq = place("sumsq", [P, T])
        sqt = place("sqt", [P, T])
        rstd = place("rstd", [P, T])
        xn = place("xn", [P, 2, T])
        hf = place("hf", [P, 2, T])
        o_misc = top[0]
        sil = place("sil", [P, T])
        gf = place("gf", [P, T])
        cst = place("cst", [P, X_END])
        par = place("par", [P, max(C_END1, E_END)])
        mod = place("mod", [P, NMOD + N_NEXT])
        modA = place("modA", [P, 3 * KT])
        gate = place("gate", [P, 3 * KT])
        cond = place("cond", [P, D])
        acc = place("acc", [P, 2, 2])
        o_cst_end = {"bm": top[0]}
        bm = place("bm", [P, H, T])
        o_cst_end["cb"] = top[0]
        cb = place("cb", [P, TT, H, 32])
        tab = place("tab", [NB + 1, H])
        assert top[0] <= nc.sbuf_usable_end - 64, top[0] - nc.sbuf_usable_end
        pm = place("pm", [P, 2 * FT, T], at=o_g)
        ht = place("ht", [P, 2 * KT, T], at=o_h)
        xin = place("xin", [P, TT, D], at=o_g + 13 * TB)
        ada0 = [place(f"ada0{j}", [P, KT, D], at=at) for j, at in enumerate((o_g + 28 * TB, o_h, o_g + 28 * TB))]
        adaw = [place(f"adaw{j}", [P, D], at=at)
                for j, at in enumerate((o_misc - 4 * TB, o_misc - 2 * TB, o_g + 20 * TB, o_g + 42 * TB))]

        def pmv(name, tile, shape, dt=F32):
            return place(name, shape, dt, at=o_g + int(tile * TB))

        def htv(name, tile, shape, dt=F32):
            return place(name, shape, dt, at=o_h + int(tile * TB))

        OHR = pmv("ohr", 0, [NB + 1, 640])
        OHF = pmv("ohf", 2, [NB + 1, 1056])
        FLIP = pmv("flip", 5, [P, P])
        SKEW = pmv("skew", 6, [P, H, T])
        CROW = pmv("crow", 10, [H, 1056])
        CSKEW = pmv("cskew", 21, [P, H, 896])
        LM = pmv("LM", 30, [P, 7, P])
        RS = pmv("RS", 31.75, [P, T])
        w2k = pmv("w2k", 32.75, [P, 2, P])
        w2v = pmv("w2v", 33.25, [P, 2, HD])
        COL = pmv("COL", 33.5, [P, TT, NCOL])
        EM = pmv("EM", 33.75, [P, TT, H])
        EGC = pmv("EGC", 33.78125, [P, TT, H])
        NGC = pmv("NGC", 33.8125, [P, TT, H])
        BG = pmv("BG", 33.84375, [P, TT, H])
        DD = pmv("DD", 33.875, [P, TT, H])
        HR = pmv("HR", 33.90625, [P, TT, H])
        sma = pmv("sma", 33.9375, [P, 1])
        cv = xn
        nsq = hf
        smt = rstd
        AR = sil
        MR = gf
        NM = [pm[:, 34 + h, :] for h in range(H)]
        VD = pmv("VD", 38, [P, TT, H, HD + 1])
        WD = pmv("WD", 40.5, [P, 2, P])
        WT_ = pmv("WTm", 41, [P, 2, T])
        ST_ = [htv(f"STm{i}", 4 * i, [P, TT, T]) for i in range(2)]
        OD = htv("OD", 8, [P, TT, H * HD])
        OQ = htv("OQ", 10, [P, TT, H * HD])
        SEG = [htv(f"SEG{h}", h, [P, TT, P]) for h in range(H)]
        ZZ = SEG
        NN = [htv(f"NN{h}", 4 + h, [P, TT, P]) for h in range(H)]
        XX = [pmv(f"XX{h}", PD_Q + h, [P, TT, P]) for h in range(H)]
        PP = [pmv(f"PP{h}", (26, 27, 34, 35)[h], [P, TT, P]) for h in range(H)]
        QK = [pmv(f"QK{h}", 36 + h, [P, TT, P]) for h in range(H)]
        TMP = [pmv(f"TMP{i}", 40 + i, [P, TT, P]) for i in range(2)]
        NK = TMP
        KD = [htv(f"KD{i}", 12 + i, [P, TT, P]) for i in range(2)]
        KB = [htv(f"KB{i}", 14 + i, [P, TT, P]) for i in range(2)]
        VB = [pmv(f"VB{i}", 42 + i, [P, TT, P]) for i in range(2)]
        KTM = [htv(f"KTM{i}", 8 + i, [P, TT, P]) for i in range(2)]
        VTM = [pmv(f"VTM{i}", PB_C + i, [P, TT, P]) for i in range(2)]
        EGP = [pmv(f"EGP{i}", PB_X + i, [P, T]) for i in range(2)]
        KBT = [pmv(f"KBT{i}", PC_V + i, [P, T]) for i in range(2)]
        UU = VTM
        WW = [pmv(f"WW{i}", PC_K + i, [P, T]) for i in range(2)]
        SSt = place("SSt", [P, 2, 2, P], at=o_misc - 4 * TB)
        VN = place("VN", [P, H, HD], at=o_misc - 2 * TB)
        X2 = pmv("X2", 38, [P, 16, 32])
        X2H = [pmv(f"X2H{i}", 34 + i, [P, 16, 32], F32R) for i in range(2)]
        X2L = [pmv(f"X2L{i}", 36 + i, [P, 16, 32], F32R) for i in range(2)]
        o_s = o_misc - 7 * TB
        HID = place("HID", [P, 4, 32], at=o_s)
        HIE = place("HIE", [P, 4, 32], at=o_s + 512)
        HIC = place("HIC", [P, 4], at=o_s + 1024)
        KCF = place("KCF", [P, 32], at=o_s + 1088)
        KCQ = place("KCQ", [P, 32], at=o_s + 1088 + 128)
        VCB = place("VCB", [P, H, HD], at=o_s + TB)
        LC = place("LC", [P, H, 32], at=o_s + TB + 1536)
        PCT = place("PCT", [P, P], at=o_s + TB + 1024)
        KCB = place("KCB", [P, 2, 32], at=o_s + 1600)
        MX = place("MX", [P, 12], at=o_s + 1088 + 256)
        SM = place("SM", [P, 2, 12], at=o_s + 1408)
        CF = place("CF", [P, 12], at=o_s + 1504)
        V6 = htv("V6", 0, [P, TT, P])
        LL = [pmv(f"LL{i}", 34 + 4 * i, [P, H, T]) for i in range(2)]
        PTR = [htv(f"PTR{i}", 1 + i, [P, T]) for i in range(4)]
        YA = htv("YA", 6, [P, TT, H * HD])
        YT = htv("YT", 10, [P, H, HD])
        YQ = htv("YQ", 8, [P, TT, H * HD])

        o_bm = o_cst_end["bm"]
        COS = place("COS", [P, T], at=o_bm)
        SIN = place("SIN", [P, T], at=o_bm + TB)
        CMASK = place("CMASK", [P, T], at=o_bm + 2 * TB)
        WS = place("WS", [P, 4, P], at=o_bm + 3 * TB)
        BS = place("BS", [P, 4, P], at=o_cst_end["cb"])
        POSI = htv("POSI", 0, [P, T], I32)
        ANG = htv("ANG", 1, [P, T])
        TRN = htv("TRN", 2, [P, T])
        RED = [htv(f"RED{i}", 3 + i, [P, T]) for i in range(2)]
        VG = [pmv(f"VG{g}", 36 + g, [P, TT, P]) for g in range(4)]
        SQ2 = [(hf, xn)[g // 2][:, g % 2, :] for g in range(4)]
        LG = [htv(f"LG{i}", 4 + 2 * i, [P, 2, T]) for i in range(2)]
        AD = [pmv(f"AD{i}", 36 + i, [P, T]) for i in range(2)]
        ADT = [pmv(f"ADT{i}", 38 + i, [P, T]) for i in range(2)]
        SGT = [pmv(f"SGT{i}", 40 + i, [P, TT, P]) for i in range(2)]
        RTM = [pmv(f"RTM{i}", 42 + i, [P, T]) for i in range(2)]
        VA = [pmv(f"VA{h}", 24 + h, [P, TT, P]) for h in range(4)]
        YD = pmv("YD", 28, [P, TT, 4 * P])
        YDQ = pmv("YDQ", 32, [P, TT, 4 * P])
        MX2 = place("MX2", [P, 2, 2], at=o_s)
        NX2 = place("NX2", [P, 2, 2], at=o_s + 32)
        SM2 = place("SM2", [P, 2, 2], at=o_s + 64)
        RC2 = place("RC2", [P, 2, 2], at=o_s + 96)
        RT2 = place("RT2", [P, 2, 1], at=o_s + 128)
        LQ = place("LQ", [P, 2], at=o_s + 160)
        LE = place("LE", [P, 2], at=o_s + 192)
        NL = place("NL", [P, 1], at=o_s + 224)
        HR2 = place("HR2", [P, TT, 4], at=o_s + 256)

        ident = cst[:, X_ID:X_ID + P]
        ones = cst[:, X_ONE:X_ONE + P]
        heads = cst[:, X_BO:X_BO + P]
        causal = cst[:, X_CM:X_CM + P]
        causalT = cst[:, X_CMT:X_CMT + P]
        tri = cst[:, X_TRI:X_TRI + P]
        rot = cst[:, X_ROT:X_ROT + P]
        eps = cst[:, X_EPS:X_EPS + 1]
        eps64 = cst[:, X_E64:X_E64 + 1]
        bank = [ctx.enter_context(nc.psum_tensor(f"bank{i}", [P, 512], F32)) for i in range(8)]

        def col(c, n=1):
            return par[:, c:c + n]

        def cbank(i):
            return bank[(5, 7)[i % 2]]

        def bc(ap, shape):
            return ap.broadcast_to(shape)

        S = Names()
        layer_sems = []

        def sem(name, layered=True):
            s = ctx.enter_context(nc.semaphore(name))
            if layered:
                layer_sems.append(s)
            return s

        S.const_in = sem("const_in", False)
        S.x_in = sem("x_in", False)
        S.x_turned = sem("x_turned", False)
        S.x_copied = sem("x_copied", False)
        S.tab_in = sem("tab_in", False)
        S.tab_set = sem("tab_set", False)
        S.bias_ps = sem("bias_ps", False)
        S.bias_sb = sem("bias_sb", False)
        S.bias_out = sem("bias_out", False)
        S.skew_in = sem("skew_in", False)
        S.bm_ps = sem("bm_ps", False)
        S.bm_set = sem("bm_set", False)
        S.cb_set = sem("cb_set", False)
        S.fin = sem("fin", False)
        S.stored0 = sem("stored0", False)
        S.stored1 = sem("stored1", False)
        S.release = sem("release", False)
        S.acked = sem("acked", False)
        S.pos_in = sem("pos_in", False)
        S.trig_v = sem("trig_v", False)
        S.trig_a = sem("trig_a", False)
        S.first_sums = sem("first_sums", False)
        S.cond = sem("cond", False)
        S.ada0_in0 = sem("ada0_in0", False)
        S.ada0_in1 = sem("ada0_in1", False)
        S.ada0_in2 = sem("ada0_in2", False)
        S.ada0_done = sem("ada0_done", False)
        S.first_sq = sem("first_sq", False)
        S.arrived = sem("arrived")
        S.w_in0 = sem("w_in0")
        S.w_in1 = sem("w_in1")
        S.w_hi = sem("w_hi")
        S.w_lo = sem("w_lo")
        S.w_used = sem("w_used")
        S.sil = sem("sil")
        S.g_mul = sem("g_mul")
        S.g_hi = sem("g_hi")
        S.g_lo = sem("g_lo")
        S.x_new = sem("x_new")
        S.par_in = sem("par_in")
        S.ada_in0 = sem("ada_in0")
        S.ada_in1 = sem("ada_in1")
        S.ada_in2 = sem("ada_in2")
        S.ada_in3 = sem("ada_in3")
        S.ada_sum = sem("ada_sum")
        S.ada_done = sem("ada_done")
        S.mod_set = sem("mod_set")
        S.pool = sem("pool")
        S.sumsq = sem("sumsq")
        S.ms = sem("ms")
        S.ln = sem("ln")
        S.rstd = sem("rstd")
        S.last_sq = sem("last_sq")
        S.hf = sem("hf")
        S.h_hi = sem("h_hi")
        S.h_lo = sem("h_lo")
        S.mixc_in0 = sem("mixc_in0")
        S.mixc_in1 = sem("mixc_in1")
        S.mixc_in2 = sem("mixc_in2")
        S.mixc_in3 = sem("mixc_in3")
        S.pm = sem("pm")
        S.cv = sem("cv")
        S.conv_silu = sem("conv_silu")
        S.g_sig = sem("g_sig")
        S.sm_v = sem("sm_v")
        S.sm_a = sem("sm_a")
        S.ar_ps = sem("ar_ps")
        S.colp = sem("colp")
        S.b_pool = sem("b_pool")
        S.b_cv = sem("b_cv")
        S.b_ss = sem("b_ss")
        S.b_rs = sem("b_rs")
        S.n_sq = sem("n_sq")
        S.n_ss = sem("n_ss")
        S.n_rs = sem("n_rs")
        S.n_out = sem("n_out")
        S.d_nmp = sem("d_nmp")
        S.d_nm = sem("d_nm")
        S.d_vt = sem("d_vt")
        S.d_vd = sem("d_vd")
        S.d_one = sem("d_one")
        S.d_s = sem("d_s")
        S.d_wd = sem("d_wd")
        S.d_wt = sem("d_wt")
        S.d_nd = sem("d_nd")
        S.d_post = sem("d_post")
        S.d_sv = sem("d_sv")
        S.o_sq = sem("o_sq")
        S.o_v = sem("o_v")
        S.o_rs = sem("o_rs")
        S.o_t = sem("o_t")
        S.c_kt = sem("c_kt")
        S.c_v1 = sem("c_v1")
        S.c_vt = sem("c_vt")
        S.c_a = sem("c_a")
        S.c_bp = sem("c_bp")
        S.c_gp = sem("c_gp")
        S.c_grp = sem("c_grp")
        S.c_v2 = sem("c_v2")
        S.c_kk = sem("c_kk")
        S.c_kq = sem("c_kq")
        S.c_qd = sem("c_qd")
        S.c_xt = sem("c_xt")
        S.c_nk = sem("c_nk")
        S.c_z = sem("c_z")
        S.c_zc = sem("c_zc")
        S.c_xz = sem("c_xz")
        S.c_xu = sem("c_xu")
        S.c_zp = sem("c_zp")
        S.c_pu = sem("c_pu")
        S.c_u = sem("c_u")
        S.c_uc = sem("c_uc")
        S.c_w = sem("c_w")
        S.c_wc = sem("c_wc")
        S.c_wp = sem("c_wp")
        S.c_vn = sem("c_vn")
        S.c_o = sem("c_o")
        S.c_od = sem("c_od")
        S.c_sp = sem("c_sp")
        S.c_st = sem("c_st")
        S.a_x2 = sem("a_x2")
        S.a_x2h = sem("a_x2h")
        S.a_x2l = sem("a_x2l")
        S.a_v = sem("a_v")
        S.a_he = sem("a_he")
        S.a_kc = sem("a_kc")
        S.a_kcs = sem("a_kcs")
        S.a_kcr = sem("a_kcr")
        S.a_vt = sem("a_vt")
        S.a_cl = sem("a_cl")
        S.a_cv = sem("a_cv")
        S.a_ce = sem("a_ce")
        S.a_ct = sem("a_ct")
        S.a_ctc = sem("a_ctc")
        S.a_co = sem("a_co")
        S.a_s = sem("a_s")
        S.a_l = sem("a_l")
        S.a_nm = sem("a_nm")
        S.a_e = sem("a_e")
        S.a_t = sem("a_t")
        S.a_tc = sem("a_tc")
        S.a_pv = sem("a_pv")
        S.a_yv = sem("a_yv")
        S.y_hi = sem("y_hi")
        S.y_lo = sem("y_lo")
        S.w_in = [S.w_in0, S.w_in1]
        S.ws_in = S.ada_in0
        S.bs_in = S.ada_in1
        S.ws_set = S.b_pool
        S.lam_v = S.b_cv
        S.lam_ps = S.b_ss
        S.lam_e = S.b_rs
        S.gelu = S.conv_silu
        S.rot_ps = S.c_kt
        S.rot_cos = S.c_qd
        S.rot_sin = S.c_v1
        S.rot_x = S.c_v2
        S.va_t = S.d_vt
        S.va_sb = S.d_vd
        S.vg_t = S.c_vt
        S.vg_sb = S.c_a
        S.mixed = S.c_u
        S.mix_b = S.c_uc
        S.mix_y = S.c_w
        S.s_ps = S.a_s
        S.s_max = S.a_l
        S.s_neg = S.a_nm
        S.s_exp = S.a_e
        S.s_small = S.a_v
        S.s_diff = S.a_cv
        S.s_t = S.a_t
        S.s_tsb = S.a_tc
        S.s_val = S.a_pv
        S.s_y = S.a_yv
        S.f_tap = S.c_z
        S.f_conv = S.c_xu
        S.ada_in = [S.ada_in0, S.ada_in1, S.ada_in2, S.ada_in3]
        S.ada0_in = [S.ada0_in0, S.ada0_in1, S.ada0_in2]
        S.stored = [S.stored0, S.stored1]
        bias_dram = nc.dram_tensor("bias_by_distance", (H, 640), F32, kind="Internal").ap()
        cbias_dram = nc.dram_tensor("bias_by_distance_up", (H, 1056), F32, kind="Internal").ap()

        layer_range = range(layer_sems[0].num, layer_sems[-1].num + 1)
        assert [s.num for s in layer_sems] == list(layer_range)

        block = ctx.enter_context(nc.Block())

        def end_layer(e, l):
            e.sem_inc(S.arrived, 1)
            e.wait_ge(S.release, l + 1)
            e.sem_inc(S.acked, 1)

        @block.sync
        def _(sp):
            sp.dma_start(cst[:, :], a["cst"]).then_inc(S.const_in, 16)
            sp.dma_start(cond[:, :], bc(a["c"], [P, D])).then_inc(S.const_in, 16)
            sp.dma_start(xin[:, :, :], a["x"].rearrange("(t p) d -> p t d", p=P)).then_inc(S.x_in, 16)
            sp.wait_ge(S.tab_set, 1)
            sp.dma_start(tab[0:NB, :], a["t5_table"]).then_inc(S.tab_in, 16)
            sp.dma_start(OHR[:, :], a["c_ohr"]).then_inc(S.tab_in, 16)
            sp.dma_start(OHF[:, :], a["c_ohf"]).then_inc(S.tab_in, 16)
            sp.dma_start(FLIP[:, :], a["c_flip"]).then_inc(S.tab_in, 16)
            sp.dma_start(ada0[0][:, :, :], a["ada_first"][:, 0:KT]).then_inc(S.ada0_in[0], 16)
            sp.wait_ge(S.bias_sb, 1)
            sp.dma_start(bias_dram, hf[0:H, :, :].rearrange("p a b -> p (a b)")[:, 0:640]).then_inc(S.bias_out, 16)
            sp.dma_start(cbias_dram, CROW[:, :]).then_inc(S.bias_out, 16)
            sp.wait_ge(S.bias_out, 32)
            sp.dma_start(SKEW[:, :, :], bass.AP(bias_dram.tensor, 0, [[1, P], [640, H], [1, T]])).then_inc(S.skew_in, 16)
            sp.dma_start(CSKEW[:, :, :], bass.AP(cbias_dram.tensor, 0, [[1, P], [1056, H], [1, 896]])).then_inc(S.skew_in, 16)
            sp.dma_start(ada0[1][:, :, :], a["ada_first"][:, KT:2 * KT]).then_inc(S.ada0_in[1], 16)
            sp.wait_ge(S.ada0_done, 1)
            sp.dma_start(ada0[2][:, :, :], a["ada_first"][:, 2 * KT:3 * KT]).then_inc(S.ada0_in[2], 16)
            sp.wait_ge(S.bm_set, H)
            sp.wait_ge(S.cb_set, 1)
            sp.wait_ge(S.x_turned, KT)

            def unit(u, src, tiles, n, first=False):
                if not first:
                    sp.wait_ge(S.w_lo, u - 1)
                sp.dma_start(wR[n][:, 0:tiles, :], src).then_inc(S.w_in[n], 16)

            def stream(ubase, count, w, l, tiles):
                if ubase == 0:
                    for n in range(2):
                        unit(n, w[l, n], tiles, n, True)
                with sp.Fori(1 if ubase == 0 else 0, count // 2) as i:
                    for n in range(2):
                        unit(ubase + 2 * i + n, w[l, 2 * i + n], tiles, n)

            def stream_ada(ubase, w, aw, l, norm, turns, done):
                def tiles(t, parity, wait=True):
                    if wait:
                        sp.wait_ge(S.ada_done, done + t - 1)
                    for j in range(2):
                        s = 2 * parity + j
                        sp.dma_start(adaw[s][:, :], aw[l, 2 * t + j]).then_inc(S.ada_in[s], 16)

                for n in range(2):
                    unit(ubase + n, w[l, n], KT, n, ubase == 0)
                sp.wait_ge(S.h_lo, KT * (norm + 1))
                tiles(0, 0, False)
                tiles(1, 1, False)

                def turn(t, parity, ada):
                    for n in range(2):
                        unit(ubase + 2 * t + n, w[l, 2 * t + n], KT, n)
                    if ada:
                        tiles(t, parity)
                turn(1, 1, False)
                with sp.Fori(1, turns // 2) as i:
                    for e in range(2):
                        turn(2 * i + e, e, True)
                with sp.Fori(turns, FT) as i:
                    turn(i, 0, False)

            def layer1(l):
                sp.dma_start(par[:, 0:C_END1], a["par1"][l]).then_inc(S.par_in, 16)
                stream_ada(U_UP1, a["ffn1_w13"], a["ada_w1"], l, 0, ADA1, 0)
                stream(U_DN1, 2 * KT, a["ffn1_w2"], l, KH)
                stream(U_IN, N_IN0, a["w_in"], l, KT)
                sp.dma_start(LM[:, :, :], a["c_lm"]).then_inc(S.mixc_in0, 16)
                sp.dma_start(RS[64:72, :], a["c_rs"]).then_inc(S.mixc_in1, 16)
                sp.dma_start(w2k[:, :, :], a["w2k"][l]).then_inc(S.mixc_in2, 16)
                sp.dma_start(w2v[:, :, :], a["w2v"][l]).then_inc(S.mixc_in3, 16)
                with sp.Fori(0, 8) as i:
                    unit(U_MIXED + 2 * i, a["w_in"][l, N_IN0 + i], KT, 0)
                    unit(U_MIXED + 2 * i + 1, a["cmp_w1"][l, i], KT, 1)
                for n in range(2):
                    unit(U_LAST + n, a["w_in"][l, N_IN - 2 + n], KT, n)
                stream(U_OUT, KT, a["w_out"], l, KT)
                stream_ada(U_UP2, a["ffn2_w13"], a["ada_w2"], l, 2, ADA2, ADA1)
                stream(U_DN2, 2 * KT, a["ffn2_w2"], l, KH)

            with sp.Fori(0, L) as l:
                layer1(l)
                sp.wait_ge(S.arrived, 4)
                sp.sem_clear(layer_range)
                sp.sem_inc(S.release, 1)

            sp.dma_start(POSI[:, :], bass.AP(a["positions"].tensor, 0, [[0, P], [1, T]])).then_inc(S.pos_in, 16)
            sp.wait_ge(S.trig_a, 2)

            def layer2(l):
                sp.dma_start(par[:, 0:E_END], a["par2"][l]).then_inc(S.par_in, 16)
                sp.dma_start(WS[:, :, :], a["sgu_w"][l]).then_inc(S.ws_in, 16)
                sp.dma_start(BS[:, :, :], bc(a["sgu_b"][l], [P, 4, P])).then_inc(S.bs_in, 16)
                stream(V_IN, N_IN2, a["w_in2"], l, KT)
                stream(V_OUT, KT, a["w_out2"], l, KT)
                stream(V_UP, 2 * FT, a["w_up"], l, KT)
                stream(V_DN, 2 * KT, a["w_down"], l, KH)

            with sp.Fori(0, L) as l:
                layer2(l)
                sp.wait_ge(S.arrived, 4)
                sp.sem_clear(layer_range)
                sp.sem_inc(S.release, 1)

            for t in range(TT):
                sp.wait_ge(S.fin, 8 * (t + 1))
                sp.dma_start(out[t * P:(t + 1) * P, :], xin[:, t, :]).then_inc(S.stored[t % 2], 16)
            for s in S.stored:
                sp.wait_ge(s, 16 * (TT // 2))

        @block.scalar
        def _(act):
            def hi(u, count, tiles, n, first=False):
                act.wait_ge(S.w_in[n], 16 * count)
                if not first:
                    act.wait_ge(S.w_used, u - 1)
                act.activation(wH[n][:, 0:tiles, :], wR[n][:, 0:tiles, :], ACT.Copy).then_inc(S.w_hi, 1)

            def hi_ahead(ubase, i, n, tiles):
                hi(ubase + 2 * i + n + 2, ubase // 2 + i + 2, tiles, n)

            def up(ubase, gbase, next_tiles):
                def turn(i, tiles):
                    hi_ahead(ubase, i, 0, tiles)
                    act.wait_ge(S.w_used, ubase + 2 * i + 1)
                    if gbase or later(i):
                        act.wait_ge(S.g_mul, gbase + i)
                    act.activation(sil[:, :], bank[0][:, :], ACT.Silu).then_inc(S.sil, 1)
                    hi_ahead(ubase, i, 1, tiles)
                turn(0, KT)
                with act.Fori(1, FT - 1) as i:
                    turn(i, KT)
                turn(FT - 1, next_tiles)

            def plain(ubase, pairs, tiles, next_tiles):
                with act.Fori(0, pairs - 1) as i:
                    for n in range(2):
                        hi_ahead(ubase, i, n, tiles)
                if next_tiles:
                    for n in range(2):
                        hi_ahead(ubase, pairs - 1, n, next_tiles)

            def norm(n, sub, start=False):
                act.wait_ge(S.ms, n + 1)
                inverse_root(rstd[:, :], bank[6][:, :], 1.0 / D, eps, S.rstd)
                if start:
                    hi(0, 1, KT, 0, True)
                for k in range(KT):
                    act.wait_ge(S.hf, KT * n + k + 1)
                    act.activation(hH[:, k, :], hf[:, k % 2, :], ACT.Identity,
                                   bias=mod[:, 3 * sub * KT + k:3 * sub * KT + k + 1]).then_inc(S.h_hi, 1)
                if start:
                    hi(1, 1, KT, 1, True)

            def last_square(xnew):
                act.wait_ge(S.x_new, xnew)
                act.activation(sqt[:, :], xT[:, KT - 1, :], ACT.Square).then_inc(S.last_sq, 1)

            logs = [0]

            def inverse_root(dst, src, scale, bias, out):
                act.activation(dst, src, ACT.Ln, bias=bias, scale=scale).then_inc(S.ln, 1)
                logs[0] += 1
                act.wait_ge(S.ln, logs[0])
                act.activation(dst, dst, ACT.Exp, scale=-0.5).then_inc(out, 1)

            def conv_silu(j):
                act.wait_ge(S.cv, 4 * (j + 1))
                act.activation(pm[:, PC_Q + j, :], cv[:, j % 2, :], ACT.Silu).then_inc(S.conv_silu, 1)

            def beside(k):
                r = slice(R_F, R_F + 8)
                if k == 0:
                    act.activation(sma[r, :], par[r, C_SMA:C_SMA + 1], ACT.Exp).then_inc(S.sm_a, 1)
                    act.wait_ge(S.sm_v, 2)
                    act.activation(smt[r, :], smt[r, :], ACT.Exp, scale=-1.0).then_inc(S.sm_a, 1)
                    act.wait_ge(S.sm_a, 2)
                    act.activation(smt[r, :], smt[r, :], ACT.Ln, bias=ones[r, 0:1]).then_inc(S.sm_a, 1)
                    act.wait_ge(S.a_x2, 10)
                    act.activation(X2H[1][:, :, :], X2[:, :, :], ACT.Copy).then_inc(S.a_x2h, 1)
                elif k == 1:
                    for p in (slice(0, 12), slice(R_BE, R_BE + 4)):
                        act.activation(pm[p, PS, :], pm[p, PS, :], ACT.Sigmoid).then_inc(S.g_sig, 1)
                elif 3 <= k < 8:
                    conv_silu(k - 3)

            def project_mixed():
                act.wait_ge(S.a_x2, 5)
                act.activation(X2H[0][:, :, :], X2[:, :, :], ACT.Copy).then_inc(S.a_x2h, 1)
                for k in range(9):
                    for n in range(2):
                        hi(U_MIXED + 2 * k + n + 2, U_MIXED // 2 + k + 2, KT, n)
                    beside(k)

            def roots(first, b):
                js = [(S.n_ss, first + i + 1, bank[i], HEAD_NORMS[first + i][1], eps64 if HEAD_NORMS[first + i][2] else eps,
                       S.n_rs) for i in range(4)]
                if b:
                    js.append((S.b_ss, 1, bank[4], 1.0 / (2 * P), eps, S.b_rs))
                for ready, count, o, scale, bias, done in js:
                    act.wait_ge(ready, count)
                    act.activation(o[:, :], o[:, :], ACT.Ln, bias=bias, scale=scale).then_inc(S.ln, 1)
                    logs[0] += 1
                act.wait_ge(S.ln, logs[0])
                for ready, count, o, scale, bias, done in js:
                    act.activation(o[:, :], o[:, :], ACT.Exp, scale=-0.5).then_inc(done, 1)

            def scalars():
                conv_silu(5)
                for j in range(2):
                    act.activation(pm[:, PC_Z + j, :], pm[:, PC_Z + j, :], ACT.Silu)
                act.wait_ge(S.pm, N_IN)
                for j in range(2):
                    act.activation(pm[:, PD_O + j, :], pm[:, PD_O + j, :], ACT.Sigmoid)
                roots(0, True)
                act.wait_ge(S.sm_v, n_cols(1))
                act.activation(EM[:, :, :], COL[:, :, K_M:K_M + 4], ACT.Exp, scale=-1.0).then_inc(S.sm_a, 1)
                act.activation(EGC[:, :, :], COL[:, :, K_GC:K_GC + 4], ACT.Exp).then_inc(S.sm_a, 1)
                act.wait_ge(S.a_v, n_a_hb(1))
                act.activation(HIE[:, :, :], HID[:, :, :], ACT.Exp, scale=-1.0).then_inc(S.a_he, 1)
                roots(4, False)
                act.wait_ge(S.a_kcs, 1)
                inverse_root(KCQ[:, :], bank[6][:, 32:64], 1.0 / HD, eps, S.a_kcr)

            def head_out(n):
                act.wait_ge(S.o_v, n_o_red(n + 1))
                inverse_root(HR[:, :, :], HR[:, :, :], 1.0 / HD, eps, S.o_rs)

            def mix_d():
                for h in range(H):
                    act.wait_ge(S.d_nmp, h + 1)
                    act.activation(NM[h], bank[h][:, :], ACT.Copy, scale=-1.0).then_inc(S.d_nm, 1)
                for h in range(H):
                    for j in range(TT):
                        u = TT * h + j
                        act.wait_ge(S.d_wd, u + 1)
                        if u >= 2:
                            act.wait_ge(S.d_sv, u - 1)
                        act.activation(WT_[:, u % 2, j * P:(j + 1) * P], WD[:, u % 2, :], ACT.Exp,
                                       bias=COL[:, j, K_A + h:K_A + h + 1]).then_inc(S.d_wt, 1)
                        if j < TT - 1:
                            act.activation(WT_[:, u % 2, (j + 1) * P:], NM[h][:, (j + 1) * P:], ACT.Exp,
                                           bias=COL[:, j, K_A + h:K_A + h + 1]).then_inc(S.d_wt, 1)
                head_out(0)

            def mix_c():
                for p in range(2):
                    act.wait_ge(S.c_vt, p + 1)
                    act.activation(VTM[p][:, :, :], bank[2 + p][:, :].rearrange("p (t c) -> p t c", t=TT),
                                   ACT.Copy).then_inc(S.c_a, 1)
                for p in range(2):
                    act.wait_ge(S.c_gp, p + 1)
                    act.activation(EGP[p][:, :], bank[6 + p][:, :], ACT.Exp).then_inc(S.c_a, 1)
                for h in range(H):
                    act.wait_ge(S.c_v1, n_c_tmp(h + 1))
                    for t in range(TT):
                        act.activation(SEG[h][:, t, :], TMP[h % 2][:, t, :], ACT.Exp,
                                       bias=NGC[:, t, h:h + 1]).then_inc(S.c_a, 1)
                for h in range(H):
                    act.wait_ge(S.c_xt, h + 1)
                    act.activation(XX[h][:, :, :], bank[h][:, :].rearrange("p (t c) -> p t c", t=TT),
                                   ACT.Copy).then_inc(S.c_a, 1)
                with act.Fori(1, 7) as k:
                    for h in range(H):
                        act.wait_ge(S.c_z, 4 * k + h - 3)
                        act.activation(ZZ[h][:, :, :], bank[h][:, :].rearrange("p (t c) -> p t c", t=TT),
                                       ACT.Copy).then_inc(S.c_zc, 1)
                for p in range(2):
                    act.wait_ge(S.c_w, p + 1)
                    act.activation(WW[p][:, :], bank[2 + p][:, :], ACT.Copy).then_inc(S.c_wc, 1)
                for t in range(TT):
                    act.wait_ge(S.c_o, t + 1)
                    act.activation(OD[:, t, :], bank[5 + t % 2][:, 0:H * HD], ACT.Copy).then_inc(S.c_od, 1)
                head_out(1)

            def mix_a():
                for n in range(2 * TT + 1):
                    i, b = n // 2, n % 2
                    if b == 0 and n < 2 * TT:
                        act.wait_ge(S.a_cv, n_a_c2(i + 1))
                        act.activation(LC[:, :, :], LC[:, :, :], ACT.Exp).then_inc(S.a_ce, 1)
                        act.wait_ge(S.a_ct, i + 1)
                        act.activation(PCT[:, :], cbank(i)[:, P:2 * P], ACT.Copy).then_inc(S.a_ctc, 1)
                    if n:
                        for h in range(H):
                            u = 4 * (n - 1) + h
                            w = ((n - 1) // 2 + 1) * P
                            act.wait_ge(S.a_t, u + 1)
                            if u >= 4:
                                act.wait_ge(S.a_pv, u - 3)
                            act.activation(PTR[h][:, 0:w], bank[2 + h % 2][:, 0:w], ACT.Copy).then_inc(S.a_tc, 1)
                    if n == 2 * TT:
                        break
                    act.wait_ge(S.a_nm, n + 1)
                    w = (i + 1) * P
                    for h in range(H):
                        act.activation(LL[b][:, h, 0:w], LL[b][:, h, 0:w], ACT.Exp,
                                       bias=MX[:, 4 * (b + 1) + h:4 * (b + 1) + h + 1],
                                       accum_out=SM[:, i % 2, 4 * (b + 1) + h:4 * (b + 1) + h + 1]).then_inc(S.a_e, 1)
                act.wait_ge(S.o_v, n_o_red(3))
                inverse_root(HR[:, 0:1, :], HR[:, 0:1, :], 1.0 / (2 * P), eps, S.o_rs)

            def mix_out():
                act.wait_ge(S.o_v, n_o_y(6))
                for k, tile in enumerate(Y_TILES):
                    act.activation(hH[:, k, :], pm[:, tile, :], ACT.Copy).then_inc(S.y_hi, 1)

            act.wait_ge(S.const_in, 32)
            act.activation(cond[:, :], cond[:, :], ACT.Silu).then_inc(S.cond, 1)
            act.wait_ge(S.x_copied, KT)
            act.activation(sqt[:, :], xT[:, KT - 1, :], ACT.Square).then_inc(S.first_sums, 1)

            def layer1(l):
                norm(0, 0, True)
                up(U_UP1, 0, KH)
                plain(U_DN1, KT, KH, KT)
                last_square(KT)
                norm(1, 1)
                plain(U_IN, N_IN0 // 2, KT, KT)
                project_mixed()
                scalars()
                mix_d()
                mix_c()
                mix_a()
                mix_out()
                plain(U_OUT, KT // 2, KT, KT)
                last_square(2 * KT)
                norm(2, 2)
                up(U_UP2, FT, KH)
                plain(U_DN2, KT, KH, 0)
                last_square(3 * KT)
                act.wait_ge(S.last_sq, 3)

            with act.Fori(0, L) as l:
                layer1(l)
                end_layer(act, l)

            act.wait_ge(S.trig_v, 22)
            act.activation(SIN[:, :], RED[0][:, :], ACT.Sin).then_inc(S.trig_a, 1)
            act.activation(COS[:, :], RED[1][:, :], ACT.Sin).then_inc(S.trig_a, 1)

            def beside2(k):
                if k < 4:
                    for tile in ((QV, QV + 1), (QV + 2, QV + 3), (QU, QU + 1), (QU + 2, QU + 3))[k]:
                        act.wait_ge(S.pm, N_IN0_2)
                        act.activation(pm[:, tile, :], pm[:, tile, :], ACT.Gelu_apprx_tanh).then_inc(S.gelu, 1)
                    if k == 3:
                        act.wait_ge(S.lam_ps, 1)
                        act.activation(LE[:, :], bank[6][:, 0:2], ACT.Exp).then_inc(S.lam_e, 1)
                elif k == 4:
                    for g in range(4):
                        act.wait_ge(S.n_ss, g + 1)
                        act.activation(bank[2 + g][:, :], bank[2 + g][:, :], ACT.Ln, bias=eps, scale=1.0 / P).then_inc(S.ln, 1)
                        logs[0] += 1
                    act.wait_ge(S.ln, logs[0])
                    for g in range(4):
                        act.activation(bank[2 + g][:, :], bank[2 + g][:, :], ACT.Exp, scale=-0.5).then_inc(S.n_rs, 1)
                elif k == 7:
                    for g in range(4):
                        act.wait_ge(S.vg_t, g + 1)
                        act.activation(VG[g][:, :, :], bank[2 + g][:, :].rearrange("p (t c) -> p t c", t=TT),
                                       ACT.Copy).then_inc(S.vg_sb, 1)

            def project2():
                for k in range(N_IN2 - N_IN0_2):
                    u = V_IN + N_IN0_2 + k + 2
                    hi(u, u // 2 + 1, KT, k % 2)
                    beside2(k)

            def mix2():
                act.wait_ge(S.pm, N_IN2)
                act.wait_ge(S.mix_y, 4)
                for k in range(4):
                    act.activation(hH[:, k, :], pm[:, Y2_TILES[k], :], ACT.Copy).then_inc(S.y_hi, 1)
                for h in range(4):
                    act.wait_ge(S.va_t, h + 1)
                    act.activation(VA[h][:, :, :], bank[2 + h][:, :].rearrange("p (t c) -> p t c", t=TT),
                                   ACT.Copy).then_inc(S.va_sb, 1)
                for n in range(17):
                    if n < 16:
                        w = (n % TT + 1) * P
                        act.wait_ge(S.s_neg, n + 1)
                        for m in range(2):
                            act.activation(LG[n % 2][:, m, 0:w], LG[n % 2][:, m, 0:w], ACT.Exp, bias=NX2[:, n % 2, m:m + 1],
                                           scale=HD ** -0.5, accum_out=SM2[:, n % 2, m:m + 1]).then_inc(S.s_exp, 1)
                    if n:
                        u = n - 1
                        w = (u % TT + 1) * P
                        act.wait_ge(S.s_t, u + 1)
                        if u >= 2:
                            act.wait_ge(S.s_val, u - 1)
                        act.activation(ADT[u % 2][:, 0:w], bank[4 + u % 2][:, 0:w], ACT.Copy).then_inc(S.s_tsb, 1)
                act.wait_ge(S.o_v, 4)
                inverse_root(HR2[:, :, :], HR2[:, :, :], 1.0 / P, eps, S.o_rs)
                for k in range(4, KT):
                    act.wait_ge(S.o_v, 5 + k)
                    act.activation(hH[:, k, :], pm[:, Y2_TILES[k], :], ACT.Copy).then_inc(S.y_hi, 1)

            def up2(ubase, next_tiles):
                def last_tap(i, half):
                    tile = i + FT * half
                    act.activation(xn[:, half, :], bank[half][:, :], ACT.Identity, bias=par[:, bass.ds(E_CB + tile, 1)],
                                   scale=par[:, bass.ds(E_CW + 3 * tile + 2, 1)]).then_inc(S.f_tap, 1)

                def turn(i, tiles):
                    hi_ahead(ubase, i, 0, tiles)
                    act.wait_ge(S.w_used, ubase + 2 * i + 1)
                    if later(i):
                        act.wait_ge(S.g_mul, i)
                    last_tap(i, 0)
                    act.wait_ge(S.f_conv, 4 * i + 2)
                    act.activation(sil[:, :], xn[:, 0, :], ACT.Silu).then_inc(S.sil, 1)
                    act.wait_ge(S.w_used, ubase + 2 * i + 2)
                    last_tap(i, 1)
                    hi_ahead(ubase, i, 1, tiles)
                turn(0, KT)
                with act.Fori(1, FT - 1) as i:
                    turn(i, KT)
                turn(FT - 1, next_tiles)

            def layer2(l):
                logs[0] = 0
                norm(0, 0, True)
                plain(V_IN, N_IN0_2 // 2, KT, KT)
                project2()
                mix2()
                plain(V_OUT, KT // 2, KT, KT)
                last_square(KT)
                norm(1, 1)
                up2(V_UP, KH)
                plain(V_DN, KT, KH, 0)
                last_square(2 * KT)
                act.wait_ge(S.last_sq, 2)

            with act.Fori(0, L) as l:
                layer2(l)
                end_layer(act, l + L)
            logs[0] = 0
            act.wait_ge(S.ms, 1)
            inverse_root(rstd[:, :], bank[6][:, :], 1.0 / D, eps, S.rstd)

        @block.vector
        def _(dve):
            dve.memset(tab[:, :], MASKED).then_inc(S.tab_set, 1)
            for k in range(KT):
                dve.wait_ge(S.x_turned, k + 1)
                dve.tensor_copy(xT[:, k, :], bank[k][:, :]).then_inc(S.x_copied, 1)
            def dots(w, dst):
                return dve.tensor_tensor_reduce(w, w, cond[:, :], 1.0, 0.0, ALU.mult, ALU.add, dst)
            dve.wait_ge(S.cond, 1)

            def first(j):
                dve.wait_ge(S.ada0_in[j], 16)
                for t in range(KT):
                    mm = dots(ada0[j][:, t, :], mod[:, NMOD + j * KT + t:NMOD + j * KT + t + 1])
                mm.then_inc(S.ada0_done, 1)
            dve.wait_ge(S.bias_ps, 1)
            brow = hf[0:H, :, :].rearrange("p a b -> p (a b)")
            dve.tensor_copy(brow[:, 0:512], bank[0][0:H, :])
            dve.tensor_copy(brow[:, 512:640], bank[1][0:H, 0:P])
            for b, c, w in ((2, 0, 512), (3, 512, 512), (4, 1024, 32)):
                mm = dve.tensor_copy(CROW[:, c:c + w], bank[b][0:H, 0:w])
            mm.then_inc(S.bias_sb, 1)
            first(0)
            dve.wait_ge(S.skew_in, 32)
            sk = CSKEW[:, :, :].rearrange("p h (c s) -> p c h s", s=16)
            for n in range(32):
                c = 31 - n
                mm = dve.tensor_copy(cb[:, :, :, n], sk[:, c:c + 8 * TT - 7:8, :, 0])
            mm.then_inc(S.cb_set, 1)
            for h in range(H):
                dve.wait_ge(S.bm_ps, h + 1)
                dve.tensor_copy(bm[:, h, :], bank[4 + h][:, :]).then_inc(S.bm_set, 1)

            first(1)
            first(2)
            dve.wait_ge(S.ada0_done, 3)

            def lo(u, tiles, n):
                dve.wait_ge(S.w_hi, u + 1)
                dve.tensor_tensor(wL[n][:, 0:tiles, :], wR[n][:, 0:tiles, :], wH[n][:, 0:tiles, :].bitcast(F32),
                                  ALU.subtract).then_inc(S.w_lo, 1)

            def up(ubase, gbase, next_tiles, turns, done):
                def columns(i, parity):
                    for j in range(2):
                        s = 2 * parity + j
                        dve.wait_ge(S.ada_in[s], 8 * (done + i - parity) + 16)
                        dots(adaw[s][:, :], acc[:, parity, j:j + 1]).then_inc(S.ada_sum, 1)
                    dve.wait_ge(S.ada_sum, 2 * (done + i) + 2)
                    dve.tensor_copy(mod[:, bass.ds(N_NEXT + 2 * (done + i), 2)], acc[:, parity, :]).then_inc(S.ada_done, 1)

                def turn(i, tiles):
                    lo(ubase + 2 * i + 2, tiles, 0)
                    dve.wait_ge(S.sil, gbase + i + 1)
                    dve.wait_ge(S.w_used, ubase + 2 * i + 2)
                    dve.tensor_tensor(gf[:, :], bank[1][:, :], sil[:, :], ALU.mult).then_inc(S.g_mul, 1)
                    dve.wait_ge(S.g_mul, gbase + i + 1)
                    dve.tensor_copy(gH[:, i, :], gf[:, :]).then_inc(S.g_hi, 1)
                    dve.wait_ge(S.g_hi, gbase + i + 1)
                    dve.tensor_tensor(gL[:, i, :], gf[:, :], gH[:, i, :].bitcast(F32), ALU.subtract).then_inc(S.g_lo, 1)
                    lo(ubase + 2 * i + 3, tiles, 1)

                with dve.Fori(0, turns // 2) as i:
                    for e in range(2):
                        turn(2 * i + e, KT)
                        columns(2 * i + e, e)
                dve.wait_ge(S.ada_done, done + turns)
                with dve.Fori(turns, FT - 1) as i:
                    turn(i, KT)
                turn(FT - 1, next_tiles)

            def add_to_x(m, b, sub):
                dve.scalar_tensor_tensor(xT[:, m, :], bank[b][:, :], gate[:, bass.ds(sub * KT + m, 1)],
                                         xT[:, m, :], ALU.mult, ALU.add).then_inc(S.x_new, 1)

            def down(ubase, sub, next_tiles):
                def tile(m, b, tiles):
                    if tiles:
                        for n in range(2):
                            lo(ubase + 2 * m + 2 + n, tiles, n)
                    dve.wait_ge(S.w_used, ubase + 2 * m + 2)
                    add_to_x(m, b, sub)
                with dve.Fori(0, KT // 2 - 1) as j:
                    for n in range(2):
                        tile(2 * j + n, 2 + n, KH)
                tile(KT - 2, 2, KH)
                tile(KT - 1, 3, next_tiles)

            def project_in(ubase, count, bcol, next_tiles):
                def turn(i, tiles):
                    for n in range(2):
                        lo(ubase + 2 * i + n + 2, tiles, n)
                        dve.wait_ge(S.w_used, ubase + 2 * i + n + 1)
                        if bcol is None:
                            dve.tensor_copy(pm[:, 2 * i + n, :], bank[n][:, :]).then_inc(S.pm, 1)
                        else:
                            dve.tensor_scalar(pm[:, 2 * i + n, :], bank[n][:, :], par[:, bass.ds(bcol + 2 * i + n, 1)], None,
                                              ALU.add).then_inc(S.pm, 1)
                with dve.Fori(0, count // 2 - 1) as i:
                    turn(i, KT)
                turn(count // 2 - 1, next_tiles)

            def project_out(ubase, sub, next_tiles):
                def turn(i, tiles):
                    for n in range(2):
                        if tiles:
                            lo(ubase + 2 * i + n + 2, tiles, n)
                        dve.wait_ge(S.w_used, ubase + 2 * i + n + 1)
                        add_to_x(2 * i + n, n, sub)
                with dve.Fori(0, KT // 2 - 1) as i:
                    turn(i, KT)
                turn(KT // 2 - 1, next_tiles)

            def norm(n, sub):
                def low(k):
                    dve.wait_ge(S.h_hi, KT * n + k + 1)
                    dve.scalar_tensor_tensor(hL[:, k, :], hf[:, k % 2, :], mod[:, 3 * sub * KT + k:3 * sub * KT + k + 1],
                                             hH[:, k, :].bitcast(F32), ALU.add, ALU.subtract).then_inc(S.h_lo, 1)
                dve.wait_ge(S.rstd, n + 1)
                for k in range(KT):
                    if k >= 2:
                        dve.wait_ge(S.h_lo, KT * n + k - 1)
                    dve.scalar_tensor_tensor(hf[:, k % 2, :], xT[:, k, :], modA[:, sub * KT + k:sub * KT + k + 1], rstd[:, :],
                                             ALU.mult, ALU.mult).then_inc(S.hf, 1)
                    if k:
                        low(k - 1)
                low(KT - 1)

            def conv(dst, src, wcol, taps, sem, n):
                dve.tensor_scalar(dst, src, col(wcol + taps - 1), None, ALU.mult).then_inc(sem, 1)
                for d in range(1, taps):
                    dve.wait_ge(sem, n + d)
                    dve.scalar_tensor_tensor(dst[:, d:], src[:, 0:T - d], col(wcol + taps - 1 - d), dst[:, d:],
                                             ALU.mult, ALU.add).then_inc(sem, 1)

            def blocks(j):
                if j:
                    dve.wait_ge(S.a_x2h, j)
                    dve.wait_ge(S.a_x2l, j)
                src = pm[:, PA_KC + j, :].rearrange("p (n s e) -> p n s e", s=8, e=2)
                for e in range(2):
                    r = slice(e * HD, (e + 1) * HD)
                    for g in range(2):
                        dve.tensor_copy(X2[r, 8 * g:8 * g + 8, 0:NCB],
                                        src[r, g:g + NCB, :, e].rearrange("p n s -> p s n")).then_inc(S.a_x2, 1)
                dve.tensor_copy(X2[:, :, NCB], col(C_POS, 16)).then_inc(S.a_x2, 1)

            def blocks_lo(j):
                dve.wait_ge(S.a_x2h, j + 1)
                dve.tensor_tensor(X2L[j][:, :, :], X2[:, :, :], X2H[j][:, :, :].bitcast(F32), ALU.subtract).then_inc(S.a_x2l, 1)

            def conv_c(j):
                if j >= 2:
                    dve.wait_ge(S.conv_silu, j - 1)
                conv(cv[:, j % 2, :], pm[:, PC_Q + j, :], C_GDW + 4 * j, 4, S.cv, 4 * j)

            def beside(k):
                r = slice(R_F, R_F + 8)
                z = pm[r, PS, :]
                if k == 0:
                    blocks(1)
                elif k == 1:
                    blocks_lo(1)
                    dve.wait_ge(S.sm_a, 3)
                    dve.scalar_tensor_tensor(z, z, 0.0, smt[r, :], ALU.max, ALU.add).then_inc(S.sm_v, 1)
                    dve.wait_ge(S.sm_v, 3)
                    dve.tensor_scalar(smt[r, :], z, sma[r, :], -1.0, ALU.mult, ALU.mult).then_inc(S.sm_v, 1)
                    conv_c(0)
                elif k == 2:
                    dve.wait_ge(S.sm_v, 4)
                    dve.wait_ge(S.mixc_in1, 16)
                    dve.tensor_tensor_scan(z, RS[r, :], smt[r, :], 0.0, ALU.mult, ALU.add).then_inc(S.sm_v, 1)
                    conv_c(1)
                elif k == 4:
                    dve.wait_ge(S.ar_ps, 1)
                    dve.tensor_copy(AR[0:4, :], bank[7][0:4, :]).then_inc(S.sm_v, 1)
                    dve.wait_ge(S.sm_v, n_ar(1))
                    dve.tensor_tensor_scan(MR[0:4, :], AR[0:4, :], AR[0:4, :], 0.0, ALU.max, ALU.max).then_inc(S.sm_v, 1)
                    conv_c(2)
                elif k == 5:
                    conv_c(3)
                elif k == 6:
                    dve.wait_ge(S.colp, 1)
                    dve.tensor_copy(COL[:, :, :], bank[6][:, 0:TT * NCOL].rearrange("p (t c) -> p t c", t=TT)).then_inc(S.sm_v, 1)
                    conv_c(4)
                elif k == 7:
                    conv_b(0)
                elif k == 8:
                    conv_b(1)

            def conv_b(j):
                dve.wait_ge(S.b_pool, n_b_cx(2))
                conv(pm[:, PB_X + j, :], pm[:, PB_C + j, :], C_SCW + 3 * j, 3, S.b_cv, 3 * j)

            def project_mixed():
                r = slice(R_F, R_F + 8)
                z = pm[r, PS, :]
                dve.tensor_scalar(z, z, par[r, C_SMB:C_SMB + 1], cst[r, X_SG:X_SG + 1], ALU.add, ALU.mult).then_inc(S.sm_v, 1)
                dve.wait_ge(S.sm_v, 1)
                dve.scalar_tensor_tensor(smt[r, :], z, -1.0, z, ALU.mult, ALU.max).then_inc(S.sm_v, 1)
                blocks(0)
                blocks_lo(0)

                def keep(t, b):
                    dve.tensor_scalar(pm[:, t, :], bank[b][:, :], par[:, C_BIN + t:C_BIN + t + 1], None,
                                      ALU.add).then_inc(S.pm, 1)
                for k in range(8):
                    u = U_MIXED + 2 * k
                    lo(u + 2, KT, 0)
                    dve.wait_ge(S.w_used, u + 1)
                    keep(N_IN0 + k, k % 2)
                    lo(u + 3, KT, 1)
                    beside(k)
                for n in range(2):
                    lo(U_OUT + n, KT, n)
                    dve.wait_ge(S.w_used, U_LAST + n + 1)
                    keep(N_IN - 2 + n, n)
                beside(8)
                conv_c(5)

            def norm_out(n):
                tile = HEAD_NORMS[n][0]
                dve.wait_ge(S.n_rs, n + 1)
                y = pm[:, tile, :]
                if tile < PS:
                    g = C_QG if tile < PA_KS else C_KG
                    dve.scalar_tensor_tensor(y, y, col(g), bank[n % 4][:, :], ALU.mult, ALU.mult).then_inc(S.n_out, 1)
                else:
                    dve.tensor_tensor(y, y, bank[n % 4][:, :], ALU.mult).then_inc(S.n_out, 1)

            def compression():
                dve.wait_ge(S.w_used, U_LAST)
                dve.tensor_copy(HID[:, :, :], bank[5][:, 0:P].rearrange("p (a n) -> p a n", a=4)).then_inc(S.a_v, 1)
                dve.wait_ge(S.a_v, n_a_hc(1))
                dve.tensor_copy(HIC[:, :], HID[:, :, NCB]).then_inc(S.a_v, 1)
                dve.wait_ge(S.a_v, n_a_hc(2))
                dve.tensor_tensor(HID[:, :, :], HID[:, :, :], bc(HIC[:, :].unsqueeze(2), [P, 4, 32]), ALU.add).then_inc(S.a_v, 1)
                for n in range(4):
                    norm_out(n)
                dve.wait_ge(S.b_rs, 1)
                for j in range(2):
                    y = pm[:, PB_B + j, :]
                    dve.scalar_tensor_tensor(y, y, col(C_MIXB + j), bank[4][:, :], ALU.mult, ALU.mult).then_inc(S.n_out, 1)
                dve.tensor_scalar(NGC[:, :, :], COL[:, :, K_GC:K_GC + 4], -1.0, None, ALU.mult)
                dve.wait_ge(S.sm_a, n_egc(2))
                dve.tensor_tensor(BG[:, :, :], COL[:, :, K_BE:K_BE + 4], EGC[:, :, :], ALU.mult).then_inc(S.sm_v, 1)
                dve.wait_ge(S.a_he, 1)
                dve.tensor_scalar(HIE[:, :, :], HIE[:, :, :], 1.0, None, ALU.add).then_inc(S.a_v, 1)
                dve.wait_ge(S.a_v, n_a_hd(1))
                dve.reciprocal(HIE[:, :, :], HIE[:, :, :]).then_inc(S.a_v, 1)
                dve.wait_ge(S.a_v, n_a_hr(1))
                dve.tensor_tensor(HID[:, :, :], HID[:, :, :], HIE[:, :, :], ALU.mult).then_inc(S.a_v, 1)
                dve.memset(KCB[:, :, :], 0.0)
                dve.memset(VCB[:, :, :], 0.0).then_inc(S.a_v, 1)
                for n in range(4, 8):
                    norm_out(n)
                dve.wait_ge(S.a_kc, 1)
                dve.tensor_copy(KCF[:, :], bank[6][:, 0:32]).then_inc(S.a_v, 1)
                dve.wait_ge(S.a_v, n_a_kcf(1))
                dve.tensor_tensor(KCQ[:, :], KCF[:, :], KCF[:, :], ALU.mult).then_inc(S.a_v, 1)
                dve.wait_ge(S.a_kc, 2)
                dve.wait_ge(S.a_v, n_a_vcz(1))
                for h in range(H):
                    dve.tensor_copy(VCB[32 * h:32 * h + 32, h, :], bank[7][32 * h:32 * h + 32, 0:HD]).then_inc(S.a_v, 1)

            def compressed_keys():
                dve.wait_ge(S.a_kcr, 1)
                for e in range(2):
                    r = slice(e * HD, (e + 1) * HD)
                    mm = dve.scalar_tensor_tensor(KCB[r, e, :], KCF[r, :], par[r, C_KG:C_KG + 1], KCQ[r, :], ALU.mult, ALU.mult)
                mm.then_inc(S.a_v, 1)

            def head_out(n, gain, tile):
                dve.wait_ge(S.o_sq, n + 1)
                dve.tensor_reduce(HR[:, :, :], OQ[:, :, :].rearrange("p t (h d) -> p t h d", h=H), AX.X,
                                  ALU.add).then_inc(S.o_v, 1)
                dve.wait_ge(S.o_rs, n + 1)
                o = OD[:, :, :].rearrange("p t (h d) -> p (t h) d", h=H)
                dve.tensor_tensor(o, o, bc(HR[:, :, :].rearrange("p t h -> p (t h)").unsqueeze(2), [P, TT * H, HD]),
                                  ALU.mult).then_inc(S.o_v, 1)
                for j in range(2):
                    dve.wait_ge(S.o_t, 2 * n + j + 1)
                    y = pm[:, tile + j, :]
                    dve.scalar_tensor_tensor(y, bank[2 + j][:, :], col(gain), y, ALU.mult, ALU.mult).then_inc(S.o_v, 1)

            def mix_d():
                compressed_keys()
                for p in range(2):
                    dve.wait_ge(S.d_vt, p + 1)
                    dve.tensor_copy(VD[:, :, 2 * p:2 * p + 2, 0:HD],
                                    bank[4 + p][:, :].rearrange("p (t h d) -> p t h d", t=TT, h=2)).then_inc(S.d_vd, 1)

                def numden(h):
                    nd = bank[h % 2][:, 0:TT * (HD + 1)].rearrange("p (t c) -> p t c", t=TT)
                    dve.wait_ge(S.d_nd, h + 1)
                    if h:
                        dve.wait_ge(S.d_post, n_d_od(h))
                    dve.scalar_tensor_tensor(DD[:, :, 0], nd[:, :, HD], -1.0, EM[:, :, h], ALU.mult,
                                             ALU.max).then_inc(S.d_post, 1)
                    dve.wait_ge(S.d_post, n_d_dd(h + 1) - 1)
                    dve.tensor_tensor(DD[:, :, 0], nd[:, :, HD], DD[:, :, 0], ALU.max).then_inc(S.d_post, 1)
                    dve.wait_ge(S.d_post, n_d_dd(h + 1))
                    dve.reciprocal(DD[:, :, 1], DD[:, :, 0]).then_inc(S.d_post, 1)
                    dve.wait_ge(S.d_post, n_d_rc(h + 1))
                    dve.tensor_tensor(OD[:, :, h * HD:(h + 1) * HD], nd[:, :, 0:HD],
                                      bc(DD[:, :, 1:2], [P, TT, HD]), ALU.mult).then_inc(S.d_post, 1)

                def diagonal(u):
                    h, j = u // TT, u % TT
                    if u >= 2:
                        dve.wait_ge(S.d_wt, wt_count(u - 2))
                    dve.tensor_tensor(WD[:, u % 2, :], NM[h][:, j * P:(j + 1) * P], causalT, ALU.add).then_inc(S.d_wd, 1)
                dve.wait_ge(S.d_nm, H)
                dve.wait_ge(S.sm_a, n_em(1))
                diagonal(0)
                for u in range(TT * H):
                    h, j = u // TT, u % TT
                    if u + 1 < TT * H:
                        diagonal(u + 1)
                    dve.wait_ge(S.d_s, u + 1)
                    dve.wait_ge(S.d_wt, wt_count(u))
                    if h >= 2 and j == 0:
                        dve.wait_ge(S.d_nd, h - 1)
                    dve.scalar_tensor_tensor(ST_[h % 2][:, j, j * P:], bank[6 + u % 2][:, j * P:], HD ** -0.5,
                                             WT_[:, u % 2, j * P:], ALU.mult, ALU.mult).then_inc(S.d_sv, 1)
                    if h and j == TT - 1:
                        numden(h - 1)
                numden(H - 1)
                head_out(0, C_MLS, PD_O)

            def mix_c():
                v4 = lambda b: bank[b][:, :].rearrange("p (t c) -> p t c", t=TT)
                for p in range(2):
                    dve.wait_ge(S.c_kt, p + 1)
                    dve.tensor_copy(KTM[p][:, :, :], v4(p)).then_inc(S.c_v1, 1)
                for p in range(2):
                    dve.wait_ge(S.c_bp, p + 1)
                    dve.wait_ge(S.c_vt, 2)
                    dve.tensor_tensor(KBT[p][:, :], pm[:, PC_K + p, :], bank[4 + p][:, :], ALU.mult).then_inc(S.c_v1, 1)
                dve.wait_ge(S.sm_v, n_bg(1))
                dve.wait_ge(S.c_v1, n_c_ktc(2))
                dve.wait_ge(S.c_a, n_c_vtc(2))
                for p in range(2):
                    for half in range(2):
                        h = 2 * p + half
                        f = slice(half * HD, (half + 1) * HD)
                        dve.tensor_tensor(KB[p][:, :, f], KTM[p][:, :, f], bc(BG[:, :, h:h + 1], [P, TT, HD]),
                                          ALU.mult).then_inc(S.c_v1, 1)
                        dve.tensor_tensor(VB[p][:, :, f], VTM[p][:, :, f],
                                          bc(COL[:, :, K_BE + h:K_BE + h + 1], [P, TT, HD]), ALU.mult).then_inc(S.c_v1, 1)
                for h in range(H):
                    dve.wait_ge(S.c_grp, h + 1)
                    if h >= 2:
                        dve.wait_ge(S.c_a, n_c_seg(TT * (h - 1)))
                    dve.tensor_tensor(TMP[h % 2][:, :, :], v4(h), bc(causalT.unsqueeze(1), [P, TT, P]),
                                      ALU.add).then_inc(S.c_v1, 1)
                for h in range(H):
                    p, f = h // 2, slice(h % 2 * HD, (h % 2 + 1) * HD)
                    dve.wait_ge(S.c_a, n_c_seg(TT * (h + 1)))
                    dve.tensor_tensor(KD[p][:, :, f], KTM[p][:, :, f], bc(SEG[h][:, :, P - 1:P], [P, TT, HD]),
                                      ALU.mult).then_inc(S.c_v2, 1)
                    dve.wait_ge(S.c_kk, h + 1)
                    dve.tensor_tensor(NN[h][:, :, :], v4(4 + h % 2), SEG[h][:, :, :], ALU.mult).then_inc(S.c_v2, 1)
                    dve.wait_ge(S.c_kq, h + 1)
                    dve.tensor_tensor(QK[h][:, :, :], v4(6 + h % 2), SEG[h][:, :, :], ALU.mult).then_inc(S.c_v2, 1)
                dve.wait_ge(S.mixc_in0, 16)
                for h in range(H):
                    dve.wait_ge(S.c_v2, n_c_nn(h + 1))
                    dve.tensor_tensor(PP[h][:, :, :], NN[h][:, :, :], bc(LM[:, 0, :].unsqueeze(1), [P, TT, P]),
                                      ALU.mult).then_inc(S.c_v2, 1)
                    dve.wait_ge(S.c_v2, n_c_n0(h + 1))
                    dve.scalar_tensor_tensor(PP[h][:, :, :], PP[h][:, :, :], -1.0, bc(ident.unsqueeze(1), [P, TT, P]),
                                             ALU.mult, ALU.add).then_inc(S.c_v2, 1)
                def level(k, last=False):
                    for h in range(H):
                        u = 4 * k + h - 4
                        if not last:
                            dve.wait_ge(S.c_xz, u + 1)
                            dve.tensor_tensor(XX[h][:, :, :], XX[h][:, :, :], v4(4 + h % 2), ALU.subtract).then_inc(S.c_xu, 1)
                        dve.wait_ge(S.c_zp, u + 1)
                        dve.tensor_tensor(PP[h][:, :, :], PP[h][:, :, :], v4(6 + h % 2), ALU.subtract).then_inc(S.c_pu, 1)
                with dve.Fori(1, 6) as k:
                    level(k)
                level(6, True)
                for p in range(2):
                    dve.wait_ge(S.c_u, p + 1)
                    dve.tensor_copy(UU[p][:, :, :], v4(p)).then_inc(S.c_uc, 1)
                for t in range(TT):
                    if t:
                        dve.wait_ge(S.c_wp, t)
                        dve.wait_ge(S.c_sp, t)
                        dve.wait_ge(S.c_o, t)
                    else:
                        dve.wait_ge(S.c_uc, 2)
                    for p in range(2):
                        v = VN[:, 2 * p:2 * p + 2, :].rearrange("p h d -> p (h d)")
                        if t:
                            dve.tensor_tensor(v, UU[p][:, t, :], bank[4][:, p * P:(p + 1) * P],
                                              ALU.subtract).then_inc(S.c_vn, 1)
                        else:
                            dve.tensor_copy(v, UU[p][:, t, :]).then_inc(S.c_vn, 1)
                    if t < TT - 1:
                        dve.wait_ge(S.c_sp, t + 1)
                        if t:
                            dve.wait_ge(S.c_st, 4 * t)
                            dve.wait_ge(S.c_o, t + 1)
                        else:
                            dve.wait_ge(S.c_qd, 3)
                        for h in range(H):
                            r = slice(h % 2 * HD, (h % 2 + 1) * HD)
                            new, old = (SSt[r, (t + n) % 2, h // 2, r] for n in (1, 0))
                            if t:
                                dve.scalar_tensor_tensor(new, old, EGP[h // 2][r, (t + 1) * P - 1:(t + 1) * P],
                                                         bank[7][r, h * HD:(h + 1) * HD], ALU.mult, ALU.add).then_inc(S.c_st, 1)
                            else:
                                dve.tensor_copy(new, bank[7][r, h * HD:(h + 1) * HD]).then_inc(S.c_st, 1)
                head_out(1, C_GDN, PC_Z)

            def mix_a():
                dve.wait_ge(S.a_vt, 1)
                dve.tensor_copy(V6[:, :, :], bank[4][:, :].rearrange("p (t c) -> p t c", t=TT)).then_inc(S.a_v, 1)

                def compressed(i):
                    dve.wait_ge(S.a_cl, i + 1)
                    if i:
                        dve.wait_ge(S.a_ct, i)
                    dve.tensor_tensor(LC[:, :, :], cbank(i)[:, 0:P].rearrange("p (h n) -> p h n", h=H), cb[:, i, :, :],
                                      ALU.add).then_inc(S.a_cv, 1)
                    dve.wait_ge(S.a_cv, n_a_c1(i + 1))
                    if i:
                        dve.wait_ge(S.a_cv, n_a_cnm(i))
                    dve.tensor_reduce(MX[:, 0:4], LC[:, :, :], AX.X, ALU.max).then_inc(S.a_cv, 1)
                    dve.wait_ge(S.a_cv, n_a_cmx(i + 1))
                    dve.tensor_scalar(MX[:, 0:4], MX[:, 0:4], MASKED / 10, -1.0, ALU.max, ALU.mult).then_inc(S.a_cv, 1)
                    dve.wait_ge(S.a_cv, n_a_cnm(i + 1))
                    dve.tensor_tensor(LC[:, :, :], LC[:, :, :], bc(MX[:, 0:4].unsqueeze(2), [P, H, 32]), ALU.add).then_inc(S.a_cv, 1)
                    dve.wait_ge(S.a_ce, i + 1)
                    if i >= 2:
                        dve.wait_ge(S.a_yv, n_a_rc(i - 1))
                    dve.tensor_reduce(SM[:, i % 2, 0:4], LC[:, :, :], AX.X, ALU.add).then_inc(S.a_cv, 1)
                    dve.wait_ge(S.a_cv, n_a_cs(i + 1))
                    dve.tensor_scalar(SM[:, i % 2, 0:4], SM[:, i % 2, 0:4], 1e-30, None, ALU.max).then_inc(S.a_cv, 1)

                def combine(i):
                    dve.wait_ge(S.a_e, 8 * (i + 1))
                    dve.wait_ge(S.a_cv, n_a_cg(i + 1))
                    if i:
                        dve.wait_ge(S.a_yv, n_a_y(5 * i))
                    dve.reciprocal(CF[:, :], SM[:, i % 2, :]).then_inc(S.a_yv, 1)
                    dve.wait_ge(S.a_yv, n_a_rc(i + 1))
                    c = CF[:, :].rearrange("p (b h) -> p b h", b=3)
                    dve.tensor_tensor(c, c, COL[:, i, 0:12].rearrange("p (h b) -> p b h", b=3), ALU.mult).then_inc(S.a_yv, 1)
                    dve.wait_ge(S.a_yv, n_a_cf(i + 1))
                    dve.wait_ge(S.a_co, i + 1)
                    dve.wait_ge(S.a_pv, 8 * (i + 1))
                    y = YA[:, i, :].rearrange("p (h d) -> p h d", h=H)
                    v = lambda ap: ap.rearrange("p (h d) -> p h d", h=H)
                    cc = lambda b: bc(CF[:, 4 * b:4 * b + 4].unsqueeze(2), [P, H, HD])
                    dve.tensor_tensor(y, v(cbank(i)[:, 256:512]), cc(0), ALU.mult).then_inc(S.a_yv, 1)
                    for b in range(2):
                        dve.tensor_tensor(YT[:, :, :], v(bank[4][:, 256 * b:256 * (b + 1)]), cc(b + 1), ALU.mult).then_inc(S.a_yv, 1)
                        dve.wait_ge(S.a_yv, n_a_y(5 * i + 2 + 2 * b))
                        dve.tensor_tensor(y, y, YT[:, :, :], ALU.add).then_inc(S.a_yv, 1)
                        dve.wait_ge(S.a_yv, n_a_y(5 * i + 3 + 2 * b))

                for n in range(2 * TT + 1):
                    i, b = n // 2, n % 2
                    if n < 2 * TT:
                        if b == 0:
                            compressed(i)
                        w = (i + 1) * P
                        if n >= 2:
                            dve.wait_ge(S.a_t, 4 * (n - 1))
                            dve.wait_ge(S.a_e, 4 * (n - 1))
                        for h in range(H):
                            dve.wait_ge(S.a_s, 4 * n + h + 1)
                            dve.tensor_tensor_reduce(LL[b][:, h, 0:w], bank[h % 2][:, 0:w], bm[:, h, 384 - P * i:384 - P * i + w],
                                                     1.0, MASKED, ALU.add, ALU.max,
                                                     MX[:, 4 * (b + 1) + h:4 * (b + 1) + h + 1]).then_inc(S.a_l, 1)
                        dve.wait_ge(S.a_l, 4 * (n + 1))
                        m = MX[:, 4 * (b + 1):4 * (b + 2)]
                        dve.tensor_scalar(m, m, -1.0, None, ALU.mult).then_inc(S.a_nm, 1)
                    if b == 0 and n:
                        combine(i - 1)
                dve.wait_ge(S.o_sq, 3)
                dve.tensor_reduce(HR[:, 0, :], YQ[:, :, :], AX.X, ALU.add).then_inc(S.o_v, 1)
                dve.wait_ge(S.o_rs, 3)
                dve.tensor_tensor(YA[:, :, :], YA[:, :, :], bc(HR[:, 0, :].unsqueeze(2), [P, TT, H * HD]),
                                  ALU.mult).then_inc(S.o_v, 1)
                for j in range(2):
                    dve.wait_ge(S.o_t, 4 + j + 1)
                    dve.tensor_scalar(pm[:, j, :], bank[2 + j][:, :], col(C_MIXA + j), None, ALU.mult).then_inc(S.o_v, 1)

            def mix_out():
                for k, tile in enumerate(Y_TILES):
                    dve.wait_ge(S.y_hi, k + 1)
                    dve.tensor_tensor(hL[:, k, :], pm[:, tile, :], hH[:, k, :].bitcast(F32), ALU.subtract).then_inc(S.y_lo, 1)

            def scaled(s, done):
                dve.scalar_tensor_tensor(modA[:, s * KT:(s + 1) * KT], mod[:, (3 * s + 1) * KT:(3 * s + 2) * KT], 1.0,
                                         col(C_NORM + s * KT, KT), ALU.add, ALU.mult).then_inc(S.mod_set, 1)
                if s < 2:
                    set_gate(s)
                dve.wait_ge(S.mod_set, done + (2 if s < 2 else 1))

            def set_gate(s):
                dve.tensor_scalar(gate[:, s * KT:(s + 1) * KT], mod[:, (3 * s + 2) * KT:(3 * s + 3) * KT],
                                  1.0 if s == 1 else 0.5, None, ALU.mult).then_inc(S.mod_set, 1)

            def layer1(l):
                dve.wait_ge(S.par_in, 16)
                dve.tensor_tensor(mod[:, 0:N_NEXT], mod[:, NMOD:NMOD + N_NEXT], col(C_ADAB, N_NEXT), ALU.add).then_inc(S.mod_set, 1)
                dve.wait_ge(S.mod_set, 1)
                scaled(0, 1)
                lo(0, KT, 0)
                norm(0, 0)
                lo(1, KT, 1)
                up(U_UP1, 0, KH, ADA1, 0)
                c = slice(N_NEXT, 8 * KT)
                dve.tensor_tensor(mod[:, c], mod[:, c], par[:, C_ADAB + N_NEXT:C_ADAB + 8 * KT], ALU.add).then_inc(S.mod_set, 1)
                down(U_DN1, 0, KT)
                scaled(1, 4)
                norm(1, 1)
                project_in(U_IN, N_IN0, C_BIN, KT)
                project_mixed()
                compression()
                mix_d()
                mix_c()
                mix_a()
                mix_out()
                project_out(U_OUT, 1, KT)
                scaled(2, 6)
                norm(2, 2)
                up(U_UP2, FT, KH, ADA2, ADA1)
                c = slice(8 * KT, NMOD)
                dve.tensor_tensor(mod[:, c], mod[:, c], par[:, C_ADAB + 8 * KT:C_ADAB + NMOD], ALU.add).then_inc(S.mod_set, 1)
                dve.wait_ge(S.mod_set, 8)
                set_gate(2)
                dve.wait_ge(S.mod_set, 9)
                down(U_DN2, 2, 0)

            with dve.Fori(0, L) as l:
                layer1(l)
                end_layer(dve, l)

            chain = [0]

            def step(mm):
                mm.then_inc(S.trig_v, 1)
                chain[0] += 1
                dve.wait_ge(S.trig_v, chain[0])
            dve.wait_ge(S.pos_in, 16)
            step(dve.memset(CMASK[:, 0:384], 0.0))
            step(dve.tensor_copy(CMASK[:, 384:512], causal))
            step(dve.tensor_copy(TRN[:, :], POSI[:, :]))
            step(dve.tensor_scalar(ANG[:, :], TRN[:, :], cst[:, X_IF:X_IF + 1], None, ALU.mult))
            for q in range(2):
                step(dve.tensor_scalar(TRN[:, :], ANG[:, :], 0.5 / np.pi, 0.25 * q, ALU.mult, ALU.add))
                step(dve.tensor_scalar(TRN[:, :], TRN[:, :], ROUND, None, ALU.add))
                step(dve.tensor_scalar(TRN[:, :], TRN[:, :], ROUND, None, ALU.subtract))
                r = RED[q][:, :]
                step(dve.scalar_tensor_tensor(r, TRN[:, :], -TURN[0], ANG[:, :], ALU.mult, ALU.add))
                step(dve.scalar_tensor_tensor(r, TRN[:, :], -TURN[1], r, ALU.mult, ALU.add))
                step(dve.scalar_tensor_tensor(r, TRN[:, :], -TURN[2], r, ALU.mult, ALU.add))
                step(dve.tensor_scalar(r, r, 0.5 * np.pi * q, None, ALU.add))
                step(dve.tensor_scalar(r, r, 3.1415925, -3.1415925, ALU.min, ALU.max))
                if q == 0:
                    step(dve.memset(mod[:, :], 0.0))
                    step(dve.memset(gate[:, :], 1.0))
            assert chain[0] == 22

            def beside2(k):
                if k == 0:
                    r = slice(0, HD)
                    dve.tensor_tensor(LQ[r, :], par[r, E_LAM:E_LAM + 2], par[r, E_LAM + 2:E_LAM + 4], ALU.mult).then_inc(S.lam_v, 1)
                if 3 <= k < 11:
                    c = k - 3
                    dve.wait_ge(S.rot_ps, c + 1)
                    dve.tensor_tensor(RTM[c % 2][:, :], bank[6 + c % 2][:, :], SIN[:, :], ALU.mult).then_inc(S.rot_sin, 1)
                    dve.wait_ge(S.rot_sin, c + 1)
                    dve.wait_ge(S.rot_cos, c + 1)
                    y = pm[:, QQ + c, :]
                    dve.tensor_tensor(y, y, RTM[c % 2][:, :], ALU.add).then_inc(S.rot_x, 1)
                if k == 5:
                    dve.wait_ge(S.lam_e, 1)
                    dve.scalar_tensor_tensor(NL[:, :], LE[:, 0:1], -1.0, LE[:, 1:2], ALU.mult, ALU.add).then_inc(S.lam_v, 1)
                    dve.wait_ge(S.lam_v, 2)
                    dve.tensor_tensor(NL[:, :], NL[:, :], par[:, E_LIN:E_LIN + 1], ALU.subtract).then_inc(S.lam_v, 1)
                    for g in range(4):
                        dve.wait_ge(S.n_rs, g + 1)
                        y = pm[:, QV + g, :]
                        dve.scalar_tensor_tensor(y, y, col(E_SGU + g), bank[2 + g][:, :], ALU.mult, ALU.mult).then_inc(S.n_out, 1)
                if k in (9, 10):
                    for g in (2 * k - 18, 2 * k - 17):
                        dve.wait_ge(S.bs_in, 16)
                        dve.wait_ge(S.mixed, g + 1)
                        dve.tensor_tensor(SGT[g % 2][:, :, :], bank[2 + g][:, :].rearrange("p (t c) -> p t c", t=TT),
                                          bc(BS[:, g:g + 1, :], [P, TT, P]), ALU.add).then_inc(S.mix_b, 1)
                        dve.wait_ge(S.mix_b, g + 1)
                        y = pm[:, QU + g, :].rearrange("p (t c) -> p t c", t=TT)
                        dve.tensor_tensor(y, y, SGT[g % 2][:, :, :], ALU.mult).then_inc(S.mix_y, 1)

            def project2():
                for k in range(N_IN2 - N_IN0_2):
                    u = V_IN + N_IN0_2 + k
                    lo(u + 2, KT, k % 2)
                    dve.wait_ge(S.w_used, u + 1)
                    dve.tensor_copy(pm[:, u, :], bank[k % 2][:, :]).then_inc(S.pm, 1)
                    beside2(k)

            def y_lo(k):
                dve.wait_ge(S.y_hi, k + 1)
                dve.tensor_tensor(hL[:, k, :], pm[:, Y2_TILES[k], :], hH[:, k, :].bitcast(F32), ALU.subtract).then_inc(S.y_lo, 1)

            def head_sum(h):
                dve.wait_ge(S.o_sq, h + 1)
                dve.tensor_reduce(HR2[:, :, h], YDQ[:, :, h * P:(h + 1) * P], AX.X, ALU.add).then_inc(S.o_v, 1)

            def mix2():
                for k in range(4):
                    y_lo(k)
                for n in range(18):
                    if 1 <= n < 17:
                        u = n - 1
                        i, b = u % TT, u % 2
                        w = (i + 1) * P
                        dve.wait_ge(S.s_exp, 2 * u + 2)
                        if u >= 2:
                            dve.wait_ge(S.s_y, u - 1)
                        dve.reciprocal(RC2[:, b, :], SM2[:, b, :]).then_inc(S.s_small, 1)
                        dve.wait_ge(S.s_small, 2 * u + 1)
                        dve.scalar_tensor_tensor(RT2[:, b, :], RC2[:, b, 1:2], NL[:, 0:1], SM2[:, b, 0:1], ALU.mult,
                                                 ALU.mult).then_inc(S.s_small, 1)
                        dve.wait_ge(S.s_small, 2 * u + 2)
                        if u >= 2:
                            dve.wait_ge(S.s_t, u - 1)
                        dve.scalar_tensor_tensor(AD[b][:, 0:w], LG[b][:, 1, 0:w], RT2[:, b, :], LG[b][:, 0, 0:w], ALU.mult,
                                                 ALU.add).then_inc(S.s_diff, 1)
                    if n < 16:
                        i, b = n % TT, n % 2
                        w = (i + 1) * P
                        for m in range(2):
                            dve.wait_ge(S.s_ps, 2 * n + m + 1)
                            if n >= 2:
                                dve.wait_ge(S.s_diff, n - 1)
                            dve.tensor_tensor_reduce(LG[b][:, m, 0:w], bank[2 * b + m][:, 0:w],
                                                     CMASK[:, 384 - P * i:384 - P * i + w], 1.0, MASKED, ALU.add, ALU.max,
                                                     MX2[:, b, m:m + 1]).then_inc(S.s_max, 1)
                        dve.wait_ge(S.s_max, 2 * n + 2)
                        dve.tensor_scalar(NX2[:, b, :], MX2[:, b, :], -HD ** -0.5, None, ALU.mult).then_inc(S.s_neg, 1)
                    if n >= 2:
                        v = n - 2
                        h, i = v // TT, v % TT
                        dve.wait_ge(S.s_val, v + 1)
                        dve.tensor_scalar(YD[:, i, h * P:(h + 1) * P], bank[6 + v % 2][:, 0:P], RC2[:, v % 2, 0:1], None,
                                          ALU.mult).then_inc(S.s_y, 1)
                    if n in (8, 12, 16):
                        head_sum(n // 4 - 2)
                head_sum(3)
                dve.wait_ge(S.o_rs, 1)
                for h in range(4):
                    o = YD[:, :, h * P:(h + 1) * P]
                    dve.tensor_tensor(o, o, bc(HR2[:, :, h:h + 1], [P, TT, P]), ALU.mult).then_inc(S.o_v, 1)
                for h in range(4):
                    dve.wait_ge(S.o_t, h + 1)
                    dve.tensor_scalar(pm[:, QY + h, :], bank[2 + h][:, :], col(E_SUB), col(E_LIN + 1), ALU.mult,
                                      ALU.mult).then_inc(S.o_v, 1)
                    if h:
                        y_lo(3 + h)
                y_lo(KT - 1)

            def up2(ubase, next_tiles):
                def taps(i, half):
                    dve.wait_ge(S.f_tap, 2 * i + half + 1)
                    for d in (1, 2):
                        y = xn[:, half, d:]
                        dve.scalar_tensor_tensor(y, bank[half][:, 0:T - d], par[:, bass.ds(E_CW + 3 * (i + FT * half) + 2 - d, 1)],
                                                 y, ALU.mult, ALU.add).then_inc(S.f_conv, 1)
                        dve.wait_ge(S.f_conv, 4 * i + 2 * half + d)

                def turn(i, tiles):
                    lo(ubase + 2 * i + 2, tiles, 0)
                    taps(i, 0)
                    taps(i, 1)
                    dve.wait_ge(S.sil, i + 1)
                    dve.tensor_tensor(gf[:, :], xn[:, 1, :], sil[:, :], ALU.mult).then_inc(S.g_mul, 1)
                    lo(ubase + 2 * i + 3, tiles, 1)
                    dve.wait_ge(S.g_mul, i + 1)
                    dve.tensor_copy(gH[:, i, :], gf[:, :]).then_inc(S.g_hi, 1)
                    dve.wait_ge(S.g_hi, i + 1)
                    dve.tensor_tensor(gL[:, i, :], gf[:, :], gH[:, i, :].bitcast(F32), ALU.subtract).then_inc(S.g_lo, 1)
                with dve.Fori(0, FT - 1) as i:
                    turn(i, KT)
                turn(FT - 1, next_tiles)

            def layer2(l):
                dve.wait_ge(S.par_in, 16)
                dve.tensor_copy(modA[:, 0:2 * KT], par[:, E_NORM:E_NORM + 2 * KT]).then_inc(S.mod_set, 1)
                lo(0, KT, 0)
                dve.wait_ge(S.mod_set, 1)
                norm(0, 0)
                lo(1, KT, 1)
                project_in(V_IN, N_IN0_2, None, KT)
                project2()
                mix2()
                project_out(V_OUT, 0, KT)
                norm(1, 1)
                up2(V_UP, KH)
                down(V_DN, 1, 0)

            with dve.Fori(0, L) as l:
                layer2(l)
                end_layer(dve, l + L)

            dve.wait_ge(S.rstd, 1)
            for k in range(KT):
                dve.scalar_tensor_tensor(xT[:, k, :], xT[:, k, :], col(E_FIN + k), rstd[:, :], ALU.mult,
                                         ALU.mult).then_inc(S.x_new, 1)
            for t in range(TT):
                for k in range(KT):
                    n = t * KT + k
                    dve.wait_ge(S.x_turned, KT + n + 1)
                    dve.tensor_copy(xin[:, t, k * P:(k + 1) * P], bank[n % 4][:, 0:P]).then_inc(S.fin, 1)

        @block.gpsimd
        def _(pool):
            pool.wait_ge(S.x_copied, KT)

            def square_sum(xbase, n, chain=S.pool, done=S.sumsq):
                c = (2 * KT - 3) * n
                for m in range(KT - 1):
                    if xbase is not None:
                        pool.wait_ge(S.x_new, xbase + m + 1)
                    dst = rstd if m else sumsq
                    pool.tensor_tensor(dst[:, :], xT[:, m, :], xT[:, m, :], ALU.mult).then_inc(chain, 1)
                    if m:
                        pool.wait_ge(chain, c + 2 * m)
                        pool.tensor_tensor(sumsq[:, :], sumsq[:, :], rstd[:, :], ALU.add).then_inc(chain, 1)
                        pool.wait_ge(chain, c + 2 * m + 1)
                pool.sem_inc(done, 1)

            def mix_b():
                pool.wait_ge(S.pm, N_IN0)
                for j in range(2):
                    y = pm[:, PB_C + j, :]
                    pool.tensor_tensor(y, y, pm[:, PB_X + j, :], ALU.mult).then_inc(S.b_pool, 1)
                squares(0)
                for j in range(2):
                    pool.wait_ge(S.b_cv, 3 * (j + 1))
                    y = pm[:, PB_B + j, :]
                    pool.tensor_tensor(y, y, pm[:, PB_X + j, :], ALU.mult).then_inc(S.b_pool, 1)
                    pool.wait_ge(S.b_pool, n_b_y(j + 1))
                    pool.tensor_tensor(pm[:, PB_C + j, :], y, y, ALU.mult).then_inc(S.b_pool, 1)

            def squares(first):
                if first:
                    pool.wait_ge(S.conv_silu, 6)
                for n in range(first, first + 4):
                    if n >= 2:
                        pool.wait_ge(S.n_ss, n - 1)
                    tile = HEAD_NORMS[n][0]
                    pool.tensor_tensor(nsq[:, n % 2, :], pm[:, tile, :], pm[:, tile, :], ALU.mult).then_inc(S.n_sq, 1)

            def head_out(n, ready, count):
                pool.wait_ge(ready, count)
                pool.tensor_tensor(OQ[:, :, :], OD[:, :, :], OD[:, :, :], ALU.mult).then_inc(S.o_sq, 1)

            def mix_c():
                pool.wait_ge(S.c_a, n_c_egp(2))
                pool.wait_ge(S.c_kq, H)
                for p in range(2):
                    y = pm[:, PC_Q + p, :]
                    pool.tensor_tensor(y, y, EGP[p][:, :], ALU.mult).then_inc(S.c_qd, 1)
                pool.memset(SSt[:, :, :, :], 0.0).then_inc(S.c_qd, 1)

                def level(k):
                    for h in range(H):
                        u = 4 * k + h - 4
                        if u >= 2:
                            pool.wait_ge(S.c_z, u - 1)
                        pool.tensor_tensor(NK[h % 2][:, :, :], NN[h][:, :, :],
                                           bc(LM[:, k:k + 1, :], [P, TT, P]), ALU.mult).then_inc(S.c_nk, 1)
                pool.wait_ge(S.c_a, n_c_seg(TT * H))
                pool.wait_ge(S.c_v2, n_c_nn(H))
                for k in range(1, 7):
                    level(k)

            def mix_a():
                pool.wait_ge(S.a_yv, n_a_y(5 * TT))
                pool.tensor_tensor(YQ[:, :, :], YA[:, :, :], YA[:, :, :], ALU.mult).then_inc(S.o_sq, 1)

            def layer1(l):
                square_sum(0, 0)
                mix_b()
                squares(4)
                pool.memset(VD[:, :, :, HD:HD + 1], 1.0).then_inc(S.d_one, 1)
                head_out(0, S.d_post, n_d_od(H))
                mix_c()
                head_out(1, S.c_od, TT)
                mix_a()
                square_sum(KT, 1)
                square_sum(2 * KT, 2)

            square_sum(None, 0, S.first_sq, S.first_sums)

            with pool.Fori(0, L) as l:
                layer1(l)
                end_layer(pool, l)

            pool.wait_ge(S.trig_a, 2)

            def layer2(l):
                pool.wait_ge(S.ws_in, 16)
                pool.tensor_tensor(WS[:, :, :], WS[:, :, :], bc(tri.unsqueeze(1), [P, 4, P]), ALU.mult).then_inc(S.ws_set, 1)
                for g in range(4):
                    pool.wait_ge(S.gelu, g + 1)
                    pool.tensor_tensor(SQ2[g], pm[:, QV + g, :], pm[:, QV + g, :], ALU.mult).then_inc(S.n_sq, 1)
                for c in range(8):
                    pool.wait_ge(S.rot_ps, c + 1)
                    y = pm[:, QQ + c, :]
                    pool.tensor_tensor(y, y, COS[:, :], ALU.mult).then_inc(S.rot_cos, 1)
                for h in range(4):
                    pool.wait_ge(S.s_y, 4 * h + 4)
                    o = YD[:, :, h * P:(h + 1) * P]
                    pool.tensor_tensor(YDQ[:, :, h * P:(h + 1) * P], o, o, ALU.mult).then_inc(S.o_sq, 1)
                square_sum(0, 0)
                square_sum(KT, 1)

            with pool.Fori(0, L) as l:
                layer2(l)
                end_layer(pool, l + L)

        @block.tensor
        def _(pe):
            pe.wait_ge(S.const_in, 32)
            pe.wait_ge(S.x_in, 16)
            for k in range(KT):
                for t in range(TT):
                    mm = pe.transpose(bank[k][:, t * P:(t + 1) * P], xin[:, t, k * P:(k + 1) * P], ident)
                mm.then_inc(S.x_turned, 1)
            pe.wait_ge(S.tab_in, 64)
            pe.wait_ge(S.x_copied, KT)
            pe.matmul(bank[0][0:H, :], tab[:, :], OHR[:, 0:512], start=True, stop=True)
            pe.matmul(bank[1][0:H, 0:P], tab[:, :], OHR[:, 512:640], start=True, stop=True)
            for b, c, w in ((2, 0, 512), (3, 512, 512), (4, 1024, 32)):
                mm = pe.matmul(bank[b][0:H, 0:w], tab[:, :], OHF[:, c:c + w], start=True, stop=True)
            mm.then_inc(S.bias_ps, 1)
            pe.wait_ge(S.skew_in, 32)
            pe.wait_ge(S.bias_sb, 1)
            for h in range(H):
                pe.matmul(bank[4 + h][:, :], FLIP[:, :], SKEW[:, h, :], start=True, stop=True).then_inc(S.bm_ps, 1)
            pe.wait_ge(S.bm_set, H)
            pe.wait_ge(S.cb_set, 1)
            pe.wait_ge(S.first_sums, 2)

            def products(o, n, tiles, rH, rL, k0, start, stop, ready=None):
                for k in range(tiles):
                    if ready:
                        pe.wait_ge(ready[0], ready[1] + k + 1)
                    r = k0 + k
                    pe.matmul(o, wH[n][:, k, :], rH[:, r, :], start=start and k == 0, stop=False)
                    pe.matmul(o, wL[n][:, k, :], rH[:, r, :], start=False, stop=False)
                    mm = pe.matmul(o, wH[n][:, k, :], rL[:, r, :], start=False, stop=stop and k == tiles - 1)
                mm.then_inc(S.w_used, 1)

            def up(ubase, gbase, ready):
                def turn(i, ready=None):
                    pe.wait_ge(S.w_lo, ubase + 2 * i + 1)
                    if gbase or later(i):
                        pe.wait_ge(S.sil, gbase + i)
                    products(bank[0][:, :], 0, KT, hH, hL, 0, True, True, ready)
                    pe.wait_ge(S.w_lo, ubase + 2 * i + 2)
                    if gbase or later(i):
                        pe.wait_ge(S.g_mul, gbase + i)
                    products(bank[1][:, :], 1, KT, hH, hL, 0, True, True)
                turn(0, ready)
                with pe.Fori(1, FT) as i:
                    turn(i)

            def down(ubase, xbase, gdone):
                pe.wait_ge(S.g_lo, gdone)

                def tile(m, b):
                    for n in range(2):
                        pe.wait_ge(S.w_lo, ubase + 2 * m + n + 1)
                        if n == 0 and (xbase or not isinstance(m, int)):
                            pe.wait_ge(S.x_new, xbase + m - 1)
                        products(bank[b][:, :], n, KH, gH, gL, n * KH, n == 0, n == 1)
                for n in range(2):
                    tile(n, 2 + n)
                with pe.Fori(1, KT // 2) as j:
                    for n in range(2):
                        tile(2 * j + n, 2 + n)

            def project(ubase, pairs, out_sem, obase, ready):
                def turn(i, ready=None):
                    for n in range(2):
                        pe.wait_ge(S.w_lo, ubase + 2 * i + n + 1)
                        if later(i):
                            pe.wait_ge(out_sem, obase + 2 * i + n - 1)
                        products(bank[n][:, :], n, KT, hH, hL, 0, True, True, None if n else ready)
                turn(0, ready)
                with pe.Fori(1, pairs) as i:
                    turn(i)

            def mean_square(n):
                if n:
                    pe.wait_ge(S.sumsq, n)
                pe.matmul(bank[6][:, :], ones, sumsq[:, :], start=True, stop=False)
                if n:
                    pe.wait_ge(S.last_sq, n)
                pe.matmul(bank[6][:, :], ones, sqt[:, :], start=False, stop=True).then_inc(S.ms, 1)

            def beside(k):
                if k == 4:
                    pe.wait_ge(S.g_sig, 2)
                    pe.wait_ge(S.sm_v, 5)
                    pe.matmul(bank[7][0:4, :], cst[:, X_SA:X_SA + 4], pm[:, PS, :], start=True, stop=True).then_inc(S.ar_ps, 1)
                elif k == 6:
                    pe.wait_ge(S.sm_v, n_mr(1))
                    for t in range(TT):
                        c = bank[6][:, t * NCOL:(t + 1) * NCOL]
                        pe.matmul(c, pm[:, PS, t * P:(t + 1) * P], cst[:, X_CS:X_CS + NCOL], start=True, stop=False)
                        mm = pe.matmul(c, MR[0:4, t * P:(t + 1) * P], cst[0:4, X_MS:X_MS + NCOL], start=False, stop=True)
                    mm.then_inc(S.colp, 1)

            def project_mixed():
                for k in range(8):
                    u = U_MIXED + 2 * k
                    pe.wait_ge(S.w_lo, u + 1)
                    pe.wait_ge(S.pm, N_IN0 + k - 1)
                    products(bank[k % 2][:, :], 0, KT, hH, hL, 0, True, True)
                    beside(k)
                    kv, hd, g = k // 4, k // 2 % 2, k % 2
                    pe.wait_ge(S.w_lo, u + 2)
                    pe.wait_ge(S.a_x2l, kv + 1)
                    products(bank[5][:, (2 * kv + hd) * 32:(2 * kv + hd + 1) * 32], 1, KT, X2H[kv], X2L[kv], g * KT,
                             g == 0, g == 1)
                for n in range(2):
                    pe.wait_ge(S.w_lo, U_LAST + n + 1)
                    pe.wait_ge(S.pm, N_IN - 3 + n)
                    products(bank[n][:, :], n, KT, hH, hL, 0, True, True)

            def head_sums(first):
                for n in range(first, first + 4):
                    pe.wait_ge(S.n_sq, n + 1)
                    if n == 0:
                        pe.wait_ge(S.pm, N_IN)
                    elif first:
                        pe.wait_ge(S.n_out, n - 3)
                    pe.matmul(bank[n % 4][:, :], heads, nsq[:, n % 2, :], start=True, stop=True).then_inc(S.n_ss, 1)

            def norms():
                head_sums(0)
                for j in range(2):
                    pe.wait_ge(S.b_pool, n_b_sq(j + 1))
                    mm = pe.matmul(bank[4][:, :], ones, pm[:, PB_C + j, :], start=j == 0, stop=j == 1)
                mm.then_inc(S.b_ss, 1)
                head_sums(4)
                pe.wait_ge(S.a_v, n_a_hid(1))
                pe.wait_ge(S.mixc_in2, 16)
                pe.wait_ge(S.mixc_in3, 16)
                for hd in range(2):
                    mm = pe.matmul(bank[6][:, 0:32], w2k[:, hd, :], HID[:, hd, :], start=hd == 0, stop=hd == 1)
                mm.then_inc(S.a_kc, 1)
                for h in range(H):
                    for hd in range(2):
                        mm = pe.matmul(bank[7][32 * h:32 * h + 32, 0:HD], HID[:, 2 + hd, :], w2v[:, hd, :],
                                       start=hd == 0, stop=hd == 1)
                mm.then_inc(S.a_kc, 1)
                pe.wait_ge(S.a_v, n_a_kcq(1))
                pe.matmul(bank[6][:, 32:64], heads, KCQ[:, :], start=True, stop=True).then_inc(S.a_kcs, 1)

            def turn_tiles(b, src, sem):
                for t in range(TT):
                    mm = pe.transpose(bank[b][:, t * P:(t + 1) * P], src(t), ident)
                mm.then_inc(sem, 1)

            def head_out(n, src=None):
                pe.wait_ge(S.o_v, n_o_nrm(n + 1))
                for j in range(2):
                    turn_tiles(2 + j, lambda t: (src or OD)[:, t, j * P:(j + 1) * P], S.o_t)

            def half(h):
                return slice(h % 2 * HD, (h % 2 + 1) * HD)

            def mix_d():
                pe.wait_ge(S.n_rs, len(HEAD_NORMS))
                for h in range(H):
                    pe.matmul(bank[h][:, :], bc(ident[0:4, h:h + 1], [4, P]), MR[0:4, :], start=True, stop=True).then_inc(S.d_nmp, 1)
                for p in range(2):
                    turn_tiles(4 + p, lambda t: pm[:, PD_V + p, t * P:(t + 1) * P], S.d_vt)

                def numden(h):
                    pe.wait_ge(S.d_sv, TT * (h + 1))
                    if h == 0:
                        pe.wait_ge(S.d_nm, 2)
                        pe.wait_ge(S.d_vd, 2)
                        pe.wait_ge(S.d_one, 1)
                    if h >= 2:
                        pe.wait_ge(S.d_post, n_d_od(h - 1))
                    for i in range(TT):
                        for j in range(i + 1):
                            mm = pe.matmul(bank[h % 2][:, i * (HD + 1):(i + 1) * (HD + 1)], ST_[h % 2][:, j, i * P:(i + 1) * P],
                                           VD[:, j, h, :], start=j == 0, stop=j == i)
                    mm.then_inc(S.d_nd, 1)
                pe.wait_ge(S.a_kcr, 1)
                pe.wait_ge(S.a_v, n_a_vcb(H))
                for h in range(H):
                    for j in range(TT):
                        u = TT * h + j
                        if u >= 2:
                            pe.wait_ge(S.d_sv, u - 1)
                        pe.matmul(bank[6 + u % 2][:, j * P:], pm[half(h), PD_K + h // 2, j * P:(j + 1) * P],
                                  pm[half(h), PD_Q + h // 2, j * P:], start=True, stop=True).then_inc(S.d_s, 1)
                    if h:
                        numden(h - 1)
                numden(H - 1)
                head_out(0)

            def mix_c():
                pe.wait_ge(S.o_v, n_o_y(2))
                pe.wait_ge(S.n_out, len(HEAD_NORMS))
                for p in range(2):
                    turn_tiles(p, lambda t: pm[:, PC_K + p, t * P:(t + 1) * P], S.c_kt)
                for p in range(2):
                    turn_tiles(2 + p, lambda t: pm[:, PC_V + p, t * P:(t + 1) * P], S.c_vt)
                for p in range(2):
                    r = R_BE + 2 * p
                    for e in range(2):
                        mm = pe.matmul(bank[4 + p][half(e), :], bc(ident[:, r + e:r + e + 1], [P, HD]), pm[:, PS, :],
                                       start=True, stop=True)
                    mm.then_inc(S.c_bp, 1)
                for p in range(2):
                    r = R_AL + 2 * p
                    for e in range(2):
                        mm = pe.matmul(bank[6 + p][half(e), :], bc(ident[:, r + e:r + e + 1], [P, HD]), pm[:, PS, :],
                                       start=True, stop=True)
                    mm.then_inc(S.c_gp, 1)
                pe.wait_ge(S.c_v1, n_c_ktc(2))
                pe.wait_ge(S.c_a, n_c_vtc(2))
                for h in range(H):
                    pe.matmul(bank[h][:, :], bc(ident[:, R_AL + h:R_AL + h + 1], [P, P]), pm[:, PS, :], start=True,
                              stop=True).then_inc(S.c_grp, 1)
                pe.wait_ge(S.c_v1, n_c_kbt(2))
                pe.wait_ge(S.c_a, n_c_egp(2))
                for h in range(H):
                    if h >= 2:
                        pe.wait_ge(S.c_v2, n_c_nn(h - 1))
                        pe.wait_ge(S.c_v2, n_c_qk(h - 1))
                    for b, r, sem in ((4, KBT[h // 2][half(h), :], S.c_kk), (6, pm[half(h), PC_Q + h // 2, :], S.c_kq)):
                        for t in range(TT):
                            mm = pe.matmul(bank[b + h % 2][:, t * P:(t + 1) * P],
                                           pm[half(h), PC_K + h // 2, t * P:(t + 1) * P], r[:, t * P:(t + 1) * P],
                                           start=True, stop=True)
                        mm.then_inc(sem, 1)
                for h in range(H):
                    pe.wait_ge(S.c_v2, n_c_p0(h + 1))
                    pe.wait_ge(S.c_v1, n_c_tmp(H))
                    turn_tiles(h, lambda t: PP[h][:, t, :], S.c_xt)
                pe.wait_ge(S.c_a, n_c_x0(H))
                pe.wait_ge(S.c_v2, n_c_nn(H))
                pe.wait_ge(S.c_v2, n_c_qk(H))
                def square(k, h, last):
                    u = 4 * k + h - 4
                    pe.wait_ge(S.c_zc, u + 1)
                    if later(k - 1) or h >= 2:
                        pe.wait_ge(S.c_pu, u - 1)
                    if not last:
                        for t in range(TT):
                            mm = pe.matmul(bank[4 + h % 2][:, t * P:(t + 1) * P], PP[h][:, t, :], ZZ[h][:, t, :], start=True,
                                           stop=True)
                        mm.then_inc(S.c_xz, 1)
                    for t in range(TT):
                        mm = pe.matmul(bank[6 + h % 2][:, t * P:(t + 1) * P], ZZ[h][:, t, :], PP[h][:, t, :], start=True, stop=True)
                    mm.then_inc(S.c_zp, 1)

                def level(k, last=False):
                    for h in range(H):
                        pe.wait_ge(S.c_nk, 4 * k + h - 3)
                        if later(k - 1):
                            pe.wait_ge(S.c_xu, 4 * k + h - 7)
                        for t in range(TT):
                            mm = pe.matmul(bank[h][:, t * P:(t + 1) * P], NK[h % 2][:, t, :], XX[h][:, t, :], start=True, stop=True)
                        mm.then_inc(S.c_z, 1)
                        if h:
                            square(k, h - 1, last)
                    square(k, H - 1, last)
                level(1)
                with pe.Fori(2, 6) as k:
                    level(k)
                level(6, True)

            def mix_c_scan():
                pe.wait_ge(S.c_pu, 24)
                pe.wait_ge(S.c_v1, n_c_kb(H))
                pe.wait_ge(S.c_v1, n_c_vb(H))
                for p in range(2):
                    for t in range(TT):
                        for h in (2 * p, 2 * p + 1):
                            mm = pe.matmul(bank[p][:, t * P + h % 2 * HD:t * P + (h % 2 + 1) * HD], PP[h][:, t, :],
                                           VB[p][:, t, half(h)], start=True, stop=True)
                    mm.then_inc(S.c_u, 1)
                for p in range(2):
                    for t in range(TT):
                        for h in (2 * p, 2 * p + 1):
                            mm = pe.matmul(bank[2 + p][half(h), t * P:(t + 1) * P], KB[p][:, t, half(h)], PP[h][:, t, :],
                                           start=True, stop=True)
                    mm.then_inc(S.c_w, 1)
                pe.wait_ge(S.c_wc, 2)
                pe.wait_ge(S.c_qd, 2)
                pe.wait_ge(S.c_v2, n_c_kd(H))
                for t in range(TT):
                    c = slice(t * P, (t + 1) * P)
                    if t:
                        pe.wait_ge(S.c_st, 4 * t)
                        for p in range(2):
                            mm = pe.matmul(bank[4][:, p * P:(p + 1) * P], WW[p][:, c], SSt[:, t % 2, p, :], start=True, stop=True)
                        mm.then_inc(S.c_wp, 1)
                    if t >= 2:
                        pe.wait_ge(S.c_od, t - 1)
                    pe.wait_ge(S.c_vn, 2 * (t + 1))
                    for h in range(H):
                        o = bank[5 + t % 2][:, h * HD:(h + 1) * HD]
                        if t and h % 2 == 0:
                            pe.matmul(bank[5 + t % 2][:, h * HD:(h + 2) * HD], pm[:, PC_Q + h // 2, c], SSt[:, t % 2, h // 2, :],
                                      start=True, stop=False)
                        mm = pe.matmul(o, QK[h][:, t, :], VN[:, h, :], start=t == 0, stop=t == 0 or h % 2 == 1)
                    mm.then_inc(S.c_o, 1)
                    if t < TT - 1:
                        for h in range(H):
                            mm = pe.matmul(bank[7][half(h), h * HD:(h + 1) * HD], KD[h // 2][:, t, half(h)],
                                           VN[:, h, :], start=True, stop=True)
                        mm.then_inc(S.c_sp, 1)
                head_out(1)

            def mix_a():
                pe.wait_ge(S.c_od, TT)
                turn_tiles(4, lambda t: pm[:, PA_VSW, t * P:(t + 1) * P], S.a_vt)
                pe.wait_ge(S.a_v, n_a_kcn(1))
                pe.wait_ge(S.a_v, n_a_vcb(H))
                pe.wait_ge(S.a_v, n_a_v6(1))
                q = lambda h, i: pm[half(h), PA_Q + h // 2, i * P:(i + 1) * P]
                for n in range(2 * TT + 1):
                    i, b = n // 2, n % 2
                    if n < 2 * TT:
                        if b == 0:
                            if i >= 2:
                                pe.wait_ge(S.a_yv, n_a_y(5 * i - 9))
                            for p in range(2):
                                mm = pe.matmul(cbank(i)[:, p * HD:(p + 1) * HD], pm[:, PA_Q + p, i * P:(i + 1) * P],
                                               KCB[:, :, :].rearrange("p e n -> p (e n)"), start=True, stop=True)
                            mm.then_inc(S.a_cl, 1)
                        for h in range(H):
                            u = 4 * n + h
                            if u >= 2:
                                pe.wait_ge(S.a_l, u - 1)
                            pe.matmul(bank[h % 2][:, 0:(i + 1) * P], q(h, i), pm[half(h), PA_KS + b, 0:(i + 1) * P],
                                      start=True, stop=True).then_inc(S.a_s, 1)
                        if b == 0:
                            pe.wait_ge(S.a_ce, i + 1)
                            pe.transpose(cbank(i)[:, P:2 * P], LC[:, :, :].rearrange("p h n -> p (h n)"), ident).then_inc(S.a_ct, 1)
                            pe.wait_ge(S.a_ctc, i + 1)
                            pe.matmul(cbank(i)[:, 256:512], PCT[:, :], VCB[:, :, :].rearrange("p h d -> p (h d)"), start=True,
                                      stop=True).then_inc(S.a_co, 1)
                    if n:
                        i, b = (n - 1) // 2, (n - 1) % 2

                        def values(h):
                            pe.wait_ge(S.a_tc, 4 * (n - 1) + h + 1)
                            if i and b == 0 and h == 0:
                                pe.wait_ge(S.a_yv, n_a_y(5 * i))
                            o = bank[4][:, 256 * b + HD * h:256 * b + HD * (h + 1)]
                            for t in range(i + 1):
                                mm = pe.matmul(o, PTR[h][:, t * P:(t + 1) * P], V6[:, t, b * HD:(b + 1) * HD],
                                               start=t == 0, stop=t == i)
                            mm.then_inc(S.a_pv, 1)
                        for h in range(H):
                            u = 4 * (n - 1) + h
                            pe.wait_ge(S.a_e, u + 1)
                            if u >= 2:
                                pe.wait_ge(S.a_tc, u - 1)
                            for t in range(i + 1):
                                mm = pe.transpose(bank[2 + h % 2][:, t * P:(t + 1) * P], LL[b][:, h, t * P:(t + 1) * P], ident)
                            mm.then_inc(S.a_t, 1)
                            if h:
                                values(h - 1)
                        values(H - 1)
                head_out(2, YA)

            def layer1(l):
                mean_square(0)
                up(U_UP1, 0, (S.h_lo, 0))
                down(U_DN1, 0, FT)
                mean_square(1)
                project(U_IN, N_IN0 // 2, S.pm, 0, (S.h_lo, KT))
                project_mixed()
                norms()
                mix_d()
                mix_c()
                mix_c_scan()
                mix_a()
                project(U_OUT, KT // 2, S.x_new, KT, (S.y_lo, 0))
                mean_square(2)
                up(U_UP2, FT, (S.h_lo, 2 * KT))
                down(U_DN2, 2 * KT, 2 * FT)
                pe.wait_ge(S.x_new, 3 * KT)

            with pe.Fori(0, L) as l:
                layer1(l)
                end_layer(pe, l)

            pe.wait_ge(S.trig_a, 2)

            def beside2(k):
                if k == 1:
                    pe.wait_ge(S.lam_v, 1)
                    pe.matmul(bank[6][:, 0:2], ones[0:HD, :], LQ[0:HD, :], start=True, stop=True).then_inc(S.lam_ps, 1)
                if k == 2:
                    for g in range(4):
                        pe.wait_ge(S.n_sq, g + 1)
                        pe.matmul(bank[2 + g][:, :], ones, SQ2[g], start=True, stop=True).then_inc(S.n_ss, 1)
                if 3 <= k < 11:
                    c = k - 3
                    if c == 0:
                        pe.wait_ge(S.lam_e, 1)
                    if c >= 2:
                        pe.wait_ge(S.rot_sin, c - 1)
                    pe.wait_ge(S.pm, N_IN0_2 + c + 1)
                    pe.matmul(bank[6 + c % 2][:, :], rot, pm[:, QQ + c, :], start=True, stop=True).then_inc(S.rot_ps, 1)
                if k == 6:
                    for g in range(4):
                        pe.wait_ge(S.n_out, g + 1)
                        turn_tiles(2 + g, lambda t: pm[:, QV + g, t * P:(t + 1) * P], S.vg_t)
                if k == 8:
                    pe.wait_ge(S.ws_set, 1)
                    for g in range(4):
                        pe.wait_ge(S.vg_sb, g + 1)
                        for t in range(TT):
                            mm = pe.matmul(bank[2 + g][:, t * P:(t + 1) * P], VG[g][:, t, :], WS[:, g, :], start=True, stop=True)
                        mm.then_inc(S.mixed, 1)

            def project2():
                for k in range(N_IN2 - N_IN0_2):
                    u = V_IN + N_IN0_2 + k
                    pe.wait_ge(S.w_lo, u + 1)
                    pe.wait_ge(S.pm, u - 1)
                    products(bank[k % 2][:, :], k % 2, KT, hH, hL, 0, True, True)
                    beside2(k)

            def mix2():
                pe.wait_ge(S.pm, N_IN2)
                pe.wait_ge(S.mix_b, 4)
                for h in range(4):
                    turn_tiles(2 + h, lambda t: pm[:, QA + h, t * P:(t + 1) * P], S.va_t)
                pe.wait_ge(S.rot_x, 8)
                pe.wait_ge(S.va_sb, 4)
                for n in range(18):
                    if n < 16:
                        h, i, b = n // TT, n % TT, n % 2
                        if n >= 2:
                            pe.wait_ge(S.s_max, 2 * n - 2)
                        for m in range(2):
                            pe.matmul(bank[2 * b + m][:, 0:(i + 1) * P], pm[half(m), QQ + h, i * P:(i + 1) * P],
                                      pm[half(m), QK_ + h, 0:(i + 1) * P], start=True, stop=True).then_inc(S.s_ps, 1)
                    if 1 <= n < 17:
                        u = n - 1
                        pe.wait_ge(S.s_diff, u + 1)
                        if u >= 2:
                            pe.wait_ge(S.s_tsb, u - 1)
                        for t in range(u % TT + 1):
                            mm = pe.transpose(bank[4 + u % 2][:, t * P:(t + 1) * P], AD[u % 2][:, t * P:(t + 1) * P], ident)
                        mm.then_inc(S.s_t, 1)
                    if n >= 2:
                        v = n - 2
                        h, i = v // TT, v % TT
                        pe.wait_ge(S.s_tsb, v + 1)
                        if v >= 2:
                            pe.wait_ge(S.s_y, v - 1)
                        for t in range(i + 1):
                            mm = pe.matmul(bank[6 + v % 2][:, 0:P], ADT[v % 2][:, t * P:(t + 1) * P], VA[h][:, t, :],
                                           start=t == 0, stop=t == i)
                        mm.then_inc(S.s_val, 1)
                for h in range(4):
                    pe.wait_ge(S.o_v, 5 + h)
                    turn_tiles(2 + h, lambda t: YD[:, t, h * P:(h + 1) * P], S.o_t)

            def up2(ubase, ready):
                def turn(i, ready=None):
                    for half in range(2):
                        pe.wait_ge(S.w_lo, ubase + 2 * i + half + 1)
                        if later(i):
                            pe.wait_ge(S.f_conv, 4 * i - 2 + 2 * half)
                        products(bank[half][:, :], half, KT, hH, hL, 0, True, True, None if half else ready)
                turn(0, ready)
                with pe.Fori(1, FT) as i:
                    turn(i)

            def layer2(l):
                mean_square(0)
                project(V_IN, N_IN0_2 // 2, S.pm, 0, (S.h_lo, 0))
                project2()
                mix2()
                project(V_OUT, KT // 2, S.x_new, 0, (S.y_lo, 0))
                mean_square(1)
                up2(V_UP, (S.h_lo, KT))
                down(V_DN, KT, FT)
                pe.wait_ge(S.x_new, 2 * KT)

            with pe.Fori(0, L) as l:
                layer2(l)
                end_layer(pe, l + L)
            mean_square(0)
            pe.wait_ge(S.x_new, KT)

            for t in range(TT):
                for k in range(KT):
                    n = t * KT + k
                    if n >= 4:
                        pe.wait_ge(S.fin, n - 3)
                    pe.transpose(bank[n % 4][:, 0:P], xT[:, k, t * P:(t + 1) * P], ident).then_inc(S.x_turned, 1)


def col_tiles(w, tiles):
    l, k, n = w.shape
    w = w.reshape(l, k // P // tiles, tiles, P, n // P, P)
    return w.transpose(0, 4, 1, 3, 2, 5).reshape(l, (n // P) * (k // P // tiles), P, tiles, P)


def bucket(dist):
    n = np.maximum(dist, 0)
    f = np.maximum(n, 1).astype(np.float32)
    large = 16 + (np.log(f / np.float32(16)) / np.float32(np.log(8.0)) * np.float32(16)).astype(np.int32)
    return np.where(dist < 0, NB, np.where(n < 16, n, np.minimum(large, NB - 1)))


def constants():
    c = np.zeros((P, X_END), np.float32)
    i = np.arange(P)
    c[:, X_ID:X_ID + P] = np.eye(P)
    c[:, X_ONE:X_ONE + P] = 1
    c[:, X_BO:X_BO + P] = i[:, None] // HD == i[None, :] // HD
    c[:, X_CM:X_CM + P] = np.where(i[None, :] <= i[:, None], 0, MASKED)
    c[:, X_CMT:X_CMT + P] = np.where(i[None, :] >= i[:, None], 0, MASKED)
    for h in range(H):
        for k in (X_SA, X_CS + K_A):
            c[R_I + h, k + h] = 1
            c[R_F + h, k + h] = -1
        c[R_F + h, X_CS + K_M + h] = 1
        c[R_BE + h, X_CS + K_BE + h] = 1
        c[R_AL + h, X_CS + K_GC + h] = 1
        c[R_F + h, X_SG] = -1
        c[R_AL + h, X_SG] = 1
    c[0:12, X_CS:X_CS + 12] = np.eye(12)
    c[:, X_TRI:X_TRI + P] = i[None, :] >= i[:, None]
    d = i % HD
    for src in np.flatnonzero(d < ROT):
        if d[src] < ROT // 2:
            c[src, X_ROT + src + ROT // 2] = 1
        else:
            c[src, X_ROT + src - ROT // 2] = -1
    theta = np.float32(500000.0) ** (-np.arange(0, ROT, 2, dtype=np.float32) / np.float32(ROT))
    c[:, X_IF] = np.where(d < ROT, theta[d % (ROT // 2)], 0)
    c[0:H, X_MS + K_M:X_MS + K_M + H] = np.eye(H)
    c[:, X_EPS] = EPS
    c[:, X_E64] = HD * EPS
    one_hot = lambda d: (np.arange(NB + 1)[:, None] == bucket(d)[None, :]).astype(np.float32)
    level = np.zeros((P, 7, P), np.float32)
    for k in range(7):
        same = i[:, None] >> (k + 1) == i[None, :] >> (k + 1)
        level[:, k] = same & ((i[:, None] >> k) % 2 == 0) & ((i[None, :] >> k) % 2 == 1)
    sums = np.ones((8, T), np.float32)
    sums[4:, ::P] = 0
    return {"cst": c, "c_lm": level, "c_rs": sums, "c_ohr": one_hot(511 - np.arange(640)),
            "c_ohf": one_hot(np.arange(1056) - 527), "c_flip": np.eye(P, dtype=np.float32)[::-1]}


SPLIT = (("a_q", 256), ("a_k_cmp", 64), ("a_v_cmp", 64), ("a_k_slc", 64), ("a_v_slc", 64), ("a_k_win", 64), ("a_v_win", 64),
         ("a_gate", 12), ("b_b", 256), ("b_c", 256), ("b_x", 256), ("c_q", 256), ("c_k", 256), ("c_v", 256), ("c_beta", 4),
         ("c_alpha", 4), ("c_z", 256), ("d_q", 256), ("d_k", 256), ("d_v", 256), ("d_i", 4), ("d_f", 4), ("d_o", 256))


def project_columns():
    at, o = {}, 0
    for n, w in SPLIT:
        at[n] = np.arange(o, o + w)
        o += w
    pad = o
    s = np.full(P, pad)
    s[0:12] = at["a_gate"]
    for r, n in ((R_I, "d_i"), (R_F, "d_f"), (R_AL, "c_alpha"), (R_BE, "c_beta")):
        s[r:r + 4] = at[n]
    order = [at["a_q"], at["a_k_slc"], at["a_k_slc"], at["a_k_win"], at["a_k_win"], at["a_k_cmp"], at["a_k_cmp"],
             at["a_v_cmp"], at["a_v_cmp"], at["a_v_slc"], at["a_v_win"], s, at["b_b"], at["b_c"], at["b_x"],
             at["c_q"], at["c_k"], at["c_v"], at["c_z"], at["d_q"], at["d_k"], at["d_v"], at["d_o"]]
    return np.concatenate(order)


def layout(inputs):
    f = lambda n: np.asarray(inputs[n])
    r = constants()
    z = lambda *s: np.zeros(s, np.float32)
    r["x"] = f("x")[0]
    r["c"] = f("c")
    r["t5_table"] = f("t5_table")
    pairs = lambda w: col_tiles(w, KT).reshape(L, 2, FT, P, KT, P).transpose(0, 2, 1, 3, 4, 5).reshape(L, 2 * FT, P, KT, P)
    order = project_columns()
    w_in = np.concatenate([f("w_in"), z(L, D, 1)], axis=2)[:, :, order]
    b_in = np.concatenate([f("b_in"), z(L, 1)], axis=1)[:, order]
    r["w_in"] = col_tiles(w_in, KT)
    r["w_out"] = col_tiles(f("w_out"), KT)
    for n in ("ffn1", "ffn2"):
        r[n + "_w13"] = pairs(f(n + "_w13"))
        r[n + "_w2"] = col_tiles(f(n + "_w2"), KH)
    r["cmp_w1"] = np.concatenate([col_tiles(f(n), KT) for n in ("cmp_k_w1", "cmp_v_w1")], axis=1)
    half = lambda w: w.reshape(L, 2, P, HD).transpose(0, 2, 1, 3)
    r["w2k"] = np.concatenate([half(f("cmp_k_w2"))] * 2, axis=3)
    r["w2v"] = half(f("cmp_v_w2"))
    ada = f("ada_w").transpose(0, 2, 1).reshape(L, NMOD, P, D)
    first = ada[:, 0:N_NEXT]
    r["ada_first"] = first[0].transpose(1, 0, 2)
    r["ada_w1"] = ada[:, N_NEXT:8 * KT]
    r["ada_w2"] = np.concatenate([ada[:, 8 * KT:], np.concatenate([first[1:], first[-1:]])], axis=1)
    cols = lambda v: v.reshape(L, -1, P).transpose(0, 2, 1)
    taps = lambda v: v.reshape(L, v.shape[1], -1, P).transpose(0, 3, 2, 1).reshape(L, P, -1)
    twice = lambda v: np.concatenate([v, v], axis=1)[:, :, None]
    small = z(L, P, 2)
    small[:, R_F:R_F + 4, 0] = f("mlstm_f_bias")
    small[:, R_AL:R_AL + 4, 0] = f("gdn_dt_bias")
    small[:, R_AL:R_AL + 4, 1] = f("gdn_A_log")
    mix = f("mix_norm_g")
    r["par1"] = np.concatenate([cols(f("norm_g")), cols(f("ada_b")), cols(b_in), twice(f("q_norm_g")), twice(f("k_norm_g")),
                                taps(f("sc_conv_w")), taps(f("gdn_conv_w")), cols(mix[:, 1]), cols(mix[:, 0]),
                                twice(f("gdn_norm_g")), twice(f("mlstm_norm_g")), small, cols(f("cmp_pos"))], axis=2)
    r["positions"] = f("positions_2")
    r["w_in2"] = col_tiles(f("w_in_2"), KT)
    r["w_out2"] = col_tiles(f("w_out_2"), KT)
    r["w_up"] = pairs(f("w_up_2"))
    r["w_down"] = col_tiles(f("w_down_2"), KH)
    r["sgu_w"] = f("sgu_w_spatial_2").transpose(0, 3, 1, 2)
    r["sgu_b"] = f("sgu_b_spatial_2")[:, None]
    lam = np.stack([f(f"lambda_{n}_2") for n in ("q1", "q2", "k1", "k2")], axis=2)
    init = 0.8 - 0.6 * np.exp(-0.3 * np.arange(L))
    r["par2"] = np.concatenate([
        cols(f("attn_norm_2")), cols(f("ffn_norm_2")), cols(np.stack([f("final_norm_2")] * L)), cols(f("sgu_v_norm_2")),
        cols(f("subln_gain_2")), np.concatenate([lam, z(L, P - HD, 4)], axis=1),
        np.broadcast_to(np.stack([init, 1 - init], axis=1)[:, None].astype(np.float32), (L, P, 2)),
        taps(f("conv_w_2")), cols(f("conv_b_2"))], axis=2)
    return {k: np.ascontiguousarray(v) for k, v in r.items()}


def kernel(**inputs):
    import concourse.bacc as bacc
    from concourse.bass_utils import run_bass_kernel_spmd

    nc = bacc.Bacc("TRN2", target_bir_lowering=False, num_devices=1)
    arrays = layout(inputs)
    args = {n: nc.dram_tensor(f"in_{n}", v.shape, mybir.dt.from_np(v.dtype), kind="ExternalInput").ap()
            for n, v in arrays.items()}
    out = nc.dram_tensor("out", (T, D), F32, kind="ExternalOutput").ap()
    build(nc, args, out)
    r = run_bass_kernel_spmd(nc, [{f"in_{n}": v for n, v in arrays.items()}], core_ids=[0])
    return r.results[0]["out"].reshape(1, T, D)
```
